# Optimizing a Trainium2 kernel written in Bass

```python
import math
import jax, jax.numpy as jnp
from jax import lax
import numpy as np

D_MODEL = 1024
BATCH = 1
SEQ = 512
DEPTH = 1

GDN_HEADS = 8
GDN_HEAD_DIM = 128
GDN_WIDTH = GDN_HEADS * GDN_HEAD_DIM
GDN_CHUNK = 64
CONV_K = 5
DIL_GROUPS = ((128, 1), (512, 4), (2048, 16))
DIL_N_GROUPS = 3
DIL_HEADS_PER_GROUP = 4
DIL_HEADS = DIL_N_GROUPS * DIL_HEADS_PER_GROUP
DIL_HEAD_DIM = 128
DIL_WIDTH = DIL_HEADS * DIL_HEAD_DIM
DIL_OUT_WIDTH = DIL_HEADS_PER_GROUP * DIL_HEAD_DIM
DIL_BLOCK = 64
REL_BUCKETS = 32
REL_MAX_DIST = 1024
D_FF = 4 * D_MODEL
EPS = 1e-6
NEG = -1e30

C_QA = 0
C_KA = C_QA + GDN_WIDTH
C_VA = C_KA + GDN_WIDTH
C_ZA = C_VA + GDN_WIDTH
C_AF = C_ZA + GDN_WIDTH
C_AB = C_AF + GDN_HEADS
C_BF = C_AB + GDN_HEADS
C_BB = C_BF + GDN_HEADS
C_QB = C_BB + GDN_HEADS
C_KB = C_QB + DIL_WIDTH
C_VB = C_KB + DIL_WIDTH
C_GA = C_VB + DIL_WIDTH
C_GB = C_GA + D_MODEL
IN_COLS = C_GB + D_MODEL


def _rmsnorm(x, w):
    xf = x.astype(jnp.float32)
    y = xf * lax.rsqrt(jnp.mean(xf * xf, axis=-1, keepdims=True) + EPS) * w.astype(jnp.float32)
    return y.astype(x.dtype)

def _l2norm(x):
    return x * lax.rsqrt(jnp.sum(x * x, axis=-1, keepdims=True) + EPS)

def _t5_bucket(rel):
    nb = REL_BUCKETS // 2
    ret = (rel > 0).astype(np.int32) * nb
    n = np.abs(rel)
    max_exact = nb // 2
    large = max_exact + (np.log(np.maximum(n, 1) / max_exact) / math.log(REL_MAX_DIST / max_exact)
                         * (nb - max_exact)).astype(np.int32)
    large = np.minimum(large, nb - 1)
    return ret + np.where(n < max_exact, n, large).astype(np.int32)

def _chunk_gated_delta(q, k, v, g, beta):
    b, s, h, dk = q.shape
    dv = v.shape[-1]
    n = s // GDN_CHUNK

    def chunks(t):
        return jnp.moveaxis(t.reshape(b, n, GDN_CHUNK, h, -1), 3, 1)

    qc, kc, vc = chunks(q), chunks(k), chunks(v)
    gc = jnp.cumsum(chunks(g[..., None])[..., 0], axis=-1)
    bc = chunks(beta[..., None])
    tri = np.tril(np.ones((GDN_CHUNK, GDN_CHUNK), bool))
    strict = np.tril(np.ones((GDN_CHUNK, GDN_CHUNK), bool), -1)
    dd = gc[..., :, None] - gc[..., None, :]
    gam = jnp.where(tri, jnp.exp(jnp.where(tri, dd, 0.0)), 0.0)
    kb = kc * bc
    a_kk = jnp.where(strict, jnp.einsum('bhnic,bhnjc->bhnij', kb, kc) * gam, 0.0)
    eye = jnp.eye(GDN_CHUNK, dtype=a_kk.dtype)
    rhs = jnp.concatenate([vc * bc, kb * jnp.exp(gc)[..., None]], axis=-1)
    sol = lax.linalg.triangular_solve(a_kk + eye, rhs, left_side=True, lower=True,
                                      unit_diagonal=True)
    u, w = sol[..., :dv], sol[..., dv:]
    a_qk = jnp.einsum('bhnic,bhnjc->bhnij', qc, kc) * gam

    def step(state, inp):
        qn, kn, un, wn, gn, aqk = inp
        v_new = un - jnp.einsum('bhck,bhkv->bhcv', wn, state)
        o = (jnp.einsum('bhck,bhkv->bhcv', qn * jnp.exp(gn)[..., None], state)
             + jnp.einsum('bhij,bhjv->bhiv', aqk, v_new))
        g_last = gn[..., -1]
        state = (state * jnp.exp(g_last)[..., None, None]
                 + jnp.einsum('bhck,bhcv->bhkv', kn * jnp.exp(g_last[..., None] - gn)[..., None], v_new))
        return state, o

    xs = tuple(jnp.moveaxis(t, 2, 0) for t in (qc, kc, u, w, gc, a_qk))
    state0 = jnp.zeros((b, h, dk, dv), jnp.float32)
    _, o = lax.scan(step, state0, xs)
    o = jnp.moveaxis(o, 0, 2)
    return jnp.moveaxis(o, 1, 3).reshape(b, s, h, dv)

def _dilated_group(q, k, v, bias, dil, half):
    b, s, h, hd = q.shape
    blk = DIL_BLOCK
    L = s // dil
    nb = -(-L // blk)
    lp = nb * blk

    def res(t):
        return t.reshape(b, L, dil, h, hd).transpose(0, 2, 1, 3, 4)

    qr = jnp.pad(res(q), ((0, 0), (0, 0), (0, lp - L), (0, 0), (0, 0))).reshape(b, dil, nb, blk, h, hd)

    def win(t):
        tp = jnp.pad(res(t), ((0, 0), (0, 0), (blk, lp - L + blk), (0, 0), (0, 0)))
        tp = tp.reshape(b, dil, nb + 2, blk, h, hd)
        return jnp.concatenate([tp[:, :, :-2], tp[:, :, 1:-1], tp[:, :, 2:]], axis=3)

    kw, vw = win(k), win(v)
    off = np.arange(3 * blk)[None, :] - blk - np.arange(blk)[:, None]
    band = np.abs(off) <= half
    key_pos = np.arange(nb)[:, None] * blk - blk + np.arange(3 * blk)[None, :]
    key_ok = (key_pos >= 0) & (key_pos < L)
    mask = band[None] & key_ok[:, None, :]
    logits = (jnp.einsum('brnqhc,brnkhc->brnhqk', qr, kw) * (hd ** -0.5)
              + bias.astype(jnp.float32))
    logits = jnp.where(mask[:, None], logits, NEG)
    lse = jax.nn.logsumexp(logits, axis=-1)
    p = jnp.exp(logits - lse[..., None])
    o = jnp.einsum('brnhqk,brnkhc->brnqhc', p, vw).reshape(b, dil, lp, h, hd)[:, :, :L]
    o = o.transpose(0, 2, 1, 3, 4).reshape(b, s, h, hd)
    lse = lse.transpose(0, 1, 2, 4, 3).reshape(b, dil, lp, h)[:, :, :L]
    lse = lse.transpose(0, 2, 1, 3).reshape(b, s, h)
    return o, lse

def _gdn_decay(a, a_log, dt_bias):
    return -jnp.exp(a_log.astype(jnp.float32)) * jax.nn.softplus(a + dt_bias.astype(jnp.float32))

def first_inputs(seed: int = 0) -> dict:
    key = jax.random.key(seed)
    ks = jax.random.split(key, 24)
    f32 = jnp.float32

    def nrm(k, shape, scale):
        return jax.random.normal(k, shape, f32) * scale

    def gain(k, shape):
        return 1.0 + 0.05 * jax.random.normal(k, shape, f32)

    dt = jnp.exp(jax.random.uniform(ks[6], (2, DEPTH, GDN_HEADS), f32, math.log(1e-3), math.log(1e-1)))
    dt_bias = dt + jnp.log(-jnp.expm1(-dt))
    a_log = jnp.log(jax.random.uniform(ks[7], (2, DEPTH, GDN_HEADS), f32, 1.0, 16.0))
    return {
        "x": jax.random.normal(ks[0], (BATCH, SEQ, D_MODEL), f32),
        "rel_bias": nrm(ks[1], (REL_BUCKETS, DIL_HEADS), 0.5),
        "ln_mix_pre": gain(ks[2], (DEPTH, D_MODEL)),
        "w_in": nrm(ks[3], (DEPTH, D_MODEL, IN_COLS), D_MODEL ** -0.5),
        "conv_w": nrm(ks[4], (DEPTH, CONV_K, 3 * GDN_WIDTH), CONV_K ** -0.5),
        "a_log_f": a_log[0],
        "a_log_b": a_log[1],
        "dt_bias_f": dt_bias[0],
        "dt_bias_b": dt_bias[1],
        "norm_a": gain(ks[5], (DEPTH, GDN_HEAD_DIM)),
        "w_branch_a": nrm(ks[8], (DEPTH, GDN_WIDTH, D_MODEL), GDN_WIDTH ** -0.5),
        "w_branch_b": nrm(ks[9], (DEPTH, DIL_OUT_WIDTH, D_MODEL), DIL_OUT_WIDTH ** -0.5),
        "w_out": nrm(ks[10], (DEPTH, D_MODEL, D_MODEL), D_MODEL ** -0.5),
        "ln_mix_post": gain(ks[11], (DEPTH, D_MODEL)),
        "ln_mlp_pre": gain(ks[12], (DEPTH, D_MODEL)),
        "w_ff1": nrm(ks[13], (DEPTH, D_MODEL, D_FF), D_MODEL ** -0.5),
        "w_ff2": nrm(ks[14], (DEPTH, D_FF, D_MODEL), D_FF ** -0.5),
        "ln_mlp_post": gain(ks[15], (DEPTH, D_MODEL)),
    }

def first_block(x, rel_bias, ln_mix_pre, w_in, conv_w, a_log_f, a_log_b, dt_bias_f, dt_bias_b,
              norm_a, w_branch_a, w_branch_b, w_out, ln_mix_post, ln_mlp_pre, w_ff1, w_ff2,
              ln_mlp_post):
    b, s, _ = x.shape
    f32 = jnp.float32
    blk = DIL_BLOCK
    off = np.arange(3 * blk)[None, :] - blk - np.arange(blk)[:, None]
    group_bias = []
    for gi, (window, dil) in enumerate(DIL_GROUPS):
        bt = rel_bias[_t5_bucket(off * dil)]
        hs = slice(gi * DIL_HEADS_PER_GROUP, (gi + 1) * DIL_HEADS_PER_GROUP)
        group_bias.append(jnp.transpose(bt[:, :, hs], (2, 0, 1)))

    for l in range(DEPTH):
        h = _rmsnorm(x, ln_mix_pre[l])
        proj = jnp.einsum('bsd,dc->bsc', h, w_in[l]).astype(f32)

        qkv = lax.conv_general_dilated(
            proj[..., C_QA:C_ZA], conv_w[l].astype(f32)[:, None, :], window_strides=(1,),
            padding=[(CONV_K // 2, CONV_K // 2)], dimension_numbers=('NWC', 'WIO', 'NWC'),
            feature_group_count=3 * GDN_WIDTH)
        qkv = jax.nn.silu(qkv)
        qa = _l2norm(qkv[..., :GDN_WIDTH].reshape(b, s, GDN_HEADS, GDN_HEAD_DIM)) * (GDN_HEAD_DIM ** -0.5)
        ka = _l2norm(qkv[..., GDN_WIDTH:2 * GDN_WIDTH].reshape(b, s, GDN_HEADS, GDN_HEAD_DIM))
        va = qkv[..., 2 * GDN_WIDTH:].reshape(b, s, GDN_HEADS, GDN_HEAD_DIM)
        g_f = _gdn_decay(proj[..., C_AF:C_AB], a_log_f[l], dt_bias_f[l])
        g_b = _gdn_decay(proj[..., C_AB:C_BF], a_log_b[l], dt_bias_b[l])
        beta_f = jax.nn.sigmoid(proj[..., C_BF:C_BB])
        beta_b = jax.nn.sigmoid(proj[..., C_BB:C_QB])
        flip = lambda t: jnp.flip(t, axis=1)
        o_a = (_chunk_gated_delta(qa, ka, va, g_f, beta_f)
               + flip(_chunk_gated_delta(flip(qa), flip(ka), flip(va), flip(g_b), flip(beta_b))))
        z = proj[..., C_ZA:C_AF].reshape(b, s, GDN_HEADS, GDN_HEAD_DIM)
        o_a = _rmsnorm(o_a, norm_a[l]) * jax.nn.silu(z)
        o_a = o_a.reshape(b, s, GDN_WIDTH).astype(x.dtype)

        qb = proj[..., C_QB:C_KB].reshape(b, s, DIL_HEADS, DIL_HEAD_DIM)
        kb = proj[..., C_KB:C_VB].reshape(b, s, DIL_HEADS, DIL_HEAD_DIM)
        vb = proj[..., C_VB:C_GA].reshape(b, s, DIL_HEADS, DIL_HEAD_DIM)
        outs, lses = [], []
        for gi, (window, dil) in enumerate(DIL_GROUPS):
            hs = slice(gi * DIL_HEADS_PER_GROUP, (gi + 1) * DIL_HEADS_PER_GROUP)
            o_g, lse_g = _dilated_group(qb[:, :, hs], kb[:, :, hs], vb[:, :, hs], group_bias[gi],
                                        dil, window // (2 * dil))
            outs.append(o_g)
            lses.append(lse_g)
        wgt = jax.nn.softmax(jnp.stack(lses, axis=0), axis=0)
        o_b = jnp.sum(wgt[..., None] * jnp.stack(outs, axis=0), axis=0)
        o_b = o_b.reshape(b, s, DIL_OUT_WIDTH).astype(x.dtype)

        gate_a = jax.nn.sigmoid(proj[..., C_GA:C_GB]).astype(x.dtype)
        gate_b = jax.nn.sigmoid(proj[..., C_GB:IN_COLS]).astype(x.dtype)
        merged = (gate_a * jnp.einsum('bsc,cd->bsd', o_a, w_branch_a[l])
                  + gate_b * jnp.einsum('bsc,cd->bsd', o_b, w_branch_b[l]))
        y = jnp.einsum('bsd,de->bse', merged, w_out[l])
        x = x + _rmsnorm(y, ln_mix_post[l])

        h2 = _rmsnorm(x, ln_mlp_pre[l])
        f = jnp.square(jax.nn.relu(jnp.einsum('bsd,df->bsf', h2, w_ff1[l])))
        f = jnp.einsum('bsf,fd->bsd', f, w_ff2[l])
        x = x + _rmsnorm(f, ln_mlp_post[l])
    return x


GRID_W = 64
HEAD_DIM = 64
RWKV_HEADS = 8
RWKV_WIDTH = RWKV_HEADS * HEAD_DIM
DECAY_RANK = 64
ICLR_RANK = 64
GATE_RANK = 128
NA_HEADS = 8
NA_WIDTH = NA_HEADS * HEAD_DIM
NA_MAX_WIN_ROWS = 8
NA_WIN_COLS = 16
N_GROUPS = 4
EXPERTS_PER_GROUP = 8
N_EXPERTS = N_GROUPS * EXPERTS_PER_GROUP
D_EXPERT = 256
TOP_K_IN_GROUP = 2
RMS_EPS = 1e-6
GN_EPS = 64e-5
NEG_INF = -1e30
RWKV_COLS = 3 * RWKV_WIDTH + 2 * DECAY_RANK + 2 * ICLR_RANK + GATE_RANK
NA_COLS = 3 * NA_WIDTH
GATE_COLS = 2 * D_MODEL
IN_COLS_2 = RWKV_COLS + NA_COLS + GATE_COLS
RWKV_SPLITS = (RWKV_WIDTH, 2 * RWKV_WIDTH, 3 * RWKV_WIDTH,
               3 * RWKV_WIDTH + DECAY_RANK, 3 * RWKV_WIDTH + 2 * DECAY_RANK,
               3 * RWKV_WIDTH + 2 * DECAY_RANK + ICLR_RANK,
               3 * RWKV_WIDTH + 2 * DECAY_RANK + 2 * ICLR_RANK)
IN_SPLITS = (RWKV_COLS, RWKV_COLS + NA_WIDTH, RWKV_COLS + 2 * NA_WIDTH, RWKV_COLS + 3 * NA_WIDTH)


def rmsnorm(x, g):
    x32 = x.astype(jnp.float32)
    y = x32 * lax.rsqrt(jnp.mean(x32 * x32, axis=-1, keepdims=True) + RMS_EPS)
    return (y * g).astype(x.dtype)

def centred_token_shift(p, mu_prev, mu_next):
    prev = jnp.pad(p, ((0, 0), (1, 0), (0, 0)))[:, :-1]
    nxt = jnp.pad(p, ((0, 0), (0, 1), (0, 0)))[:, 1:]
    return p + mu_prev * (prev - p) + mu_next * (nxt - p)

def rwkv_log_decay(lora, w0, up):
    w_raw = (w0 + jnp.tanh(lora) @ up).astype(jnp.float32)
    return -jnp.exp(-jax.nn.softplus(-w_raw) - 0.5)

def rwkv_step(S, inp):
    r_t, w_t, k_t, v_t, kk_t, a_t = inp
    sa = jnp.einsum('dbhij,dbhj->dbhi', S, -kk_t)
    S = (S * w_t[..., None, :] + sa[..., :, None] * (kk_t * a_t)[..., None, :]
         + v_t[..., :, None] * k_t[..., None, :])
    y = jnp.einsum('dbhij,dbhj->dbhi', S, r_t)
    return S, y

def rwkv7_bidirectional(p, mu_prev, mu_next, w0_f, w_up_f, w0_b, w_up_b, a0_f, a_up_f,
                        a0_b, a_up_b, g_up, k_k, k_a, r_k, lnx_g, lnx_b):
    B, T, _ = p.shape
    dt = p.dtype
    p = centred_token_shift(p, mu_prev, mu_next)
    r, k, v, wl_f, wl_b, al_f, al_b, gl = jnp.split(p, RWKV_SPLITS, axis=-1)
    lw_f = rwkv_log_decay(wl_f, w0_f, w_up_f)
    lw_b = rwkv_log_decay(wl_b, w0_b, w_up_b)
    a_f = jax.nn.sigmoid(a0_f + al_f @ a_up_f)
    a_b = jax.nn.sigmoid(a0_b + al_b @ a_up_b)
    g = jax.nn.sigmoid(gl) @ g_up

    def heads(t):
        return t.reshape(B, T, RWKV_HEADS, HEAD_DIM).astype(jnp.float32)

    r_h, v_h = heads(r), heads(v)
    kk = heads(k * k_k)
    kk = kk * lax.rsqrt(jnp.sum(kk * kk, axis=-1, keepdims=True) + 1e-12)
    k_f = heads(k * (1.0 + (a_f - 1.0) * k_a))
    k_b = heads(k * (1.0 + (a_b - 1.0) * k_a))
    a_fh, a_bh = heads(a_f), heads(a_b)
    w_fh, w_bh = jnp.exp(heads(lw_f)), jnp.exp(heads(lw_b))

    def both(f, b):
        return jnp.stack([f, jnp.flip(b, axis=1)], axis=0).transpose(2, 0, 1, 3, 4)

    xs = (both(r_h, r_h), both(w_fh, w_bh), both(k_f, k_b), both(v_h, v_h),
          both(kk, kk), both(a_fh, a_bh))
    S0 = jnp.zeros((2, B, RWKV_HEADS, HEAD_DIM, HEAD_DIM), jnp.float32)
    _, ys = lax.scan(rwkv_step, S0, xs)
    y_f = ys[:, 0].transpose(1, 0, 2, 3)
    y_b = jnp.flip(ys[:, 1].transpose(1, 0, 2, 3), axis=1)
    y = y_f + y_b
    mean = jnp.mean(y, axis=-1, keepdims=True)
    var = jnp.mean(jnp.square(y - mean), axis=-1, keepdims=True)
    y = ((y - mean) * lax.rsqrt(var + GN_EPS)).reshape(B, T, RWKV_WIDTH) * lnx_g + lnx_b
    bonus = jnp.sum(r_h * (k_f + k_b) * r_k, axis=-1, keepdims=True) * v_h
    y = (y + bonus.reshape(B, T, RWKV_WIDTH)) * g
    return y.astype(dt)

def neighbourhood_attention_2d(q, k, v, q_gain, k_gain, rpb):
    B, T, _ = q.shape
    dt = q.dtype
    rows = T // GRID_W
    kh = min(NA_MAX_WIN_ROWS, rows)

    def qk_norm(t, g):
        t32 = t.reshape(B, T, NA_HEADS, HEAD_DIM).astype(jnp.float32)
        return t32 * lax.rsqrt(jnp.mean(t32 * t32, axis=-1, keepdims=True) + RMS_EPS) * g

    def grid(t):
        return t.reshape(B, rows, GRID_W, NA_HEADS, HEAD_DIM).transpose(0, 3, 1, 2, 4)

    qg = grid(qk_norm(q, q_gain) * (HEAD_DIM ** -0.5))
    kg = grid(qk_norm(k, k_gain))
    vg = grid(v.reshape(B, T, NA_HEADS, HEAD_DIM).astype(jnp.float32))

    cols = np.arange(GRID_W)
    col_start = np.clip(cols - NA_WIN_COLS // 2, 0, GRID_W - NA_WIN_COLS)
    col_mask = ((cols[None, :] >= col_start[:, None])
                & (cols[None, :] < col_start[:, None] + NA_WIN_COLS))
    col_off = np.clip(cols[None, :] - cols[:, None] + NA_WIN_COLS - 1, 0, 2 * NA_WIN_COLS - 2)

    def row_block(i):
        start = jnp.clip(i - kh // 2, 0, rows - kh)
        k_blk = lax.dynamic_slice_in_dim(kg, start, kh, axis=2)
        v_blk = lax.dynamic_slice_in_dim(vg, start, kh, axis=2)
        q_blk = lax.dynamic_index_in_dim(qg, i, axis=2, keepdims=False)
        s = jnp.einsum('bhqd,bhrkd->bhqrk', q_blk, k_blk)
        row_off = start + jnp.arange(kh) - i + NA_MAX_WIN_ROWS - 1
        bias = rpb.astype(jnp.float32)[:, row_off][:, :, col_off]
        s = s + bias.transpose(0, 2, 1, 3)[None]
        s = jnp.where(col_mask[:, None, :], s, NEG_INF)
        prob = jax.nn.softmax(s, axis=(-2, -1))
        return jnp.einsum('bhqrk,bhrkd->bhqd', prob, v_blk)

    out = lax.map(row_block, jnp.arange(rows))
    out = out.transpose(1, 0, 3, 2, 4).reshape(B, T, NA_WIDTH)
    return out.astype(dt)

def hierarchical_moe(h, w_rg, b_rg, w_re, b_re, w_gate_e, w_up_e, w_down_e):
    B, T, D = h.shape
    ht = h.reshape(B * T, D)
    n_tok = ht.shape[0]
    g_logits = (ht @ w_rg + b_rg).astype(jnp.float32)
    g_sel = jnp.argmax(g_logits, axis=-1)
    p_group = jnp.take_along_axis(jax.nn.softmax(g_logits, axis=-1), g_sel[:, None], axis=-1)
    e_logits = (ht @ w_re + b_re).astype(jnp.float32).reshape(n_tok, N_GROUPS, EXPERTS_PER_GROUP)
    e_in_group = jnp.take_along_axis(e_logits, g_sel[:, None, None], axis=1)[:, 0]
    top_val, top_idx = lax.top_k(e_in_group, TOP_K_IN_GROUP)
    weights = p_group * jax.nn.softmax(top_val, axis=-1)
    expert_id = g_sel[:, None] * EXPERTS_PER_GROUP + top_idx
    combine = jnp.sum(jax.nn.one_hot(expert_id, N_EXPERTS, dtype=jnp.float32) * weights[..., None], axis=1)
    combine = combine.astype(h.dtype)
    y = jnp.zeros_like(ht)
    for e in range(N_EXPERTS):
        he = jax.nn.silu(ht @ w_gate_e[e]) * (ht @ w_up_e[e])
        y = y + combine[:, e:e + 1] * (he @ w_down_e[e])
    return y.reshape(B, T, D)

def second_inputs(seed: int = 0) -> dict:
    key = jax.random.key(seed)
    ks = iter(jax.random.split(key, 40))
    L = DEPTH

    def nrm(shape, scale):
        return jax.random.normal(next(ks), shape, jnp.float32) * scale

    def unif(shape, lo, hi):
        return jax.random.uniform(next(ks), shape, jnp.float32, lo, hi)

    return {
        'x': nrm((BATCH, SEQ, D_MODEL), 1.0),
        'norm1_g': 1.0 + nrm((L, D_MODEL), 0.02),
        'w_in': nrm((L, D_MODEL, IN_COLS_2), D_MODEL ** -0.5),
        'mu_prev': unif((L, RWKV_COLS), 0.0, 0.5),
        'mu_next': unif((L, RWKV_COLS), 0.0, 0.5),
        'w0_f': unif((L, RWKV_WIDTH), -6.0, 1.0),
        'w_up_f': nrm((L, DECAY_RANK, RWKV_WIDTH), DECAY_RANK ** -0.5),
        'w0_b': unif((L, RWKV_WIDTH), -6.0, 1.0),
        'w_up_b': nrm((L, DECAY_RANK, RWKV_WIDTH), DECAY_RANK ** -0.5),
        'a0_f': nrm((L, RWKV_WIDTH), 0.5),
        'a_up_f': nrm((L, ICLR_RANK, RWKV_WIDTH), ICLR_RANK ** -0.5),
        'a0_b': nrm((L, RWKV_WIDTH), 0.5),
        'a_up_b': nrm((L, ICLR_RANK, RWKV_WIDTH), ICLR_RANK ** -0.5),
        'g_up': nrm((L, GATE_RANK, RWKV_WIDTH), GATE_RANK ** -0.5),
        'k_k': 0.85 + nrm((L, RWKV_WIDTH), 0.05),
        'k_a': 1.0 + nrm((L, RWKV_WIDTH), 0.05),
        'r_k': nrm((L, RWKV_HEADS, HEAD_DIM), 0.1),
        'lnx_g': 1.0 + nrm((L, RWKV_WIDTH), 0.02),
        'lnx_b': nrm((L, RWKV_WIDTH), 0.01),
        'q_gain': 1.0 + nrm((L, HEAD_DIM), 0.02),
        'k_gain': 1.0 + nrm((L, HEAD_DIM), 0.02),
        'rpb': nrm((L, NA_HEADS, 2 * NA_MAX_WIN_ROWS - 1, 2 * NA_WIN_COLS - 1), 0.1),
        'b_gate': nrm((L, GATE_COLS), 0.01),
        'w_o_rwkv': nrm((L, RWKV_WIDTH, D_MODEL), RWKV_WIDTH ** -0.5),
        'w_o_na': nrm((L, NA_WIDTH, D_MODEL), NA_WIDTH ** -0.5),
        'w_out': nrm((L, D_MODEL, D_MODEL), D_MODEL ** -0.5),
        'norm2_g': 1.0 + nrm((L, D_MODEL), 0.02),
        'w_router_group': nrm((L, D_MODEL, N_GROUPS), D_MODEL ** -0.5),
        'b_router_group': nrm((L, N_GROUPS), 0.01),
        'w_router_expert': nrm((L, D_MODEL, N_EXPERTS), D_MODEL ** -0.5),
        'b_router_expert': nrm((L, N_EXPERTS), 0.01),
        'w_gate_e': nrm((L, N_EXPERTS, D_MODEL, D_EXPERT), D_MODEL ** -0.5),
        'w_up_e': nrm((L, N_EXPERTS, D_MODEL, D_EXPERT), D_MODEL ** -0.5),
        'w_down_e': nrm((L, N_EXPERTS, D_EXPERT, D_MODEL), D_EXPERT ** -0.5),
    }

def second_block(x, norm1_g, w_in, mu_prev, mu_next, w0_f, w_up_f, w0_b, w_up_b, a0_f, a_up_f,
              a0_b, a_up_b, g_up, k_k, k_a, r_k, lnx_g, lnx_b, q_gain, k_gain, rpb, b_gate,
              w_o_rwkv, w_o_na, w_out, norm2_g, w_router_group, b_router_group,
              w_router_expert, b_router_expert, w_gate_e, w_up_e, w_down_e):
    for l in range(DEPTH):
        h = rmsnorm(x, norm1_g[l])
        p = h @ w_in[l]
        p_rwkv, q, k, v, gate_logits = jnp.split(p, IN_SPLITS, axis=-1)
        y_a = rwkv7_bidirectional(p_rwkv, mu_prev[l], mu_next[l], w0_f[l], w_up_f[l], w0_b[l],
                                  w_up_b[l], a0_f[l], a_up_f[l], a0_b[l], a_up_b[l], g_up[l],
                                  k_k[l], k_a[l], r_k[l], lnx_g[l], lnx_b[l]) @ w_o_rwkv[l]
        y_b = neighbourhood_attention_2d(q, k, v, q_gain[l], k_gain[l], rpb[l]) @ w_o_na[l]
        g_a, g_b = jnp.split(jax.nn.sigmoid(gate_logits + b_gate[l]), 2, axis=-1)
        x = x + (g_a * y_a + g_b * y_b) @ w_out[l]
        x = x + hierarchical_moe(rmsnorm(x, norm2_g[l]), w_router_group[l], b_router_group[l],
                                 w_router_expert[l], b_router_expert[l], w_gate_e[l],
                                 w_up_e[l], w_down_e[l])
    return x


def setup_inputs(seed=0):
    out = dict(first_inputs(seed))
    for name, value in second_inputs(seed + 1).items():
        if name != "x":
            out[name + "_2"] = value
    return out


def reference(
    x, rel_bias, ln_mix_pre, w_in, conv_w, a_log_f, a_log_b, dt_bias_f, dt_bias_b, norm_a,
    w_branch_a, w_branch_b, w_out, ln_mix_post, ln_mlp_pre, w_ff1, w_ff2, ln_mlp_post,
    norm1_g_2, w_in_2, mu_prev_2, mu_next_2, w0_f_2, w_up_f_2, w0_b_2, w_up_b_2, a0_f_2,
    a_up_f_2, a0_b_2, a_up_b_2, g_up_2, k_k_2, k_a_2, r_k_2, lnx_g_2, lnx_b_2, q_gain_2,
    k_gain_2, rpb_2, b_gate_2, w_o_rwkv_2, w_o_na_2, w_out_2, norm2_g_2, w_router_group_2,
    b_router_group_2, w_router_expert_2, b_router_expert_2, w_gate_e_2, w_up_e_2, w_down_e_2,
):
    x = first_block(
        x, rel_bias, ln_mix_pre, w_in, conv_w, a_log_f, a_log_b, dt_bias_f, dt_bias_b, norm_a,
        w_branch_a, w_branch_b, w_out, ln_mix_post, ln_mlp_pre, w_ff1, w_ff2, ln_mlp_post,
    )
    return second_block(
        x, norm1_g_2, w_in_2, mu_prev_2, mu_next_2, w0_f_2, w_up_f_2, w0_b_2, w_up_b_2, a0_f_2,
        a_up_f_2, a0_b_2, a_up_b_2, g_up_2, k_k_2, k_a_2, r_k_2, lnx_g_2, lnx_b_2, q_gain_2,
        k_gain_2, rpb_2, b_gate_2, w_o_rwkv_2, w_o_na_2, w_out_2, norm2_g_2, w_router_group_2,
        b_router_group_2, w_router_expert_2, b_router_expert_2, w_gate_e_2, w_up_e_2,
        w_down_e_2,
    )


_drawn_inputs = setup_inputs


def setup_inputs(seed=0):
    import zlib

    import numpy as np

    out = dict(_drawn_inputs(seed))
    spreads = {}
    factors = {'norm1_g_2': 5.305,
     'w_up_f_2': 3.574,
     'w_up_b_2': 3.596,
     'k_a_2': 2.777,
     'lnx_g_2': 64.0,
     'lnx_b_2': 64.0,
     'q_gain_2': 25.886,
     'k_gain_2': 27.119,
     'rpb_2': 31.662,
     'b_gate_2': 25.955,
     'norm2_g_2': 11.932,
     'b_router_group_2': 64.0,
     'b_router_expert_2': 28.2,
     'k_k_2': 7.341}
    for name, (base, spread) in spreads.items():
        noise = np.random.default_rng([zlib.crc32(name.encode()), seed]).standard_normal(out[name].shape)
        drawn = base * np.exp(spread * noise) if base else spread * noise
        out[name] = __import__('jax').numpy.asarray(drawn.astype(out[name].dtype))
    for name, factor in factors.items():
        out[name] = (out[name] * factor).astype(out[name].dtype)
    return out
```

```python
import math
from contextlib import ExitStack
from collections import namedtuple

import numpy as np
import concourse.bass as bass
from concourse import mybir

F32 = mybir.dt.float32
ALU = mybir.AluOpType
ACT = mybir.ActivationFunctionType
AX = mybir.AxisListType.X
U32 = mybir.dt.uint32
ds = bass.ds

P = 128
T = 512
NT = T // P
D = 1024
KT = D // P
EPS = 1e-6
NEG = -1e30
CLIP = 0.0

GH, GD = 8, 128
C_QA, C_KA, C_VA, C_ZA, C_AB = 0, 1024, 2048, 3072, 4096
C_QB = 4128
DG, DHG = 3, 4
DW = DG * DHG * P
C_KB, C_VB = C_QB + DW, C_QB + 2 * DW
C_GA, C_GB = C_QB + 3 * DW, C_QB + 3 * DW + D
SIG = 4
DF = 4 * D
LINES, LINE = 9, 2 * P - 1

RW = 512
R_LORA = 3 * RW
N_Q, N_K, N_V = 1920, 2432, 2944
N_GA, N_GB = 3456, 4480
NAROW, NAR = 64, 8
NEXP, NGRP, DE = 32, 4, 256
GN_EPS = 64e-5
DECAY = math.exp(-0.5)

CC = {}
_at = 0
for _n, _w in (("ident", P), ("ones", P), ("blk64", P), ("le", P), ("ge", P), ("lt", P), ("gt", P),
               ("levf", 7 * P), ("levb", 7 * P), ("colmask", 64), ("idx", 32), ("iota", P), ("tok", 4)):
    CC[_n] = (_at, _w)
    _at += _w
NCONST = _at


def t5_bucket(rel):
    nb = 16
    ret = (rel > 0).astype(np.int32) * nb
    n = np.abs(rel)
    large = 8 + (np.log(np.maximum(n, 1) / 8) / math.log(1024 / 8) * 8).astype(np.int32)
    return ret + np.where(n < 8, n, np.minimum(large, nb - 1)).astype(np.int32)


def constants():
    c = np.zeros((P, NCONST), np.float32)
    r, q = np.arange(P)[:, None], np.arange(P)[None, :]

    def put(name, a):
        c[:, CC[name][0]:CC[name][0] + CC[name][1]] = a

    put("ident", r == q)
    put("ones", 1.0)
    put("blk64", (r // 64) == (q // 64))
    put("le", r <= q)
    put("ge", r >= q)
    put("lt", r < q)
    put("gt", r > q)
    for lev in range(7):
        b = 1 << lev
        m = (r // (2 * b) == q // (2 * b)) & ((r // b) % 2 == 1) & ((q // b) % 2 == 0)
        c[:, CC["levf"][0] + lev * P:CC["levf"][0] + (lev + 1) * P] = m
        c[:, CC["levb"][0] + lev * P:CC["levb"][0] + (lev + 1) * P] = m.T
    qc = 63 - (np.arange(P) % 64)
    st = np.clip(qc - 8, 0, 48)[:, None]
    kc = np.arange(64)[None, :]
    put("colmask", np.where((kc >= st) & (kc < st + 16), 0.0, NEG))
    put("iota", q)
    put("tok", r + P * np.arange(4)[None, :])
    put("idx", 64.0 - np.arange(32)[None, :])
    m = np.arange(LINE) - (P - 1)
    hot = np.zeros((32, LINES, LINE + 1), np.float32)
    band = np.full((LINES, LINE + 1), NEG, np.float32)
    for j in range(LINES):
        if j < 7:
            off = 4 * m + (j - 3)
            rel, ok = off, np.abs(off) <= 64
        elif j == 7:
            rel, ok = m * 4, np.abs(m) <= 64
        else:
            rel, ok = m * 4, m % 4 == 0
        bk = t5_bucket(rel)
        hot[bk, j, np.arange(LINE)] = 1.0
        band[j, :LINE] = np.where(ok, 0.0, NEG)
    return c, hot.reshape(32, -1), np.ascontiguousarray(np.broadcast_to(band.reshape(1, -1), (4, LINES * (LINE + 1))))


def bcast_rows(row, n, width, parts=P):
    return bass.AP(tensor=row.tensor, offset=row.offset, ap=[[0, parts], [1, width]])


class Shared:
    pass


class Chain:

    def __init__(self, eng, sem):
        self.eng, self.sem, self.n = eng, sem, 0

    def link(self, ins):
        self.n += 1
        ins.then_inc(self.sem, 1)
        self.eng.wait_ge(self.sem, self.n)

    def clear(self):
        if self.n:
            self.eng.sem_clear(self.sem)
            self.n = 0


class Phase:

    def __init__(self, nc, name, sems):
        self.nc, self.name, self.names = nc, name, sems

    def __enter__(self):
        self.ctx = ExitStack()
        self.ctx.__enter__()
        self.used = []
        self.s = namedtuple("Semaphores", self.names)(*[self.sem(n) for n in self.names.split()])
        return self

    def sem(self, name):
        self.used.append(self.nc.alloc_semaphore(name=f"{self.name}_{name}"))
        return self.used[-1]

    def sems(self, name, n):
        return [self.sem(f"{name}{i}") for i in range(n)]

    def sb(self, name, shape, dt=F32):
        return self.ctx.enter_context(self.nc.sbuf_tensor(f"{self.name}_{name}", shape, dt))

    def banks(self, n=8):
        return [self.ctx.enter_context(self.nc.psum_tensor(f"{self.name}_bank{i}", [P, 512], F32)) for i in range(n)]

    def block(self):
        return self.ctx.enter_context(self.nc.Block())

    def __exit__(self, *failed):
        if failed[0] is not None:
            return False
        self.ctx.__exit__(None, None, None)
        self.nc.clear_and_free_semaphores(self.used)
        self.nc.all_engine_barrier()
        return False


def norm_phase(nc, G, name, ln_row, first=None, add_row=None, rows_dram=None):
    with Phase(nc, name, "x_in ln_in const_in mean root h_ready turned rows_out chain") as ph:
        s = ph.s
        lnw = ph.sb("lnw", [P, 2, D])
        h = ph.sb("h", [P, NT, D])
        ss = ph.sb("ss", [P, 4 * NT])
        bank = ph.banks()
        block = ph.block()
        rows = [r for r in (add_row, ln_row) if r is not None]

        @block.sync
        def _(sp):
            if first is not None:
                sp.dma_start(G.X[:], first[0][0].rearrange("(t p) d -> p t d", p=P)).then_inc(s.x_in, 16)
                sp.dma_start(G.const[:], first[1]).then_inc(s.const_in, 16)
            for j, row in enumerate(rows):
                sp.dma_start(lnw[:, j], bcast_rows(row, 1, D)).then_inc(s.ln_in, 16)
            if rows_dram is not None:
                for t in range(NT):
                    sp.wait_ge(s.h_ready, t + 1)
                    sp.dma_start(rows_dram[t * P:(t + 1) * P, :], h[:, t, :]).then_inc(s.rows_out, 16)
                sp.wait_ge(s.rows_out, 16 * NT)

        @block.vector
        def _(dve):
            c = Chain(dve, s.chain)
            if first is not None:
                for j, value in enumerate((EPS, GN_EPS, 1e-12, 1.0)):
                    dve.memset(G.eps[:, j:j + 1], value)
                dve.wait_ge(s.x_in, 16)

            def rms(src, turn):
                for t in range(NT):
                    ins = dve.tensor_tensor_reduce(h[:, t, :], src[:, t, :], src[:, t, :], 1.0, 0.0, ALU.mult, ALU.add,
                                                   ss[:, t:t + 1])
                c.link(ins)
                dve.tensor_scalar(ss[:, NT:2 * NT], ss[:, 0:NT], 1.0 / D, EPS, ALU.mult, ALU.add).then_inc(s.mean, 1)
                dve.wait_ge(s.root, turn)
                c.link(dve.reciprocal(ss[:, 3 * NT:4 * NT], ss[:, 2 * NT:3 * NT]))

            if add_row is not None:
                rms(G.Y, 1)
                dve.wait_ge(s.ln_in, 16 * len(rows))
                for t in range(NT):
                    ins = dve.scalar_tensor_tensor(G.Y[:, t, :], G.Y[:, t, :], ss[:, 3 * NT + t:3 * NT + t + 1], lnw[:, 0],
                                                   ALU.mult, ALU.mult)
                c.link(ins)
                for t in range(NT):
                    ins = dve.tensor_tensor(G.X[:, t, :], G.X[:, t, :], G.Y[:, t, :], ALU.add)
                c.link(ins)
            rms(G.X, len(rows))
            dve.wait_ge(s.ln_in, 16 * len(rows))
            for t in range(NT):
                dve.scalar_tensor_tensor(h[:, t, :], G.X[:, t, :], ss[:, 3 * NT + t:3 * NT + t + 1], lnw[:, len(rows) - 1],
                                         ALU.mult, ALU.mult).then_inc(s.h_ready, 1)

        @block.scalar
        def _(act):
            for n in range(len(rows)):
                act.wait_ge(s.mean, n + 1)
                act.activation(ss[:, 2 * NT:3 * NT], ss[:, NT:2 * NT], ACT.Sqrt).then_inc(s.root, 1)
            for k in range(KT):
                act.wait_ge(s.turned, k + 1)
                act.activation(G.hT[:, k, :], bank[k][:, :], ACT.Copy)

        @block.tensor
        def _(pe):
            if first is not None:
                pe.wait_ge(s.const_in, 16)
            for k in range(KT):
                for t in range(NT):
                    if k == 0:
                        pe.wait_ge(s.h_ready, t + 1)
                    ins = pe.transpose(bank[k][:, t * P:(t + 1) * P], h[:, t, k * P:(k + 1) * P], G.c("ident"))
                ins.then_inc(s.turned, 1)


def attention_phase(nc, G, w_in, rel_bias, hot, band, lines_dram):
    W9 = 9
    with Phase(nc, "att", "small line_mm lines_ready lines_out toep proj logits logits_taken "
               "negmax expd p_ready turned pt_ready out out_taken copied chain") as ph:
        s = ph.s
        w_ready = ph.sems("w_ready", W9)
        wr = ph.sb("wr", [P, W9, KT, P])
        rb = ph.sb("rb", [32, 12])
        hots = ph.sb("hots", [32, LINES * (LINE + 1)])
        bands = ph.sb("bands", [4, LINES * (LINE + 1)])
        lines = ph.sb("lines", [4, LINES * (LINE + 1)])
        bias = ph.sb("bias", [P, DHG, LINES, P])
        qT = ph.sb("qT", [P, DG, SIG, P])
        kT = ph.sb("kT", [P, DG, SIG, P])
        v = ph.sb("v", [P, SIG, DG, P])
        L = ph.sb("L", [P, 2, 6 * P])
        PT = ph.sb("PT", [P, 2, 6 * P])
        st = ph.sb("st", [P, 2, 4])
        bank = ph.banks()
        block = ph.block()
        LW = LINE + 1
        obT = G.obT[:].rearrange("p h (l s) -> p h l s", s=SIG)
        hview = G.hT[:].rearrange("p k (l s) -> p k s l", s=SIG)
        cols = [(C_QB, C_KB, C_VB)[n % 3] + (n // 3) * DHG * P for n in range(W9)]
        wv = w_in.rearrange("(k p) c -> p k c", p=P)

        @block.sync
        def _(sp):
            sp.dma_start(rb[:], rel_bias).then_inc(s.small, 16)
            sp.dma_start(hots[:], hot).then_inc(s.small, 16)
            sp.dma_start(bands[:], band).then_inc(s.small, 16)
            for n in range(W9):
                sp.dma_start(wr[:, n], wv[:, :, cols[n]:cols[n] + P]).then_inc(w_ready[n], 16)
            sp.wait_ge(s.lines_ready, 3)
            sp.dma_start(lines_dram, lines[:]).then_inc(s.lines_out, 16)
            sp.wait_ge(s.lines_out, 16)
            for h in range(DHG):
                src = bass.AP(tensor=lines_dram.tensor, offset=lines_dram.offset + h * LINES * LW,
                              ap=[[1, P], [LW, LINES], [1, P]])
                sp.dma_start(bias[:, h], src).then_inc(s.toep, 16)
            with sp.Fori(1, DHG) as i:
                for n in range(W9):
                    col = sp.snap(i * P + cols[n])
                    used = sp.snap(i * W9 + (n + 1 - W9))
                    sp.wait_ge(s.proj, used)
                    sp.dma_start(wr[:, n], wv[:, :, ds(col, P)]).then_inc(w_ready[n], 16)

        @block.tensor
        def _(pe):
            pe.wait_ge(s.small, 48)
            for b in range(4):
                ins = pe.matmul(bank[b][0:4, 0:2 * LW if b < 3 else LW], rb[:, 0:4],
                                hots[:, b * 2 * LW:min((b * 2 + 2) * LW, 7 * LW)], start=True, stop=True)
            pe.matmul(bank[4][0:4, 0:LW], rb[:, 4:8], hots[:, 7 * LW:8 * LW], start=True, stop=True)
            pe.matmul(bank[5][0:4, 0:LW], rb[:, 8:12], hots[:, 8 * LW:9 * LW], start=True, stop=True).then_inc(s.line_mm, 1)
            pe.wait_ge(s.lines_ready, 3)

            def logits(i, rho):
                pe.wait_ge(s.logits_taken, i * SIG + (rho + 1))
                pe.matmul(bank[3][:, :], qT[:, 0, rho, :], kT[:, 0, :, :], start=True, stop=True)
                pe.matmul(bank[4][:, 0:P], qT[:, 1, rho, :], kT[:, 1, rho, :], start=True, stop=True)
                pe.matmul(bank[4][:, P:2 * P], qT[:, 2, rho, :], kT[:, 2, rho, :], start=True, stop=True).then_inc(s.logits, 1)

            def values(i, rho):
                pe.wait_ge(s.p_ready, i * SIG + (rho + 1))
                pe.wait_ge(s.pt_ready, i * SIG + (rho + 1))
                for j in range(6):
                    ins = pe.transpose(bank[5 + j // 4][:, (j % 4) * P:(j % 4 + 1) * P], L[:, rho % 2, j * P:(j + 1) * P], G.c("ident"))
                ins.then_inc(s.turned, 1)
                pe.wait_ge(s.pt_ready, i * SIG + (rho + 2))
                pe.wait_ge(s.out_taken, i * SIG + (rho + 1))
                for j in range(6):
                    sig, g = (j, 0) if j < 4 else (rho, j - 3)
                    ins = pe.matmul(bank[7][:, 0:P], v[:, sig, g, :], PT[:, rho % 2, j * P:(j + 1) * P], start=(j == 0), stop=(j == 5))
                ins.then_inc(s.out, 1)

            with pe.Fori(0, DHG) as i:
                for n in range(W9):
                    g, which = n // 3, n % 3
                    pe.wait_ge(w_ready[n], i * 16 + 16)
                    pe.wait_ge(s.copied, i * W9 + (n + 1))
                    if which < 2:
                        for k in range(KT):
                            ins = pe.matmul(bank[which][:, :], wr[:, n, k, :], G.hT[:, k, :], start=(k == 0), stop=(k == KT - 1))
                    else:
                        for sig in range(SIG):
                            for k in range(KT):
                                ins = pe.matmul(bank[2][:, sig * P:(sig + 1) * P], hview[:, k, sig, :], wr[:, n, k, :],
                                                start=(k == 0), stop=(k == KT - 1))
                    ins.then_inc(s.proj, 1)
                pe.wait_ge(s.copied, i * W9 + (W9 + 3))
                for rho in range(SIG):
                    logits(i, rho)
                    if rho:
                        values(i, rho - 1)
                values(i, SIG - 1)

        @block.scalar
        def _(act):
            act.sem_inc(s.copied, 3)
            act.sem_inc(s.pt_ready, 1)
            with act.Fori(0, DHG) as i:
                act.wait_ge(s.out_taken, i * SIG + 1)
                for n in range(W9):
                    g, which = n // 3, n % 3
                    act.wait_ge(s.proj, i * W9 + (n + 1))
                    if which < 2:
                        src = bank[which][:, :].rearrange("p (l s) -> p s l", s=SIG)
                        if which == 0:
                            src = src[:, :, ::-1]
                        ins = act.activation((qT, kT)[which][:, g], src, ACT.Copy, scale=P ** -0.5 if which == 0 else 1.0)
                    else:
                        ins = act.activation(v[:, :, g, :], bank[2][:, :].rearrange("p (s c) -> p s c", s=SIG), ACT.Copy)
                    ins.then_inc(s.copied, 1)

                def exps(rho):
                    act.wait_ge(s.negmax, i * SIG + (rho + 1))
                    act.activation(L[:, rho % 2, :], L[:, rho % 2, :], ACT.Exp, bias=st[:, rho % 2, 1:2],
                                   accum_out=st[:, rho % 2, 2:3]).then_inc(s.expd, 1)

                def turn(rho):
                    act.wait_ge(s.turned, i * SIG + (rho + 1))
                    act.activation(PT[:, rho % 2, 0:512], bank[5][:, :], ACT.Copy)
                    act.activation(PT[:, rho % 2, 512:768], bank[6][:, 0:256], ACT.Copy).then_inc(s.pt_ready, 1)

                for rho in range(SIG):
                    exps(rho)
                    if rho:
                        turn(rho - 1)
                turn(SIG - 1)

        @block.vector
        def _(dve):
            c = Chain(dve, s.chain)
            dve.sem_inc(s.logits_taken, 1)
            dve.sem_inc(s.out_taken, 1)
            dve.wait_ge(s.line_mm, 1)
            dve.wait_ge(s.small, 48)
            for b in range(6):
                j0 = b * 2 if b < 4 else b + 3
                n = 2 if b < 3 else 1
                ins = dve.tensor_tensor(lines[:, j0 * LW:(j0 + n) * LW], bank[b][0:4, 0:n * LW], bands[:, j0 * LW:(j0 + n) * LW], ALU.add)
                if b in (1, 3, 5):
                    ins.then_inc(s.lines_ready, 1)
            def take_out(i, rho):
                dve.wait_ge(s.out, i * SIG + (rho + 1))
                src = bank[7][:, P - 1::-1][:, 0:P].rearrange("p (a l) -> p a l", a=1)
                dve.tensor_scalar(obT[:, ds(i, 1), :, rho], src, 1.0, None, ALU.mult).then_inc(s.out_taken, 1)

            dve.wait_ge(s.toep, 16 * DHG)
            with dve.Fori(0, DHG) as i:
                for rho in range(SIG):
                    r = rho % 2
                    if rho >= 2:
                        dve.wait_ge(s.turned, i * SIG + (rho - 1))
                    dve.wait_ge(s.logits, i * SIG + (rho + 1))
                    lo = L[:, r, :].rearrange("p (a j c) -> p a j c", a=1, c=P)
                    dve.tensor_tensor(lo[:, :, 0:4], bank[3][:, :].rearrange("p (a j c) -> p a j c", a=1, c=P), bias[:, ds(i, 1), 3 - rho:7 - rho, :], ALU.add)
                    dve.tensor_tensor(lo[:, :, 4:6], bank[4][:, 0:2 * P].rearrange("p (a j c) -> p a j c", a=1, c=P),
                                      bias[:, ds(i, 1), 7:9, :], ALU.add).then_inc(s.logits_taken, 1)
                    dve.wait_ge(s.logits_taken, i * SIG + (rho + 2))
                    c.link(dve.tensor_reduce(st[:, r, 0:1], L[:, r, :], AX, ALU.max))
                    dve.tensor_scalar(st[:, r, 1:2], st[:, r, 0:1], -1.0, None, ALU.mult).then_inc(s.negmax, 1)
                    dve.wait_ge(s.expd, i * SIG + (rho + 1))
                    c.link(dve.reciprocal(st[:, r, 3:4], st[:, r, 2:3]))
                    dve.tensor_scalar(L[:, r, :], L[:, r, :], st[:, r, 3:4], None, ALU.mult).then_inc(s.p_ready, 1)
                    if rho:
                        take_out(i, rho - 1)
                take_out(i, SIG - 1)
                c.clear()


LEV = 7
InvertSems = namedtuple("InvertSems", "tw xs x yz nt")


def over4(a):
    return a.unsqueeze(1).to_broadcast([P, 4, P])


def each4(col):
    return col.unsqueeze(2).to_broadcast([P, 4, P])


def four(bank):
    return bank[:, :].rearrange("p (n c) -> p n c", n=4)


def invert_pe(pe, G, s, NTm, Tm, Wm, Xs, banks, i2, i14):
    bX, bY, bZ = banks
    for lev in range(LEV):
        for d in range(2):
            if lev:
                pe.wait_ge(s.tw, i14 + (2 * (lev - 1) + d + 1))
            else:
                pe.wait_ge(s.nt, i2 + (d + 1))
            for n in range(4):
                rhs = Tm[:, d, n, :] if lev else G.c("ident")
                ins = pe.matmul(bX[d][:, n * P:(n + 1) * P], NTm[:, d, n, :], rhs, start=True, stop=True)
            ins.then_inc(s.x, 1)
        if lev == 0:
            continue
        for d in range(2):
            pe.wait_ge(s.xs, i14 + (2 * lev + d + 1))
            for n in range(4):
                if lev < LEV - 1:
                    pe.matmul(bY[d][:, n * P:(n + 1) * P], Wm[:, d, n, :], Xs[:, d, n, :], start=True, stop=True)
            for n in range(4):
                ins = pe.matmul(bZ[d][:, n * P:(n + 1) * P], Xs[:, d, n, :], Wm[:, d, n, :], start=True, stop=True)
            ins.then_inc(s.yz, 1)


def invert_dve(dve, G, s, NTm, Tm, Wm, Xs, banks, i14, i12):
    bX, bY, bZ = banks
    for lev in range(LEV):
        for d in range(2):
            mask = G.c("levb" if d else "levf", lev * P, (lev + 1) * P)
            maskT = G.c("levf" if d else "levb", lev * P, (lev + 1) * P)
            dve.wait_ge(s.x, i14 + (2 * lev + d + 1))
            if lev:
                dve.tensor_tensor(Xs[:, d], four(bX[d]), over4(mask), ALU.mult).then_inc(s.xs, 1)
            else:
                dve.tensor_tensor(Xs[:, d], four(bX[d]), over4(mask), ALU.mult)
                dve.tensor_tensor(Wm[:, d], NTm[:, d], over4(maskT), ALU.mult).then_inc(s.xs, 1)
                dve.wait_ge(s.xs, i14 + (d + 1))
                dve.tensor_tensor(Tm[:, d], over4(G.c("ident")), Xs[:, d], ALU.subtract)
                dve.tensor_tensor(Wm[:, d], over4(G.c("ident")), Wm[:, d], ALU.subtract).then_inc(s.tw, 1)
        if lev == 0:
            continue
        for d in range(2):
            dve.wait_ge(s.yz, i12 + (2 * (lev - 1) + d + 1))
            if lev < LEV - 1:
                dve.tensor_tensor(Tm[:, d], Tm[:, d], four(bY[d]), ALU.subtract)
            dve.tensor_tensor(Wm[:, d], Wm[:, d], four(bZ[d]), ALU.subtract).then_inc(s.tw, 1)


K_G, K_GC, K_B, K_NEG, K_EGL, K_ESUM = range(6)
NK = 6


def gdn_phase(nc, G, w_in, dt_row, alog_row, convw, norm_col):
    with Phase(nc, "gdn", "small ab abs_ sc1 sc2 sc3 gd cum cums sm_ready proj cb conv silu sq ssq rn qk kvt tok "
               "smh gB rb kk egB dmin dexp bst qe kdec nt x xs yz tw ks r u vn o su st oc osum osq oss orn fin "
               "chain achain") as ph:
        s = ph.s
        w_ready = ph.sems("w_ready", 4)
        wr = ph.sb("wr", [P, 4, KT, P])
        wab = ph.sb("wab", [P, KT, 32])
        dtb = ph.sb("dtb", [P, 16])
        alog = ph.sb("alog", [P, 16])
        cw = ph.sb("cw", [P, GH, 15])
        cwh = ph.sb("cwh", [P, 15])
        na = ph.sb("na", [P, 1])
        ab = ph.sb("ab", [P, NT, 32])
        tmp = ph.sb("tmp", [P, 6, NT, 16])
        gd = ph.sb("gd", [P, 16, NT])
        sm = ph.sb("sm", [P, GH, NK, 2, NT])
        smh = ph.sb("smh", [P, NK, 2, NT])
        cb = ph.sb("cb", [P, 3, T + 4])
        cv = ph.sb("cv", [P, 3, T])
        zs = ph.sb("zs", [P, T])
        sq = ph.sb("sq", [P, 2, T])
        rn = ph.sb("rn", [P, 2, T])
        qT = ph.sb("qT", [P, T])
        kT = ph.sb("kT", [P, T])
        ktok = ph.sb("ktok", [P, NT, P])
        vtok = ph.sb("vtok", [P, NT, P])
        kdec = ph.sb("kdec", [P, 2, NT, P])
        gB = ph.sb("gB", [P, 2, NT, P])
        egB = ph.sb("egB", [P, 2, T])
        qe = ph.sb("qe", [P, 2, T])
        Dx = ph.sb("Dx", [P, 2, NT, P])
        bst = ph.sb("bst", [P, 2, NT, P])
        AqT = ph.sb("AqT", [P, 2, NT, P])
        NTm = ph.sb("NTm", [P, 2, NT, P])
        Tm = ph.sb("Tm", [P, 2, NT, P])
        Wm = ph.sb("Wm", [P, 2, NT, P])
        Xs = ph.sb("Xs", [P, 2, NT, P])
        S = ph.sb("S", [P, 2, 2, P])
        R = ph.sb("R", [P, 2, 2, P])
        vn = ph.sb("vn", [P, 2, 2, P])
        osb = ph.sb("osb", [P, T])
        bank = ph.banks()
        block = ph.block()
        inv = (NTm, Tm, Wm, Xs, ((bank[2], bank[3]), (bank[4], bank[5]), (bank[6], bank[7])))
        cols = (C_QA, C_KA, C_VA, C_ZA)
        wv = w_in.rearrange("(k p) c -> p k c", p=P)
        incl, strict = (G.c("le"), G.c("ge")), (G.c("lt"), G.c("gt"))

        def chunk(d, st):
            return st if d == 0 else NT - 1 - st

        @block.sync
        def _(sp):
            sp.dma_start(wab[:], wv[:, :, C_AB:C_AB + 32]).then_inc(s.small, 16)
            sp.dma_start(dtb[:], bcast_rows(dt_row, 1, 16)).then_inc(s.small, 16)
            sp.dma_start(alog[:], bcast_rows(alog_row, 1, 16)).then_inc(s.small, 16)
            sp.dma_start(cw[:], convw).then_inc(s.small, 16)
            sp.dma_start(na[:], norm_col).then_inc(s.small, 16)
            for n in range(4):
                sp.dma_start(wr[:, n], wv[:, :, cols[n]:cols[n] + P]).then_inc(w_ready[n], 16)
            with sp.Fori(1, GH) as i:
                for n in range(4):
                    col = sp.snap(i * P + cols[n])
                    used = sp.snap(i * 4 + (n + 1 - 4))
                    sp.wait_ge(s.proj, used)
                    sp.dma_start(wr[:, n], wv[:, :, ds(col, P)]).then_inc(w_ready[n], 16)

        @block.gpsimd
        def _(pool):
            with pool.Fori(0, GH) as i:
                pool.wait_ge(s.smh, i + 1)
                pool.wait_ge(s.small, 80)
                for d in range(2):
                    pool.tensor_tensor(gB[:, d], over4(G.c("ones")), each4(smh[:, K_G, d, :]), ALU.mult).then_inc(s.gB, 1)
                for d in range(2):
                    pool.tensor_tensor(bst[:, d], over4(strict[d]), each4(smh[:, K_B, d, :]), ALU.mult).then_inc(s.bst, 1)
                pool.wait_ge(s.tok, i * 2 + 1)
                for d in range(2):
                    pool.tensor_tensor(kdec[:, d], ktok[:], each4(smh[:, K_EGL, d, :]), ALU.mult).then_inc(s.kdec, 1)
                for d in range(2):
                    pool.wait_ge(s.egB, i * 2 + (d + 1))
                    pool.tensor_tensor(qe[:, d], qT[:], egB[:, d], ALU.mult).then_inc(s.qe, 1)

        @block.tensor
        def _(pe):
            pe.wait_ge(s.small, 80)
            for t in range(NT):
                for k in range(KT):
                    ins = pe.matmul(bank[0][:, t * 32:(t + 1) * 32], G.hT[:, k, t * P:(t + 1) * P], wab[:, k, :],
                                    start=(k == 0), stop=(k == KT - 1))
            ins.then_inc(s.ab, 1)
            pe.wait_ge(s.gd, 1)
            pe.matmul(bank[1][:, 0:32], incl[0], gd[:, 0:8, :], start=True, stop=True)
            pe.matmul(bank[1][:, 32:64], incl[1], gd[:, 8:16, :], start=True, stop=True)
            pe.matmul(bank[1][:, 64:128], G.c("ones"), gd[:, :, :], start=True, stop=True).then_inc(s.cum, 1)
            pe.wait_ge(s.sm_ready, 1)
            with pe.Fori(0, GH) as i:
                pe.wait_ge(s.osum, i + 1)
                for n in range(4):
                    pe.wait_ge(w_ready[n], i * 16 + 16)
                    pe.wait_ge(s.cb, i * 4 + (n + 1))
                    for k in range(KT):
                        ins = pe.matmul(bank[n % 2][:, :], wr[:, n, k, :], G.hT[:, k, :], start=(k == 0), stop=(k == KT - 1))
                    ins.then_inc(s.proj, 1)
                pe.wait_ge(s.fin, i + 1)
                for d in range(2):
                    pe.wait_ge(s.gB, i * 2 + (d + 1))
                    for n in range(4):
                        ins = pe.matmul(bank[4 + d][:, n * P:(n + 1) * P], gB[:, d, n, :], incl[d], start=True, stop=True)
                    ins.then_inc(s.rb, 1)
                for j in range(2):
                    pe.wait_ge(s.sq, i * 2 + (j + 1))
                    pe.matmul(bank[2 + j][:, :], G.c("ones"), sq[:, j, :], start=True, stop=True).then_inc(s.ssq, 1)
                pe.wait_ge(s.qk, i * 2 + 2)
                for n in range(4):
                    ins = pe.transpose(bank[2][:, n * P:(n + 1) * P], kT[:, n * P:(n + 1) * P], G.c("ident"))
                ins.then_inc(s.kvt, 1)
                for n in range(4):
                    ins = pe.transpose(bank[3][:, n * P:(n + 1) * P], cv[:, 2, n * P:(n + 1) * P], G.c("ident"))
                ins.then_inc(s.kvt, 1)
                for n in range(4):
                    c0 = slice(n * P, (n + 1) * P)
                    pe.matmul(bank[6][:, c0], kT[:, c0], kT[:, c0], start=True, stop=True)
                for n in range(4):
                    c0 = slice(n * P, (n + 1) * P)
                    ins = pe.matmul(bank[7][:, c0], kT[:, c0], qT[:, c0], start=True, stop=True)
                ins.then_inc(s.kk, 1)
                pe.wait_ge(s.tok, i * 2 + 2)
                pe.wait_ge(s.egB, i * 2 + 2)
                invert_pe(pe, G, s, *inv, i * 2, i * 14)
                for st in range(NT):
                    for d in range(2):
                        n = chunk(d, st)
                        if st:
                            pe.wait_ge(s.st, i * 6 + (2 * (st - 1) + d + 1))
                            pe.matmul(bank[2 + d][:, 0:P], kT[:, n * P:(n + 1) * P], S[:, d, (st - 1) % 2, :],
                                      start=True, stop=True).then_inc(s.ks, 1)
                    for d in range(2):
                        n = chunk(d, st)
                        if st:
                            pe.wait_ge(s.r, i * 6 + (2 * (st - 1) + d + 1))
                        else:
                            pe.wait_ge(s.tw, i * 14 + (12 + d + 1))
                        pe.matmul(bank[4 + d][:, 0:P], Wm[:, d, n, :], R[:, d, st % 2, :] if st else vtok[:, n, :],
                                  start=True, stop=True).then_inc(s.u, 1)
                    for d in range(2):
                        n = chunk(d, st)
                        pe.wait_ge(s.vn, i * 8 + (2 * st + d + 1))
                        pe.wait_ge(s.kdec, i * 2 + (d + 1))
                        if st < NT - 1:
                            pe.matmul(bank[6 + d][:, 0:P], kdec[:, d, n, :], vn[:, d, st % 2, :], start=True, stop=True).then_inc(s.su, 1)
                        pe.wait_ge(s.qe, i * 2 + (d + 1))
                        if st:
                            pe.matmul(bank[d][:, n * P:(n + 1) * P], S[:, d, (st - 1) % 2, :], qe[:, d, n * P:(n + 1) * P],
                                      start=True, stop=False)
                        pe.matmul(bank[d][:, n * P:(n + 1) * P], vn[:, d, st % 2, :], AqT[:, d, n, :],
                                  start=(st == 0), stop=True).then_inc(s.o, 1)
                pe.wait_ge(s.osq, i + 1)
                pe.matmul(bank[2][:, :], G.c("ones"), sq[:, 0, :], start=True, stop=True).then_inc(s.oss, 1)

        @block.scalar
        def _(act):
            c = Chain(act, s.achain)
            act.sem_inc(s.cb, 2)
            act.wait_ge(s.abs_, 1)
            act.activation(tmp[:, 3], tmp[:, 2], ACT.Exp).then_inc(s.sc1, 1)
            c.link(act.activation(tmp[:, 5], ab[:, :, 16:32], ACT.Exp, scale=-1.0))
            act.activation(alog[:], alog[:], ACT.Exp).then_inc(s.sc2, 1)
            act.activation(tmp[:, 4], tmp[:, 3], ACT.Ln, bias=G.eps[:, 3:4]).then_inc(s.sc3, 1)
            act.wait_ge(s.cums, 2)
            smv = [sm[:, :, k, :, :].rearrange("p h d n -> p d h n") for k in range(NK)]
            gcv = smv[K_GC]
            act.activation(smv[K_NEG], gcv, ACT.Exp)
            act.activation(smv[K_EGL], smv[K_EGL], ACT.Exp)
            act.activation(smv[K_ESUM], smv[K_ESUM], ACT.Exp).then_inc(s.sc3, 1)
            c.clear()
            with act.Fori(0, GH) as i:
                act.wait_ge(s.conv, i * 3 + 1)
                act.wait_ge(s.fin, i + 1)
                for n in range(3):
                    act.wait_ge(s.proj, i * 4 + (n + 1))
                    act.activation(cb[:, n, 2:T + 2], bank[n % 2][:, :], ACT.Copy).then_inc(s.cb, 1)
                act.wait_ge(s.proj, i * 4 + 4)
                act.activation(zs[:], bank[1][:, :], ACT.Silu).then_inc(s.cb, 1)
                for j in range(3):
                    act.wait_ge(s.conv, i * 3 + (j + 2))
                    c.link(act.activation(cv[:, j, :], cv[:, j, :], ACT.Silu))
                for j in range(2):
                    act.activation(sq[:, j, :], cv[:, j, :], ACT.Square).then_inc(s.sq, 1)
                for j in range(2):
                    act.wait_ge(s.ssq, i * 2 + (j + 1))
                    c.link(act.activation(rn[:, j, :], bank[2 + j][:, :], ACT.Ln, bias=G.eps[:, 0:1]))
                    act.activation(rn[:, j, :], rn[:, j, :], ACT.Exp, scale=-0.5).then_inc(s.rn, 1)
                for d in range(2):
                    act.wait_ge(s.dmin, i * 2 + (d + 1))
                    act.activation(egB[:, d], bank[4 + d][:, :], ACT.Exp).then_inc(s.egB, 1)
                for d in range(2):
                    act.activation(Dx[:, d], Dx[:, d], ACT.Exp).then_inc(s.dexp, 1)
                act.wait_ge(s.kvt, i * 2 + 1)
                act.activation(ktok[:], four(bank[2]), ACT.Copy).then_inc(s.tok, 1)
                act.wait_ge(s.kvt, i * 2 + 2)
                act.activation(vtok[:], four(bank[3]), ACT.Copy).then_inc(s.tok, 1)
                for st in range(NT):
                    for d in range(2):
                        n = chunk(d, st)
                        act.wait_ge(s.u, i * 8 + (2 * st + d + 1))
                        act.activation(vn[:, d, st % 2, :], bank[4 + d][:, 0:P], ACT.Copy,
                                       scale=smh[:, K_B, d, n:n + 1]).then_inc(s.vn, 1)
                act.wait_ge(s.o, i * 8 + 8)
                act.activation(osb[:], bank[0][:, :], ACT.Copy).then_inc(s.oc, 1)
                act.wait_ge(s.osum, i + 2)
                act.activation(sq[:, 0, :], osb[:], ACT.Square).then_inc(s.osq, 1)
                act.wait_ge(s.oss, i + 1)
                c.link(act.activation(rn[:, 0, :], bank[2][:, :], ACT.Ln, bias=G.eps[:, 0:1], scale=1.0 / P))
                act.activation(rn[:, 0, :], rn[:, 0, :], ACT.Exp, scale=-0.5).then_inc(s.orn, 1)
                c.clear()

        @block.vector
        def _(dve):
            c = Chain(dve, s.chain)
            dve.sem_inc(s.osum, 1)
            dve.sem_inc(s.fin, 1)
            dve.sem_inc(s.conv, 1)
            c.link(dve.memset(cb[:], 0.0))
            dve.wait_ge(s.ab, 1)
            dve.wait_ge(s.small, 80)
            c.link(dve.tensor_copy(ab[:], bank[0][:, 0:NT * 32].rearrange("p (t c) -> p t c", c=32)))
            c.link(dve.tensor_tensor(tmp[:, 0], ab[:, :, 0:16], dtb[:].unsqueeze(1).to_broadcast([P, NT, 16]), ALU.add))
            dve.tensor_scalar(tmp[:, 1], tmp[:, 0], 0.0, None, ALU.max)
            c.link(dve.tensor_scalar(tmp[:, 2], tmp[:, 0], -1.0, None, ALU.mult))
            dve.tensor_tensor(tmp[:, 2], tmp[:, 0], tmp[:, 2], ALU.min).then_inc(s.abs_, 1)
            dve.wait_ge(s.sc2, 1)
            c.link(dve.tensor_scalar(alog[:], alog[:], -1.0, None, ALU.mult))
            c.link(dve.tensor_scalar(tmp[:, 5], tmp[:, 5], 1.0, None, ALU.add))
            c.link(dve.reciprocal(tmp[:, 5], tmp[:, 5]))
            dve.wait_ge(s.sc3, 1)
            c.link(dve.tensor_tensor(tmp[:, 4], tmp[:, 4], tmp[:, 1], ALU.add))
            dve.tensor_tensor(gd[:].rearrange("p m n -> p n m"), tmp[:, 4], alog[:].unsqueeze(1).to_broadcast([P, NT, 16]),
                              ALU.mult).then_inc(s.gd, 1)
            dve.wait_ge(s.gd, 1)
            smv = [sm[:, :, k, :, :].rearrange("p h d n -> p d h n") for k in range(NK)]
            dve.tensor_copy(smv[K_G], gd[:].rearrange("p (d h) n -> p d h n", d=2))
            for d in range(2):
                dve.tensor_copy(sm[:, :, K_B, d, :], tmp[:, 5, :, d * 8:(d + 1) * 8].rearrange("p n h -> p h n"))
            dve.wait_ge(s.cum, 1)
            cum = bank[1][:, 0:64].rearrange("p (d h n) -> p d h n", d=2, h=8)
            tot = bank[1][:, 64:128].rearrange("p (d h n) -> p d h n", d=2, h=8)
            c.link(dve.tensor_copy(smv[K_GC], cum))
            dve.tensor_copy(smv[K_ESUM], tot).then_inc(s.cums, 1)
            dve.tensor_tensor(smv[K_EGL], tot, smv[K_GC], ALU.subtract).then_inc(s.cums, 1)
            dve.wait_ge(s.sc3, 2)
            dve.tensor_scalar(smv[K_NEG], smv[K_NEG], -1.0, None, ALU.mult).then_inc(s.sm_ready, 1)
            dve.wait_ge(s.sm_ready, 1)
            c.clear()
            with dve.Fori(0, GH) as i:
                dve.wait_ge(s.fin, i + 1)
                smf, smhf = sm[:].rearrange("p h k d n -> p h (k d n)"), smh[:].rearrange("p k d n -> p (k d n)")
                dve.tensor_scalar(smhf.unsqueeze(1), smf[:, ds(i, 1), :], 1.0, None, ALU.mult).then_inc(s.smh, 1)
                c.link(dve.tensor_scalar(cwh[:].unsqueeze(1), cw[:, ds(i, 1), :], 1.0, None, ALU.mult))
                for j in range(3):
                    dve.wait_ge(s.cb, i * 4 + (j + 3))
                    c.link(dve.tensor_scalar(cv[:, j, :], cb[:, j, 0:T], cwh[:, 5 * j:5 * j + 1], None, ALU.mult))
                    for tap in range(1, 5):
                        ins = dve.scalar_tensor_tensor(cv[:, j, :], cb[:, j, tap:tap + T], cwh[:, 5 * j + tap:5 * j + tap + 1],
                                                       cv[:, j, :], ALU.mult, ALU.add)
                        if tap < 4:
                            c.link(ins)
                    ins.then_inc(s.conv, 1)
                for d in range(2):
                    dve.wait_ge(s.rb, i * 2 + (d + 1))
                    c.link(dve.tensor_tensor(Dx[:, d], four(bank[4 + d]), each4(smh[:, K_GC, d, :]), ALU.subtract))
                    dve.tensor_scalar(Dx[:, d], Dx[:, d], 0.0, None, ALU.min).then_inc(s.dmin, 1)
                dve.wait_ge(s.rn, i * 2 + 1)
                dve.scalar_tensor_tensor(qT[:], cv[:, 0, :], P ** -0.5, rn[:, 0, :], ALU.mult, ALU.mult).then_inc(s.qk, 1)
                dve.wait_ge(s.rn, i * 2 + 2)
                dve.tensor_tensor(kT[:], cv[:, 1, :], rn[:, 1, :], ALU.mult).then_inc(s.qk, 1)
                for d in range(2):
                    dve.wait_ge(s.dexp, i * 2 + (d + 1))
                    c.link(dve.tensor_tensor(Dx[:, d], Dx[:, d], over4(incl[d]), ALU.mult))
                    dve.wait_ge(s.bst, i * 2 + (d + 1))
                    c.link(dve.tensor_tensor(bst[:, d], bst[:, d], Dx[:, d], ALU.mult))
                    dve.wait_ge(s.kk, i + 1)
                    dve.tensor_tensor(AqT[:, d], Dx[:, d], four(bank[7]), ALU.mult)
                    dve.tensor_tensor(NTm[:, d], bst[:, d], four(bank[6]), ALU.mult).then_inc(s.nt, 1)
                dve.wait_ge(s.nt, i * 2 + 2)
                invert_dve(dve, G, s, *inv, i * 14, i * 12)
                for st in range(NT):
                    if st:
                        for d in range(2):
                            n = chunk(d, st)
                            dve.wait_ge(s.ks, i * 6 + (2 * (st - 1) + d + 1))
                            dve.scalar_tensor_tensor(R[:, d, st % 2, :], bank[2 + d][:, 0:P], smh[:, K_NEG, d, n:n + 1],
                                                     vtok[:, n, :], ALU.mult, ALU.add).then_inc(s.r, 1)
                    if st < NT - 1:
                        for d in range(2):
                            n = chunk(d, st)
                            dve.wait_ge(s.su, i * 6 + (2 * st + d + 1))
                            if st:
                                dve.wait_ge(s.st, i * 6 + (2 * (st - 1) + d + 1))
                                ins = dve.scalar_tensor_tensor(S[:, d, st % 2, :], S[:, d, (st - 1) % 2, :], smh[:, K_ESUM, d, n:n + 1],
                                                               bank[6 + d][:, 0:P], ALU.mult, ALU.add)
                            else:
                                ins = dve.tensor_copy(S[:, d, 0, :], bank[6 + d][:, 0:P])
                            ins.then_inc(s.st, 1)
                dve.wait_ge(s.oc, i + 1)
                dve.tensor_tensor(osb[:], osb[:], bank[1][:, :], ALU.add).then_inc(s.osum, 1)
                dve.wait_ge(s.orn, i + 1)
                c.link(dve.scalar_tensor_tensor(osb[:], osb[:], na[:, 0:1], rn[:, 0, :], ALU.mult, ALU.mult))
                dve.tensor_tensor(G.oaT[:, ds(i, 1), :], osb[:].unsqueeze(1), zs[:].unsqueeze(1), ALU.mult).then_inc(s.fin, 1)
                c.clear()


def merge_phase(nc, G, name, w_a, w_b, wg_dram, cols, gate_bias=None):
    ka, kb = w_a.shape[0] // P, w_b.shape[0] // P
    kn = (ka, kb, KT, KT)
    with Phase(nc, name, "gates mm sig part mixed chain bias_in bias_h") as ph:
        s = ph.s
        w_ready = ph.sems("w_ready", 8)
        wr = ph.sb("wr", [P, 8, KT, P])
        sg = ph.sb("sg", [P, 2, 2, T])
        gb = ph.sb("gb", [P, KT, 2])
        gbh = ph.sb("gbh", [P, 2, 2])
        bank = ph.banks()
        block = ph.block()
        views = [w.rearrange("(k p) c -> p k c", p=P) for w in (w_a, w_b, wg_dram, wg_dram)]
        first = (0, 0) + tuple(cols)
        ops = (G.oaT, G.obT, G.hT, G.hT)

        @block.sync
        def _(sp):
            if gate_bias is not None:
                sp.dma_start(gb[:], gate_bias).then_inc(s.bias_in, 16)
            for m in range(8):
                j, n = m // 4, m % 4
                sp.dma_start(wr[:, m, 0:kn[n]], views[n][:, :, first[n] + j * P:first[n] + (j + 1) * P]).then_inc(w_ready[m], 16)
            with sp.Fori(1, KT // 2) as i:
                for m in range(8):
                    j, n = m // 4, m % 4
                    col = sp.snap(i * 2 * P + (first[n] + j * P))
                    used = sp.snap(i * 8 + (m + 1 - 8))
                    sp.wait_ge(s.mm, used)
                    sp.dma_start(wr[:, m, 0:kn[n]], views[n][:, :, ds(col, P)]).then_inc(w_ready[m], 16)

        @block.tensor
        def _(pe):
            with pe.Fori(0, KT // 2) as i:
                for m in range(8):
                    j, n = m // 4, m % 4
                    if n == 0:
                        pe.wait_ge(s.mixed, i * 2 + (j + 1))
                    pe.wait_ge(w_ready[m], i * 16 + 16)
                    for k in range(kn[n]):
                        ins = pe.matmul(bank[m][:, :], wr[:, m, k, :], ops[n][:, k, :], start=(k == 0), stop=(k == kn[n] - 1))
                    ins.then_inc(s.mm, 1)

        @block.scalar
        def _(act):
            with act.Fori(0, KT // 2) as i:
                for j in range(2):
                    act.wait_ge(s.mixed, i * 2 + (j + 1))
                    if gate_bias is not None:
                        act.wait_ge(s.bias_h, i * 2 + (j + 1))
                    for n in range(2):
                        act.wait_ge(s.mm, i * 8 + (j * 4 + n + 3))
                        act.activation(sg[:, j, n, :], bank[j * 4 + 2 + n][:, :], ACT.Sigmoid,
                                       bias=gbh[:, j, n:n + 1] if gate_bias is not None else 0.0).then_inc(s.sig, 1)

        @block.vector
        def _(dve):
            dve.sem_inc(s.mixed, 2)
            if gate_bias is not None:
                dve.wait_ge(s.bias_in, 16)
            with dve.Fori(0, KT // 2) as i:
                for j in range(2):
                    if gate_bias is not None:
                        dve.wait_ge(s.mixed, i * 2 + (j + 1))
                        dve.tensor_scalar(gbh[:, j:j + 1, :], gb[:, ds(i * 2 + j, 1), :], 1.0, None, ALU.mult).then_inc(s.bias_h, 1)
                for j in range(2):
                    for n in range(2):
                        dve.wait_ge(s.sig, i * 4 + (j * 2 + n + 1))
                        dve.tensor_tensor(sg[:, j, n, :], sg[:, j, n, :], bank[j * 4 + n][:, :], ALU.mult).then_inc(s.part, 1)
                    dve.wait_ge(s.part, i * 4 + (j * 2 + 2))
                    dve.tensor_tensor(G.mT[:, ds(i * 2 + j, 1), :], sg[:, j, 0:1, :], sg[:, j, 1:2, :], ALU.add).then_inc(s.mixed, 1)


def out_phase(nc, G, name, w_out, residual):
    with Phase(nc, name, "done chain") as ph:
        s = ph.s
        w_ready = ph.sems("w_ready", KT)
        wr = ph.sb("wr", [P, KT, D])
        bank = ph.banks()
        block = ph.block()

        @block.sync
        def _(sp):
            for k in range(KT):
                sp.dma_start(wr[:, k, :], w_out[k * P:(k + 1) * P, :]).then_inc(w_ready[k], 16)

        @block.tensor
        def _(pe):
            for k in range(KT):
                pe.wait_ge(w_ready[k], 16)
                for t in range(NT):
                    for half in range(2):
                        ins = pe.matmul(bank[2 * t + half][:, :], G.mT[:, k, t * P:(t + 1) * P], wr[:, k, half * 512:(half + 1) * 512],
                                        start=(k == 0), stop=(k == KT - 1))
                        if k == KT - 1:
                            ins.then_inc(s.done, 1)

        @block.vector
        def _(dve):
            for b in range(8):
                dve.wait_ge(s.done, b + 1)
                t, c0 = b // 2, slice((b % 2) * 512, (b % 2 + 1) * 512)
                if residual:
                    dve.tensor_tensor(G.X[:, t, c0], G.X[:, t, c0], bank[b][:, :], ALU.add)
                else:
                    dve.tensor_copy(G.Y[:, t, c0], bank[b][:, :])


def mlp_phase(nc, G, name, groups, view_up, view_gate, view_down, comb=None):
    gated = view_gate is not None
    nu = 4 if gated else 2
    with Phase(nc, name, "up hid relu down added comb_h zero he") as ph:
        s = ph.s
        names = ("up", "gate", "down") if gated else ("up", "down")
        ready = {n: ph.sems(f"{n}_ready", 2) for n in names}
        wu = ph.sb("wu", [P, 2, KT, DE])
        wg = ph.sb("wg", [P, 2, KT, DE]) if gated else None
        wd = ph.sb("wd", [P, 2, 2, D])
        he = ph.sb("he", [P, 2, 2, T])
        rl = ph.sb("rl", [P, 2, T])
        ce = ph.sb("ce", [P, 2, NT])
        bank = ph.banks()
        block = ph.block()

        @block.sync
        def _(sp):
            def load(g, j, waits):
                for n in names:
                    if waits is not None:
                        sp.wait_ge(*waits[n])
                    dst, view = {"up": (wu, view_up), "gate": (wg, view_gate), "down": (wd, view_down)}[n]
                    sp.dma_start(dst[:, j], view(g)).then_inc(ready[n][j], 16)

            load(0, 0, None)
            load(1, 1, None)
            with sp.Fori(1, groups // 2) as i:
                for j in range(2):
                    g = sp.snap(i * 2 + j)
                    upv = sp.snap((i * 2 + (j - 1)) * nu)
                    dnv = sp.snap((i * 2 + (j - 1)) * 8)
                    load(g, j, {"up": (s.up, upv), "gate": (s.up, upv), "down": (s.down, dnv)})

        @block.tensor
        def _(pe):
            def up(i, j):
                for n in names[:-1]:
                    pe.wait_ge(ready[n][j], i * 16 + 16)
                for m in range(nu):
                    f, w = (m // 2, (wg, wu)[m % 2]) if gated else (m, wu)
                    b = m if gated else 2 * j + m
                    if gated:
                        if m == 0:
                            pe.wait_ge(s.he, (i * 2 + j) * 2 + 2)
                    elif m == 0:
                        pe.wait_ge(s.relu, (i * 2 + j) * 2 + 2)
                    for k in range(KT):
                        ins = pe.matmul(bank[b][:, :], w[:, j, k, f * P:(f + 1) * P], G.hT[:, k, :], start=(k == 0), stop=(k == KT - 1))
                    ins.then_inc(s.up, 1)

            def down(i, j):
                pe.wait_ge(ready["down"][j], i * 16 + 16)
                pe.wait_ge(s.he, (i * 2 + j) * 2 + 2 + 2)
                for o in range(8):
                    t, half = o // 2, o % 2
                    pe.wait_ge(s.added, (i * 2 + j) * 8 + (o + 1))
                    for f in range(2):
                        ins = pe.matmul(bank[4 + o % 4][:, :], he[:, j, f, t * P:(t + 1) * P], wd[:, j, f, half * 512:(half + 1) * 512],
                                        start=(f == 0), stop=(f == 1))
                    ins.then_inc(s.down, 1)

            up(0, 0)
            with pe.Fori(0, groups // 2 - 1) as i:
                up(i, 1)
                down(i, 0)
                up(i + 1, 0)
                down(i, 1)
            last = groups // 2 - 1
            up(last, 1)
            down(last, 0)
            down(last, 1)

        @block.scalar
        def _(act):
            act.sem_inc(s.relu, 4)
            with act.Fori(0, groups // 2) as i:
                for j in range(2):
                    for f in range(2):
                        if gated:
                            act.wait_ge(s.up, (i * 2 + j) * nu + (2 * f + 1))
                            act.wait_ge(s.he, (i * 2 + j) * 2 + f + 1)
                            act.activation(rl[:, f, :], bank[2 * f][:, :], ACT.Silu).then_inc(s.relu, 1)
                        else:
                            act.wait_ge(s.up, (i * 2 + j) * nu + (f + 1))
                            act.wait_ge(s.he, (i * 2 + j) * 2 + f + 1)
                            act.activation(rl[:, f, :], bank[2 * j + f][:, :], ACT.Relu).then_inc(s.relu, 1)

        @block.vector
        def _(dve):
            dve.sem_inc(s.he, 2)
            dve.sem_inc(s.added, 4)
            dve.memset(G.Y[:], 0.0).then_inc(s.zero, 1)
            dve.wait_ge(s.zero, 1)

            def hidden(i, j):
                if gated:
                    if not (isinstance(i, int) and i == 0 and j == 0):
                        dve.wait_ge(s.added, (i * 2 + j) * 8 - 4)
                    dve.tensor_scalar(ce[:, j:j + 1, :], comb[:, ds(i * 2 + j, 1), :] if not isinstance(i, int)
                                      else comb[:, 2 * i + j:2 * i + j + 1, :], 1.0, None, ALU.mult).then_inc(s.comb_h, 1)
                for f in range(2):
                    dve.wait_ge(s.relu, (i * 2 + j) * 2 + (f + 1 + 4))
                    if gated:
                        dve.wait_ge(s.up, (i * 2 + j) * nu + (2 * f + 2))
                        dve.tensor_tensor(he[:, j, f, :], rl[:, f, :], bank[2 * f + 1][:, :], ALU.mult).then_inc(s.he, 1)
                    else:
                        dve.tensor_tensor(he[:, j, f, :], rl[:, f, :], rl[:, f, :], ALU.mult).then_inc(s.he, 1)

            def add(i, j):
                if gated:
                    dve.wait_ge(s.comb_h, i * 2 + (j + 1))
                for o in range(8):
                    y = G.Y[:, o // 2, (o % 2) * 512:(o % 2 + 1) * 512]
                    dve.wait_ge(s.down, (i * 2 + j) * 8 + (o + 1))
                    if o == 0:
                        dve.wait_ge(s.added, (i * 2 + j) * 8 + 4)
                    if gated:
                        ins = dve.scalar_tensor_tensor(y, bank[4 + o % 4][:, :], ce[:, j, o // 2:o // 2 + 1], y, ALU.mult, ALU.add)
                    else:
                        ins = dve.tensor_tensor(y, y, bank[4 + o % 4][:, :], ALU.add)
                    ins.then_inc(s.added, 1)

            hidden(0, 0)
            with dve.Fori(0, groups // 2 - 1) as i:
                hidden(i, 1)
                add(i, 0)
                hidden(i + 1, 0)
                add(i, 1)
            last = groups // 2 - 1
            hidden(last, 1)
            add(last, 0)
            add(last, 1)


SLOTS = 40


def router_phase(nc, G, w_router, b_router, rows, expert, place, weight):
    NR = NGRP + NEXP
    with Phase(nc, "rt", "ins mm dif e1 e2 picked counted sel listed chain") as ph:
        s = ph.s
        wr = ph.sb("wr", [P, KT, NR])
        br = ph.sb("br", [P, NR])
        lg = ph.sb("lg", [P, NT, NR])
        w4 = ph.sb("w4", [P, 4, NT, NGRP])
        w32 = ph.sb("w32", [P, 5, NT, NEXP])
        c1 = ph.sb("c1", [P, 10, NT])
        both = ph.sb("both", [P, NT, NEXP])
        cnt = ph.sb("cnt", [P, NT, NEXP])
        ne = ph.sb("ne", [P, 6, NEXP])
        pos = ph.sb("pos", [P, 6, 2, NT])
        R1 = ph.sb("R1", [P, 2, NT, P])
        S1 = ph.sb("S1", [P, 2, NT, SLOTS])
        past = ph.sb("past", [P, SLOTS, NEXP])
        es = ph.sb("es", [P, SLOTS])
        bank = ph.banks(3)
        block = ph.block()

        @block.sync
        def _(sp):
            sp.dma_start(wr[:], w_router.rearrange("(k p) c -> p k c", p=P)).then_inc(s.ins, 16)
            sp.dma_start(br[:], bcast_rows(b_router, 1, NR)).then_inc(s.ins, 16)

        @block.tensor
        def _(pe):
            pe.wait_ge(s.ins, 32)
            for t in range(NT):
                for k in range(KT):
                    ins = pe.matmul(bank[0][:, t * NR:(t + 1) * NR], G.hT[:, k, t * P:(t + 1) * P], wr[:, k, :],
                                    start=(k == 0), stop=(k == KT - 1))
            ins.then_inc(s.mm, 1)
            pe.wait_ge(s.picked, 1)
            for t in range(NT):
                for u in range(t + 1):
                    pe.matmul(bank[1][:, t * NEXP:(t + 1) * NEXP], G.c("lt" if u == t else "ones"), both[:, u, :],
                              start=(u == 0), stop=(u == t))
            for u in range(NT):
                ins = pe.matmul(bank[1][:, NT * NEXP:(NT + 1) * NEXP], G.c("ones"), both[:, u, :], start=(u == 0), stop=(u == NT - 1))
            ins.then_inc(s.counted, 1)
            pe.wait_ge(s.sel, 1)
            for m in range(2 * NT):
                ins = pe.matmul(bank[2][:, 0:SLOTS], R1[:, m // NT, m % NT, :], S1[:, m // NT, m % NT, :],
                                start=(m == 0), stop=(m == 2 * NT - 1))
            ins.then_inc(s.listed, 1)

        @block.scalar
        def _(act):
            act.wait_ge(s.dif, 1)
            act.activation(w4[:, 1], w4[:, 1], ACT.Exp).then_inc(s.e1, 1)
            act.wait_ge(s.dif, 2)
            act.activation(c1[:, 6], c1[:, 6], ACT.Exp).then_inc(s.e2, 1)

        @block.vector
        def _(dve):
            c = Chain(dve, s.chain)

            def wide(col, n):
                return col.unsqueeze(2).to_broadcast([P, NT, n])

            def first_max(x, n, value, mask, work):
                index = G.c("idx", 0, n).unsqueeze(1).to_broadcast([P, NT, n])
                c.link(dve.tensor_reduce(value, x, AX, ALU.max))
                c.link(dve.tensor_tensor(work, x, wide(value, n), ALU.is_equal))
                c.link(dve.tensor_tensor(work, work, index, ALU.mult))
                c.link(dve.tensor_reduce(c1[:, 9], work, AX, ALU.max))
                c.link(dve.tensor_tensor(mask, work, wide(c1[:, 9], n), ALU.is_equal))

            dve.wait_ge(s.mm, 1)
            c.link(dve.tensor_tensor(lg[:], bank[0][:, 0:NT * NR].rearrange("p (t c) -> p t c", t=NT),
                                     br[:].unsqueeze(1).to_broadcast([P, NT, NR]), ALU.add))
            g, e = lg[:, :, 0:NGRP], lg[:, :, NGRP:NR]
            first_max(g, NGRP, c1[:, 0], w4[:, 0], w4[:, 2])
            dve.tensor_tensor(w4[:, 1], g, wide(c1[:, 0], NGRP), ALU.subtract).then_inc(s.dif, 1)
            dve.wait_ge(s.e1, 1)
            c.link(dve.tensor_reduce(c1[:, 1], w4[:, 1], AX, ALU.add))
            c.link(dve.reciprocal(c1[:, 2], c1[:, 1]))
            em, el = w32[:, 0], w32[:, 1]
            for q in range(NGRP):
                ins = dve.tensor_scalar(em[:, :, 8 * q:8 * q + 8], w4[:, 0, :, q:q + 1].to_broadcast([P, NT, 8]), 1.0, None, ALU.mult)
            c.link(ins)
            c.link(dve.tensor_tensor(el, e, em, ALU.mult))
            c.link(dve.tensor_scalar(em, em, -NEG, NEG, ALU.mult, ALU.add))
            c.link(dve.tensor_tensor(el, el, em, ALU.add))
            first_max(el, NEXP, c1[:, 3], w32[:, 2], w32[:, 4])
            c.link(dve.tensor_scalar(em, w32[:, 2], NEG, None, ALU.mult))
            c.link(dve.tensor_tensor(el, el, em, ALU.add))
            first_max(el, NEXP, c1[:, 4], w32[:, 3], w32[:, 4])
            dve.tensor_tensor(c1[:, 6], c1[:, 4], c1[:, 3], ALU.subtract).then_inc(s.dif, 1)
            dve.wait_ge(s.e2, 1)
            c.link(dve.tensor_scalar(c1[:, 7], c1[:, 6], 1.0, None, ALU.add))
            c.link(dve.reciprocal(c1[:, 7], c1[:, 7]))
            c.link(dve.tensor_tensor(weight[:, :, 0], c1[:, 7], c1[:, 2], ALU.mult))
            dve.tensor_tensor(weight[:, :, 1], weight[:, :, 0], c1[:, 6], ALU.mult)
            mk = (w32[:, 2], w32[:, 3])
            dve.tensor_tensor(both[:], mk[0], mk[1], ALU.add).then_inc(s.picked, 1)
            dve.wait_ge(s.counted, 1)
            c.link(dve.tensor_copy(cnt[:], bank[1][:, 0:NT * NEXP].rearrange("p (t e) -> p t e", t=NT)))
            c.link(dve.tensor_copy(ne[:, 0], bank[1][:, NT * NEXP:(NT + 1) * NEXP]))

            def steps(out, x, first, n, spare):
                c.link(dve.tensor_scalar(out, x, float(first), None, ALU.is_ge))
                for m in range(1, n):
                    c.link(dve.tensor_scalar(spare, x, float(first + P * m), None, ALU.is_ge))
                    c.link(dve.tensor_tensor(out, out, spare, ALU.add))

            steps(ne[:, 1], ne[:, 0], 1, NT, ne[:, 2])
            c.link(dve.tensor_copy(ne[:, 3], ne[:, 1]))
            src, dst = 3, 4
            for m in range(5):
                sh = 1 << m
                c.link(dve.tensor_copy(ne[:, dst, 0:sh], ne[:, src, 0:sh]))
                c.link(dve.tensor_tensor(ne[:, dst, sh:NEXP], ne[:, src, sh:NEXP], ne[:, src, 0:NEXP - sh], ALU.add))
                src, dst = dst, src
            last = ne[:, src]
            c.link(dve.tensor_tensor(ne[:, 5], last, ne[:, 1], ALU.subtract))
            for q in range(2):
                for what, table in ((0, cnt[:]), (1, ne[:, 5].unsqueeze(1).to_broadcast([P, NT, NEXP]))):
                    c.link(dve.tensor_tensor(w32[:, 4], mk[q], table, ALU.mult))
                    c.link(dve.tensor_reduce(pos[:, what, q, :], w32[:, 4], AX, ALU.add))
            steps(pos[:, 2], pos[:, 0], P, NT - 1, pos[:, 5])
            c.link(dve.tensor_tensor(pos[:, 3], pos[:, 1], pos[:, 2], ALU.add))
            c.link(dve.scalar_tensor_tensor(pos[:, 4], pos[:, 2], -float(P), pos[:, 0], ALU.mult, ALU.add))
            c.link(dve.scalar_tensor_tensor(pos[:, 5], pos[:, 3], float(P), pos[:, 4], ALU.mult, ALU.add))
            dve.tensor_copy(place[:].rearrange("p t q -> p q t"), pos[:, 5])
            for q in range(2):
                for t in range(NT):
                    dve.tensor_scalar(R1[:, q, t, :], G.c("iota"), pos[:, 4, q, t:t + 1], G.c("tok", t, t + 1), ALU.is_equal, ALU.mult)
                    ins = dve.tensor_scalar(S1[:, q, t, :], G.c("iota", 0, SLOTS), pos[:, 3, q, t:t + 1], None, ALU.is_equal)
            ins.then_inc(s.sel, 1)
            c.link(dve.tensor_tensor(past[:], last.unsqueeze(1).to_broadcast([P, SLOTS, NEXP]),
                                     G.c("iota", 0, SLOTS).unsqueeze(2).to_broadcast([P, SLOTS, NEXP]), ALU.is_le))
            c.link(dve.tensor_reduce(es[:], past[:], AX, ALU.add))
            c.link(dve.tensor_scalar(expert[:], es[:], float(NEXP - 1), None, ALU.min))
            dve.wait_ge(s.listed, 1)
            dve.tensor_copy(rows[:], bank[2][:, 0:SLOTS])


def moe_phase(nc, G, w_gate, w_up, w_down, rows, expert, rows_dram, y_dram):
    with Phase(nc, "moe", "turned hg_in act_s hid turned2 heT gu down stored y0 y1") as ph:
        s = ph.s
        gu_ready, dn_ready, h_in, y_out = (ph.sems(n, 2) for n in ("gu_ready", "dn_ready", "h_in", "y_out"))
        wgu = ph.sb("wgu", [P, 2, KT, 2 * DE])
        wd = ph.sb("wd", [P, 2, 2, D])
        hg = ph.sb("hg", [P, 2, D])
        hgT = ph.sb("hgT", [P, 2, KT, P])
        sl = ph.sb("sl", [P, 2, DE])
        he = ph.sb("he", [P, 2, DE])
        heT = ph.sb("heT", [P, 2, 2, P])
        yo = ph.sb("yo", [P, 2, D])
        bank = ph.banks()
        block = ph.block()
        HALF = SLOTS // 2

        @block.sync
        def _(sp):
            def load(slot, j, gu_used, dn_used):
                e = sp.value_load(expert[0:1, ds(slot, 1)] if not isinstance(slot, int) else expert[0:1, slot:slot + 1],
                                  min_val=0, max_val=NEXP - 1)
                if gu_used is not None:
                    sp.wait_ge(s.gu, gu_used)
                sp.dma_start(wgu[:, j, :, 0:DE], one_of(w_gate, e)).then_inc(gu_ready[j], 16)
                sp.dma_start(wgu[:, j, :, DE:2 * DE], one_of(w_up, e)).then_inc(gu_ready[j], 16)
                if dn_used is not None:
                    sp.wait_ge(s.down, dn_used)
                sp.dma_start(wd[:, j], one_of(w_down, e)).then_inc(dn_ready[j], 16)

            load(0, 0, None, None)
            load(1, 1, None, None)
            with sp.Fori(1, HALF) as i:
                for j in range(2):
                    load(sp.snap(i * 2 + j), j, sp.snap(i * 2 + (j - 1)), sp.snap(i * 4 + 2 * (j - 1)))

        @block.gpsimd
        def _(pool):
            for slot in range(SLOTS):
                j = slot % 2
                if slot >= 2:
                    pool.wait_ge(s.turned, 2 * (slot - 1))
                pool.indirect_dma_start(hg[:, j, :], None, rows_dram, bass.IndirectOffsetOnAxis(rows[:, slot:slot + 1], 0)
                                        ).then_inc(h_in[j], 16)

        @block.tensor
        def _(pe):
            def turn(i, j):
                pe.wait_ge(h_in[j], i * 16 + 16)
                for half in range(2):
                    pe.wait_ge(s.act_s, (i * 2 + j) * 2 + half + 1)
                    for k in range(4):
                        kk = 4 * half + k
                        ins = pe.transpose(bank[half][:, k * P:(k + 1) * P], hg[:, j].rearrange("p (c k) -> p k c", k=KT)[:, kk], G.c("ident"))
                    ins.then_inc(s.turned, 1)

            def gate_up(i, j):
                pe.wait_ge(gu_ready[j], i * 32 + 32)
                pe.wait_ge(s.act_s, (i * 2 + j) * 2 + 4)
                pe.wait_ge(s.hid, i * 2 + (j + 1))
                for k in range(KT):
                    ins = pe.matmul(bank[2 + j][:, :], hgT[:, j, k, :], wgu[:, j, k, :], start=(k == 0), stop=(k == KT - 1))
                ins.then_inc(s.gu, 1)

            def turn_hidden(i, j):
                pe.wait_ge(s.hid, i * 2 + (j + 3))
                pe.wait_ge(s.heT, i * 2 + (j + 1))
                for f in range(2):
                    ins = pe.transpose(bank[4][:, f * P:(f + 1) * P], he[:, j, f * P:(f + 1) * P], G.c("ident"))
                ins.then_inc(s.turned2, 1)

            def down(i, j):
                pe.wait_ge(dn_ready[j], i * 16 + 16)
                pe.wait_ge(s.heT, i * 2 + (j + 2))
                for half in range(2):
                    pe.wait_ge(s.y0 if half == 0 else s.y1, i * 2 + (j + 1))
                    for f in range(2):
                        ins = pe.matmul(bank[5 + half][:, :], heT[:, j, f, :], wd[:, j, f, half * 512:(half + 1) * 512],
                                        start=(f == 0), stop=(f == 1))
                    ins.then_inc(s.down, 1)

            def body(i, more):
                gate_up(i, 1)
                turn_hidden(i, 0)
                if more:
                    turn(i + 1, 0)
                down(i, 0)
                if more:
                    gate_up(i + 1, 0)
                turn_hidden(i, 1)
                if more:
                    turn(i + 1, 1)
                down(i, 1)

            turn(0, 0)
            gate_up(0, 0)
            turn(0, 1)
            with pe.Fori(0, HALF - 1) as i:
                body(i, True)
            body(HALF - 1, False)

        @block.scalar
        def _(act):
            act.sem_inc(s.act_s, 2)
            act.sem_inc(s.y0, 1)

            def rows_in(i, j):
                for half in range(2):
                    act.wait_ge(s.turned, (i * 2 + j) * 2 + (half + 1))
                    if half == 0:
                        act.wait_ge(s.gu, i * 2 + (j - 1)) if not (isinstance(i, int) and i == 0) else None
                    act.activation(hgT[:, j, 4 * half:4 * half + 4, :], four(bank[half]), ACT.Copy).then_inc(s.act_s, 1)

            def silu(i, j):
                act.wait_ge(s.gu, i * 2 + (j + 1))
                act.activation(sl[:, j, :], bank[2 + j][:, 0:DE], ACT.Silu).then_inc(s.hg_in, 1)

            def take(i, j):
                act.wait_ge(s.down, (i * 2 + j) * 2 + 1)
                act.wait_ge(y_out[j], i * 16) if not (isinstance(i, int) and i == 0) else None
                act.activation(yo[:, j, 0:512], bank[5][:, :], ACT.Copy).then_inc(s.y0, 1)
                act.wait_ge(s.y0, i * 2 + (j + 2))
                act.wait_ge(s.y1, i * 2 + (j + 2))
                if isinstance(i, int):
                    act.dma_start(y_dram[(2 * i + j) * P:(2 * i + j + 1) * P, :], yo[:, j, :]).then_inc(y_out[j], 16)
                else:
                    act.dma_start(y_dram[ds(act.snap(i * (2 * P) + j * P), P), :], yo[:, j, :]).then_inc(y_out[j], 16)

            def body(i, more, first=False):
                silu(i, 1)
                if more:
                    rows_in(i + 1, 0)
                take(i, 0)
                if more:
                    silu(i + 1, 0)
                    rows_in(i + 1, 1)
                take(i, 1)

            rows_in(0, 0)
            silu(0, 0)
            rows_in(0, 1)
            body(0, True)
            with act.Fori(1, HALF - 1) as i:
                body(i, True)
            body(HALF - 1, False)
            for j in range(2):
                act.wait_ge(y_out[j], 16 * HALF)

        @block.vector
        def _(dve):
            dve.sem_inc(s.hid, 2)
            dve.sem_inc(s.heT, 1)
            dve.sem_inc(s.y1, 1)

            def hidden(i, j):
                dve.wait_ge(s.hg_in, i * 2 + (j + 1))
                if not (isinstance(i, int) and i == 0):
                    dve.wait_ge(s.turned2, i * 2 + (j - 1))
                dve.tensor_tensor(he[:, j, :], sl[:, j, :], bank[2 + j][:, DE:2 * DE], ALU.mult).then_inc(s.hid, 1)

            def take_hidden(i, j):
                dve.wait_ge(s.turned2, i * 2 + (j + 1))
                dve.tensor_copy(heT[:, j].rearrange("p f c -> p (f c)"), bank[4][:, 0:2 * P]).then_inc(s.heT, 1)

            def take(i, j):
                dve.wait_ge(s.down, (i * 2 + j) * 2 + 2)
                if not (isinstance(i, int) and i == 0):
                    dve.wait_ge(y_out[j], i * 16)
                dve.tensor_copy(yo[:, j, 512:D], bank[6][:, :]).then_inc(s.y1, 1)

            def body(i, more):
                hidden(i, 1)
                take_hidden(i, 0)
                take(i, 0)
                if more:
                    hidden(i + 1, 0)
                take_hidden(i, 1)
                take(i, 1)

            hidden(0, 0)
            body(0, True)
            with dve.Fori(1, HALF - 1) as i:
                body(i, True)
            body(HALF - 1, False)


def one_of(view, e):
    return view[ds(e, 1)].rearrange("a p k c -> p (a k) c")


def final_phase(nc, G, place, weight, y_dram, out):
    with Phase(nc, "fin", "sum out chain") as ph:
        s = ph.s
        got = ph.sems("got", 2 * NT)
        yg = ph.sb("yg", [P, 2 * NT, D])
        block = ph.block()

        @block.gpsimd
        def _(pool):
            for m in range(2 * NT):
                pool.indirect_dma_start(yg[:, m, :], None, y_dram, bass.IndirectOffsetOnAxis(place[:, m // 2, m % 2:m % 2 + 1], 0)
                                        ).then_inc(got[m], 16)

        @block.vector
        def _(dve):
            c = Chain(dve, s.chain)
            for m in range(2 * NT):
                t, q = m // 2, m % 2
                dve.wait_ge(got[m], 16)
                ins = dve.scalar_tensor_tensor(G.X[:, t], yg[:, m, :], weight[:, t, q:q + 1], G.X[:, t], ALU.mult, ALU.add)
                if q == 0:
                    c.link(ins)
                else:
                    ins.then_inc(s.sum, 1)

        @block.sync
        def _(sp):
            for t in range(NT):
                sp.wait_ge(s.sum, t + 1)
                sp.dma_start(out[0, t * P:(t + 1) * P, :], G.X[:, t, :]).then_inc(s.out, 16)
            sp.wait_ge(s.out, 16 * NT)


def grid_attention_phase(nc, G, w_in, rpb, gains, pad_dram):
    with Phase(nc, "na", "rpb_in zeroed padded pad_out toep small proj copied sqd ssq rn qk pn logits taken negmax expd "
               "p_ready turned pt out out_taken bias_ready chain achain") as ph:
        s = ph.s
        w_ready = ph.sems("w_ready", 3)
        wr = ph.sb("wr", [P, 3, KT, P])
        pad = ph.sb("pad", [120, 127])
        bias = ph.sb("bias", [P, 8, 14, 64])
        gn = ph.sb("gn", [P, 2])
        raw = ph.sb("raw", [P, 2, T])
        sq = ph.sb("sq", [P, 2, T])
        rn = ph.sb("rn", [P, 2, T])
        qT = ph.sb("qT", [P, T])
        kT = ph.sb("kT", [P, T])
        v = ph.sb("v", [P, NT, P])
        L = ph.sb("L", [P, 2, T])
        PT = ph.sb("PT", [P, 2, T])
        st = ph.sb("st", [P, 2, 4])
        bank = ph.banks()
        block = ph.block()
        cols = (N_Q, N_K, N_V)
        wv = w_in.rearrange("(k p) c -> p k c", p=P)

        @block.sync
        def _(sp):
            for n in range(3):
                sp.dma_start(wr[:, n], wv[:, :, cols[n]:cols[n] + P]).then_inc(w_ready[n], 16)
            sp.dma_start(gn[:], gains).then_inc(s.small, 16)
            sp.wait_ge(s.zeroed, 1)
            sp.dma_start(pad[:, 48:79], rpb.rearrange("h r c -> (h r) c")).then_inc(s.rpb_in, 16)
            sp.wait_ge(s.rpb_in, 16)
            sp.dma_start(pad_dram, pad[:]).then_inc(s.pad_out, 16)
            sp.wait_ge(s.pad_out, 16)
            for h in range(8):
                for half in range(2):
                    src = bass.AP(tensor=pad_dram.tensor, offset=pad_dram.offset + (h * 15 + 1 - half) * 127,
                                  ap=[[1, 64], [127, 14], [1, 64]])
                    sp.dma_start(bias[64 * half:64 * half + 64, h], src).then_inc(s.toep, 16)
            with sp.Fori(1, 4) as i:
                for n in range(3):
                    col = sp.snap(i * P + cols[n])
                    used = sp.snap(i * 3 + (n + 1 - 3))
                    sp.wait_ge(s.proj, used)
                    sp.dma_start(wr[:, n], wv[:, :, ds(col, P)]).then_inc(w_ready[n], 16)

        @block.tensor
        def _(pe):
            with pe.Fori(0, 4) as i:
                for n in range(3):
                    pe.wait_ge(w_ready[n], i * 16 + 16)
                    pe.wait_ge(s.copied, i * 3 + (n + 1))
                    if n < 2:
                        for k in range(KT):
                            ins = pe.matmul(bank[n][:, :], wr[:, n, k, :], G.hT[:, k, :], start=(k == 0), stop=(k == KT - 1))
                    else:
                        for t in range(NT):
                            for k in range(KT):
                                ins = pe.matmul(bank[2][:, t * P:(t + 1) * P], G.hT[:, k, t * P:(t + 1) * P], wr[:, n, k, :],
                                                start=(k == 0), stop=(k == KT - 1))
                    ins.then_inc(s.proj, 1)
                for n in range(2):
                    pe.wait_ge(s.sqd, i * 2 + (n + 1))
                    pe.matmul(bank[3 + n][:, :], G.c("blk64"), sq[:, n, :], start=True, stop=True).then_inc(s.ssq, 1)
                pe.wait_ge(s.qk, i * 2 + 2)
                pe.wait_ge(s.copied, i * 3 + 6)

                def logits(m):
                    e, t = m // 4, m % 4
                    pe.wait_ge(s.taken, i * 8 + (m + 1))
                    pe.matmul(bank[3][:, :], qT[64 * e:64 * e + 64, t * P:(t + 1) * P], kT[64 * e:64 * e + 64, :],
                              start=True, stop=True).then_inc(s.logits, 1)

                def values(m):
                    e, t = m // 4, m % 4
                    pe.wait_ge(s.p_ready, i * 8 + (m + 1))
                    pe.wait_ge(s.pt, i * 8 + (m + 1))
                    for n in range(NT):
                        ins = pe.transpose(bank[5][:, n * P:(n + 1) * P], L[:, m % 2, n * P:(n + 1) * P], G.c("ident"))
                    ins.then_inc(s.turned, 1)
                    pe.wait_ge(s.pt, i * 8 + (m + 2))
                    if m == 0:
                        pe.wait_ge(s.out_taken, i + 1)
                    for n in range(NT):
                        ins = pe.matmul(bank[6][64 * e:64 * e + 64, t * P:(t + 1) * P], v[:, n, 64 * e:64 * e + 64],
                                        PT[:, m % 2, n * P:(n + 1) * P], start=(n == 0), stop=(n == NT - 1))
                    ins.then_inc(s.out, 1)

                for m in range(8):
                    logits(m)
                    if m:
                        values(m - 1)
                values(7)

        @block.scalar
        def _(act):
            c = Chain(act, s.achain)
            act.sem_inc(s.copied, 3)
            act.sem_inc(s.pt, 1)
            with act.Fori(0, 4) as i:
                act.wait_ge(s.out_taken, i + 1)
                for n in range(3):
                    act.wait_ge(s.proj, i * 3 + (n + 1))
                    if n < 2:
                        act.activation(raw[:, n, :], bank[n][:, :], ACT.Copy).then_inc(s.copied, 1)
                        act.wait_ge(s.copied, i * 3 + (n + 4))
                        act.activation(sq[:, n, :], raw[:, n, :], ACT.Square).then_inc(s.sqd, 1)
                    else:
                        act.activation(v[:], four(bank[2]), ACT.Copy).then_inc(s.copied, 1)
                for n in range(2):
                    act.wait_ge(s.ssq, i * 2 + (n + 1))
                    c.link(act.activation(rn[:, n, :], bank[3 + n][:, :], ACT.Ln, bias=G.eps[:, 0:1], scale=1.0 / 64))
                    act.activation(rn[:, n, :], rn[:, n, :], ACT.Exp, scale=-0.5).then_inc(s.rn, 1)

                def exps(m):
                    act.wait_ge(s.negmax, i * 8 + (m + 1))
                    act.activation(L[:, m % 2, :], L[:, m % 2, :], ACT.Exp, bias=st[:, m % 2, 1:2],
                                   accum_out=st[:, m % 2, 2:3]).then_inc(s.expd, 1)

                def turn(m):
                    act.wait_ge(s.turned, i * 8 + (m + 1))
                    act.activation(PT[:, m % 2, :], bank[5][:, :], ACT.Copy).then_inc(s.pt, 1)

                for m in range(8):
                    exps(m)
                    if m:
                        turn(m - 1)
                turn(7)
                c.clear()

        @block.vector
        def _(dve):
            c = Chain(dve, s.chain)
            dve.sem_inc(s.taken, 1)
            dve.sem_inc(s.out_taken, 1)
            dve.memset(pad[:], 0.0).then_inc(s.zeroed, 1)
            dve.wait_ge(s.small, 16)
            c.link(dve.tensor_scalar(gn[:, 0:1], gn[:, 0:1], 64 ** -0.5, None, ALU.mult))
            dve.wait_ge(s.toep, 16 * 16)
            bf = bias[:].rearrange("p h x c -> p (h x) c")
            c.link(dve.tensor_tensor(bf, bf, G.c("colmask").unsqueeze(1).to_broadcast([P, 8 * 14, 64]), ALU.add))
            c.clear()
            with dve.Fori(0, 4) as i:
                for n in range(2):
                    dve.wait_ge(s.rn, i * 2 + (n + 1))
                    c.link(dve.tensor_tensor(raw[:, n, :], raw[:, n, :], rn[:, n, :], ALU.mult))
                    if n == 0:
                        src = raw[:, 0, :].rearrange("p (r c) -> p r c", c=NAROW)[:, :, ::-1]
                        dve.tensor_scalar(qT[:].rearrange("p (r c) -> p r c", c=NAROW), src, gn[:, 0:1], None, ALU.mult).then_inc(s.qk, 1)
                    else:
                        dve.tensor_scalar(kT[:], raw[:, 1, :], gn[:, 1:2], None, ALU.mult).then_inc(s.qk, 1)
                for m in range(8):
                    e, t, r = m // 4, m % 4, m % 2
                    if m >= 2:
                        dve.wait_ge(s.turned, i * 8 + (m - 1))
                    dve.wait_ge(s.logits, i * 8 + (m + 1))
                    b = bias[:, ds(i * 2 + e, 1), 6 - 2 * t:14 - 2 * t, :]
                    dve.tensor_tensor(L[:, r, :].rearrange("p (a x c) -> p a x c", a=1, c=64), bank[3][:, :].rearrange("p (a x c) -> p a x c", a=1, c=64),
                                      b, ALU.add).then_inc(s.taken, 1)
                    dve.wait_ge(s.taken, i * 8 + (m + 2))
                    c.link(dve.tensor_reduce(st[:, r, 0:1], L[:, r, :], AX, ALU.max))
                    dve.tensor_scalar(st[:, r, 1:2], st[:, r, 0:1], -1.0, None, ALU.mult).then_inc(s.negmax, 1)
                    dve.wait_ge(s.expd, i * 8 + (m + 1))
                    c.link(dve.reciprocal(st[:, r, 3:4], st[:, r, 2:3]))
                    dve.tensor_scalar(L[:, r, :], L[:, r, :], st[:, r, 3:4], None, ALU.mult).then_inc(s.p_ready, 1)
                dve.wait_ge(s.out, i * 8 + 8)
                src = bank[6][:, :].rearrange("p (r c) -> p r c", c=NAROW)[:, :, ::-1]
                dst = G.obT[:, ds(i, 1), :].rearrange("p a (r c) -> p (a r) c", c=NAROW)
                dve.tensor_scalar(dst, src, 1.0, None, ALU.mult).then_inc(s.out_taken, 1)
                c.clear()


def rwkv_pre_phase(nc, G, w_in, A, lw, af, gg):
    HR = 64
    with Phase(nc, "rp", "proj cb shifted act_done up lw_added out_done ins chain") as ph:
        s = ph.s
        w_ready = ph.sems("w_ready", 3)
        wr = ph.sb("wr", [P, 3, KT, P])
        mul = ph.sb("mul", [P, 5, 3])
        cb = ph.sb("cb", [P, 5, T + 2])
        lo = ph.sb("lo", [P, 5, T])
        wup = ph.sb("wup", [HR, 2, RW])
        aup = ph.sb("aup", [HR, 2, RW])
        gup = ph.sb("gup", [P, RW])
        w0 = ph.sb("w0", [P, 2, RW])
        a0 = ph.sb("a0", [P, 2, 4])
        bank = ph.banks()
        block = ph.block()
        wv = w_in.rearrange("(k p) c -> p k c", p=P)

        @block.sync
        def _(sp):
            for n in range(3):
                c0 = R_LORA + n * P
                sp.dma_start(wr[:, n], wv[:, :, c0:c0 + P]).then_inc(w_ready[n], 16)
            for dst, src in ((mul[:], A.mu_lora), (wup[:, 0], A.w_up_f[0]), (wup[:, 1], A.w_up_b[0]), (aup[:, 0], A.a_up_f[0]),
                             (aup[:, 1], A.a_up_b[0]), (gup[:], A.g_up[0]), (w0[:, 0], bcast_rows(A.w0_f, 1, RW)),
                             (w0[:, 1], bcast_rows(A.w0_b, 1, RW)), (a0[:], A.a0)):
                sp.dma_start(dst, src).then_inc(s.ins, 16)

        parts = ((0, 0, HR), (0, HR, HR), (1, 0, HR), (1, HR, HR), (2, 0, P))

        @block.tensor
        def _(pe):
            for j, (n, c0, m) in enumerate(parts):
                pe.wait_ge(w_ready[n], 16)
                for k in range(KT):
                    ins = pe.matmul(bank[j][0:m, :], wr[:, n, k, c0:c0 + m], G.hT[:, k, :], start=(k == 0), stop=(k == KT - 1))
                ins.then_inc(s.proj, 1)
            pe.wait_ge(s.ins, 16 * 9)
            pe.wait_ge(s.cb, 5)
            pe.wait_ge(s.act_done, 3)
            for o in range(20):
                if o < 8:
                    d, n = o // 4, o % 4
                    ins = pe.matmul(bank[o][:, :], lo[0:HR, d, n * P:(n + 1) * P], wup[:, d, :], start=True, stop=True)
                elif o < 16:
                    d, n = (o - 8) // 4, o % 4
                    pe.wait_ge(s.lw_added, o - 7)
                    ins = pe.matmul(bank[o - 8][:, :], aup[:, d, n * P:(n + 1) * P], lo[0:HR, 2 + d, :], start=True, stop=True)
                else:
                    n = o - 16
                    pe.wait_ge(s.out_done, n + 1)
                    ins = pe.matmul(bank[n][:, :], gup[:, n * P:(n + 1) * P], lo[:, 4, :], start=True, stop=True)
                ins.then_inc(s.up, 1)

        @block.scalar
        def _(act):
            act.wait_ge(s.shifted, 1)
            for j, (n, c0, m) in enumerate(parts):
                act.wait_ge(s.proj, j + 1)
                act.activation(cb[0:m, j, 1:T + 1], bank[j][0:m, :], ACT.Copy).then_inc(s.cb, 1)
            act.wait_ge(s.shifted, 6)
            for j, func in ((0, ACT.Tanh), (1, ACT.Tanh), (4, ACT.Sigmoid)):
                m = parts[j][2]
                act.activation(lo[0:m, j, :], lo[0:m, j, :], func).then_inc(s.act_done, 1)
            for o in range(8, 20):
                n = o % 4
                act.wait_ge(s.up, o + 1)
                if o < 16:
                    d = (o - 8) // 4
                    act.activation(af[:, d, n, :], bank[o - 8][:, :], ACT.Sigmoid, bias=a0[:, d, n:n + 1]).then_inc(s.out_done, 1)
                else:
                    act.activation(gg[:, n, :], bank[n][:, :], ACT.Copy).then_inc(s.out_done, 1)
            act.wait_ge(s.lw_added, 8)
            for d in range(2):
                act.activation(lw[:, d], lw[:, d], ACT.Sigmoid)

        @block.vector
        def _(dve):
            c = Chain(dve, s.chain)
            dve.memset(cb[:], 0.0).then_inc(s.shifted, 1)
            dve.wait_ge(s.ins, 16 * 9)
            c.link(dve.tensor_tensor(mul[:, :, 1:2], mul[:, :, 0:1], mul[:, :, 2:3], ALU.add))
            c.link(dve.tensor_scalar(mul[:, :, 1:2], mul[:, :, 1:2], -1.0, 1.0, ALU.mult, ALU.add))
            for j, (n, c0, m) in enumerate(parts):
                dve.wait_ge(s.cb, j + 1)
                c.link(dve.tensor_scalar(lo[0:m, j, :], cb[0:m, j, 0:T], mul[0:m, j, 0:1], None, ALU.mult))
                c.link(dve.scalar_tensor_tensor(lo[0:m, j, :], cb[0:m, j, 1:T + 1], mul[0:m, j, 1:2], lo[0:m, j, :], ALU.mult, ALU.add))
                dve.scalar_tensor_tensor(lo[0:m, j, :], cb[0:m, j, 2:T + 2], mul[0:m, j, 2:3], lo[0:m, j, :], ALU.mult, ALU.add).then_inc(s.shifted, 1)
            for o in range(8):
                dve.wait_ge(s.up, o + 1)
                dve.tensor_tensor(lw[:, o // 4, o % 4, :], bank[o][:, :], w0[:, o // 4, :], ALU.add).then_inc(s.lw_added, 1)


def rwkv_phase(nc, G, w_in, A, lw, af, gg):
    HR = 64
    with Phase(nc, "rw", "small proj cb shifted lwp cum cs ex sc kkp sq ssq rn feat ft tok gram nt x xs yz tw "
               "rhs rr uu un su st yy yc ys mean cen sq2 var rv bon bo fin chain achain pads dropped") as ph:
        s = ph.s
        w_ready = ph.sems("w_ready", 3)
        wr = ph.sb("wr", [P, 3, KT, P])
        mu = ph.sb("mu", [P, 4, 9])
        muh = ph.sb("muh", [P, 3, 3])
        par = ph.sb("par", [P, 4, 6])
        parh = ph.sb("parh", [P, 6])
        rkv = ph.sb("rkv", [P, 3, T])
        ar = ph.sb("ar", [P, 2, T])
        kkp = ph.sb("kkp", [P, T])
        sq = ph.sb("sq", [P, T])
        rn = ph.sb("rn", [P, T])
        ft = ph.sb("ft", [P, 2, 4, T])
        tk = ph.sb("tk", [P, 2, 2, NT, P])
        vtok = ph.sb("vtok", [P, NT, P])
        NTm = ph.sb("NTm", [P, 2, 2, NT, P])
        GA = ph.sb("GA", [P, 3, 2, 2, NT, P])
        Tm = ph.sb("Tm", [P, 2, NT, P])
        Xs = ph.sb("Xs", [P, 2, NT, P])
        Wm = ph.sb("Wm", [P, 2, 2, NT, P])
        ms = ph.sb("ms", [P, 6, 2, NT])
        S = ph.sb("S", [P, 2, 2, P])
        St = ph.sb("St", [P, 2, P])
        R = ph.sb("R", [P, 2, 2, P])
        bank = ph.banks()
        block = ph.block()
        wv = w_in.rearrange("(k p) c -> p k c", p=P)
        cb = NTm[:].rearrange("p a b c d -> p (a b c d)")[:, 0:3 * (T + 2)].rearrange("p (j c) -> p j c", j=3)
        lwp = Wm[:, 0]
        Ein, Eex = Tm, Xs
        Einv = GA[:, 2, 0]
        ysb = kkp
        un = ar[:, 1, :].rearrange("p (d a c) -> p d a c", d=2, a=2)
        kd = GA[:, 0, 0].rearrange("p d n c -> p d (n c)")
        kk = GA[:, 1, 0, 0].rearrange("p n c -> p (n c)")
        incl, strict = (G.c("le"), G.c("ge")), (G.c("lt"), G.c("gt"))
        A_, B_, K_, R_ = range(4)
        flat = lambda a: a.rearrange("p n c -> p (n c)")

        def chunk(d, st):
            return st if d == 0 else NT - 1 - st

        @block.sync
        def _(sp):
            for n in range(3):
                sp.dma_start(wr[:, n], wv[:, :, n * RW:n * RW + P]).then_inc(w_ready[n], 16)
            sp.dma_start(mu[:], A.mu_rkv).then_inc(s.small, 16)
            sp.dma_start(par[:], A.rw_par).then_inc(s.small, 16)
            with sp.Fori(1, 4) as i:
                for n in range(3):
                    col = sp.snap(i * P + n * RW)
                    used = sp.snap(i * 3 + (n + 1 - 3))
                    sp.wait_ge(s.proj, used)
                    sp.dma_start(wr[:, n], wv[:, :, ds(col, P)]).then_inc(w_ready[n], 16)

        grams = [(ty, e, d) for e in range(2) for d in range(2) for ty in range(4)]
        gram_ops = ((B_, A_), (K_, A_), (B_, R_), (K_, R_))

        @block.tensor
        def _(pe):
            with pe.Fori(0, 4) as i:
                pe.wait_ge(s.fin, i + 1)
                for n in range(3):
                    pe.wait_ge(w_ready[n], i * 16 + 16)
                    for k in range(KT):
                        ins = pe.matmul(bank[n][:, :], wr[:, n, k, :], G.hT[:, k, :], start=(k == 0), stop=(k == KT - 1))
                    ins.then_inc(s.proj, 1)
                for d in range(2):
                    pe.wait_ge(s.lwp, i * 2 + (d + 1))
                    for m, (b, mask) in enumerate(((3, incl[d]), (5, strict[d]))):
                        for n in range(NT):
                            ins = pe.matmul(bank[b + d][:, n * P:(n + 1) * P], lwp[:, d, n, :], mask, start=True, stop=True)
                    ins.then_inc(s.cum, 1)
                pe.wait_ge(s.sq, i + 1)
                pe.matmul(bank[7][:, :], G.c("blk64"), sq[:, :], start=True, stop=True).then_inc(s.ssq, 1)
                pe.wait_ge(s.rn, i + 1)
                pe.wait_ge(s.ex, i + 1)
                for d in range(2):
                    pe.wait_ge(s.ft, i * 2 + (d + 1))
                    for m, kind in enumerate((B_, K_)):
                        for n in range(NT):
                            ins = pe.transpose(bank[3 + 2 * d + m][:, n * P:(n + 1) * P], ft[:, d, kind, n * P:(n + 1) * P], G.c("ident"))
                        ins.then_inc(s.feat, 1)
                for n in range(NT):
                    ins = pe.transpose(bank[7][:, n * P:(n + 1) * P], rkv[:, 2, n * P:(n + 1) * P], G.c("ident"))
                ins.then_inc(s.feat, 1)
                pe.wait_ge(s.cb, i * 3 + 3)
                for m, (ty, e, d) in enumerate(grams):
                    if m < 8 and m >= 3:
                        pe.wait_ge(s.tok, i * 5 + (m - 2))
                    if m >= 8:
                        pe.wait_ge(s.gram, i * 16 + (m - 7))
                    l, r = gram_ops[ty]
                    for n in range(NT):
                        c0 = slice(n * P, (n + 1) * P)
                        ins = pe.matmul(bank[m % 8][:, c0], ft[64 * e:64 * e + 64, d, l, c0], ft[64 * e:64 * e + 64, d, r, c0],
                                        start=True, stop=True)
                    ins.then_inc(s.nt, 1)
                pe.wait_ge(s.gram, i * 16 + 16)
                for e in range(2):
                    invert_pe(pe, G, InvertSems(s.tw, s.xs, s.x, s.yz, s.gram), NTm[:, e], Tm, Wm[:, e], Xs,
                              ((bank[2], bank[3]), (bank[4], bank[5]), (bank[6], bank[7])), i * 16, i * 28 + e * 14)
                for st in range(NT):
                    for d in range(2):
                        n = chunk(d, st)
                        c0 = slice(n * P, (n + 1) * P)
                        if st:
                            pe.wait_ge(s.st, i * 6 + (2 * (st - 1) + d + 1))
                        else:
                            pe.wait_ge(s.tw, i * 28 + 28)
                        if st:
                            pe.matmul(bank[2 + d][:, 0:P], ft[:, d, A_, c0], S[:, d, (st - 1) % 2, :], start=True, stop=False)
                        for e in range(2):
                            h0 = slice(64 * e, 64 * e + 64)
                            ins = pe.matmul(bank[2 + d][:, h0], GA[:, 0, e, d, n, :], vtok[:, n, h0], start=(st == 0), stop=(st == 0 or e == 1))
                        ins.then_inc(s.rhs, 1)
                    for d in range(2):
                        n = chunk(d, st)
                        pe.wait_ge(s.rr, i * 8 + (2 * st + d + 1))
                        for e in range(2):
                            h0 = slice(64 * e, 64 * e + 64)
                            ins = pe.matmul(bank[4 + d][:, h0], Wm[:, e, d, n, :], R[:, d, st % 2, h0], start=True, stop=True)
                        ins.then_inc(s.uu, 1)
                    for d in range(2):
                        n = chunk(d, st)
                        c0 = slice(n * P, (n + 1) * P)
                        pe.wait_ge(s.un, i * 8 + (2 * st + d + 1))
                        if st < NT - 1:
                            pe.matmul(bank[6 + d][:, 0:P], tk[:, d, 0, n, :], un[:, d, st % 2, :], start=True, stop=False)
                            pe.matmul(bank[6 + d][:, 0:P], tk[:, d, 1, n, :], vtok[:, n, :], start=False, stop=True).then_inc(s.su, 1)
                        if st:
                            pe.matmul(bank[d][:, c0], S[:, d, (st - 1) % 2, :], ft[:, d, R_, c0], start=True, stop=False)
                        for e in range(2):
                            h0 = slice(64 * e, 64 * e + 64)
                            pe.matmul(bank[d][h0, c0], un[:, d, st % 2, h0], GA[:, 1, e, d, n, :], start=(st == 0), stop=False)
                            ins = pe.matmul(bank[d][h0, c0], vtok[:, n, h0], GA[:, 2, e, d, n, :], start=False, stop=True)
                        ins.then_inc(s.yy, 1)
                pe.wait_ge(s.bon, i + 1)
                pe.matmul(bank[4][:, :], G.c("blk64"), ar[:, 0, :], start=True, stop=True).then_inc(s.bo, 1)
                pe.wait_ge(s.ys, i + 1)
                pe.matmul(bank[2][:, :], G.c("blk64"), ysb[:, :], start=True, stop=True).then_inc(s.mean, 1)
                pe.wait_ge(s.sq2, i + 1)
                pe.matmul(bank[3][:, :], G.c("blk64"), sq[:, :], start=True, stop=True).then_inc(s.var, 1)

        @block.scalar
        def _(act):
            c = Chain(act, s.achain)
            with act.Fori(0, 4) as i:
                act.wait_ge(s.pads, i + 1)
                for n in range(3):
                    act.wait_ge(s.proj, i * 3 + (n + 1))
                    act.activation(cb[:, n, 1:T + 1], bank[n][:, :], ACT.Copy).then_inc(s.cb, 1)
                act.wait_ge(s.kkp, i + 1)
                act.activation(sq[:], kkp[:], ACT.Square).then_inc(s.sq, 1)
                act.wait_ge(s.cs, i * 2 + 2)
                for d in range(2):
                    act.activation(Einv[:, d], Ein[:, d], ACT.Exp, scale=-1.0)
                    c.link(act.activation(Eex[:, d], Eex[:, d], ACT.Exp))
                    act.activation(Ein[:, d], Ein[:, d], ACT.Exp)
                act.activation(ms[:, 2:4], ms[:, 2:4], ACT.Exp).then_inc(s.ex, 1)
                act.wait_ge(s.ssq, i + 1)
                c.link(act.activation(rn[:], bank[7][:, :], ACT.Ln, bias=G.eps[:, 2:3]))
                act.activation(rn[:], rn[:], ACT.Exp, scale=-0.5).then_inc(s.rn, 1)
                for m in range(5):
                    act.wait_ge(s.feat, i * 5 + (m + 1))
                    dst = tk[:, m // 2, m % 2] if m < 4 else vtok[:]
                    act.activation(dst, four(bank[3 + m]), ACT.Copy).then_inc(s.tok, 1)
                for st in range(NT):
                    for d in range(2):
                        act.wait_ge(s.uu, i * 8 + (2 * st + d + 1))
                        act.activation(un[:, d, st % 2, :], bank[4 + d][:, 0:P], ACT.Copy, scale=-1.0).then_inc(s.un, 1)
                act.wait_ge(s.yy, i * 8 + 8)
                act.activation(ysb[:], bank[0][:, :], ACT.Copy).then_inc(s.yc, 1)
                act.wait_ge(s.cen, i + 1)
                act.activation(sq[:], ysb[:], ACT.Square).then_inc(s.sq2, 1)
                act.wait_ge(s.var, i + 1)
                c.link(act.activation(rn[:], bank[3][:, :], ACT.Ln, bias=G.eps[:, 1:2], scale=1.0 / HR))
                act.activation(rn[:], rn[:], ACT.Exp, scale=-0.5).then_inc(s.rv, 1)
                c.clear()

        @block.vector
        def _(dve):
            c = Chain(dve, s.chain)
            dve.sem_inc(s.fin, 1)
            dve.wait_ge(s.small, 32)
            mv = mu[:].rearrange("p t (j c) -> p (t j) c", c=3)
            c.link(dve.tensor_tensor(mv[:, :, 1:2], mv[:, :, 0:1], mv[:, :, 2:3], ALU.add))
            c.link(dve.tensor_scalar(mv[:, :, 1:2], mv[:, :, 1:2], -1.0, 1.0, ALU.mult, ALU.add))
            c.link(dve.tensor_scalar(par[:, :, 5:6], par[:, :, 1:2], -1.0, 1.0, ALU.mult, ALU.add))
            c.clear()
            with dve.Fori(0, 4) as i:
                dve.wait_ge(s.fin, i + 1)
                dve.tensor_scalar(muh[:].rearrange("p a b -> p (a b)").unsqueeze(1), mu[:, ds(i, 1), :], 1.0, None, ALU.mult)
                c.link(dve.tensor_scalar(parh[:].unsqueeze(1), par[:, ds(i, 1), :], 1.0, None, ALU.mult))
                dve.memset(cb[:, :, 0:1], 0.0)
                dve.memset(cb[:, :, T + 1:T + 2], 0.0).then_inc(s.pads, 1)
                for d in range(2):
                    dve.tensor_scalar(lwp[:, d], lw[:, d, :, ds(i * P, P)], -DECAY, None, ALU.mult).then_inc(s.lwp, 1)
                dve.wait_ge(s.pads, i + 1)
                for j in range(3):
                    dve.wait_ge(s.cb, i * 3 + (j + 1))
                    c.link(dve.tensor_scalar(rkv[:, j, :], cb[:, j, 0:T], muh[:, j, 0:1], None, ALU.mult))
                    for tap in (1, 2):
                        c.link(dve.scalar_tensor_tensor(rkv[:, j, :], cb[:, j, tap:tap + T], muh[:, j, tap:tap + 1], rkv[:, j, :],
                                                        ALU.mult, ALU.add))
                r, k, v = rkv[:, 0, :], rkv[:, 1, :], rkv[:, 2, :]
                dve.tensor_scalar(kkp[:], k, parh[:, 0:1], None, ALU.mult).then_inc(s.kkp, 1)
                for d in range(2):
                    dve.wait_ge(s.cum, i * 2 + (d + 1))
                    mid, end = (63, 127) if d == 0 else (64, 0)
                    cin = four(bank[3 + d])
                    dve.tensor_copy(ms[:, 0, d, :].unsqueeze(2), cin[:, :, mid:mid + 1])
                    dve.tensor_copy(ms[:, 2, d, :].unsqueeze(2), cin[:, :, mid:mid + 1])
                    c.link(dve.tensor_copy(ms[:, 1, d, :].unsqueeze(2), cin[:, :, end:end + 1]))
                    dve.tensor_tensor(Ein[:, d], cin, each4(ms[:, 0, d, :]), ALU.subtract)
                    dve.tensor_tensor(Eex[:, d], four(bank[5 + d]), each4(ms[:, 0, d, :]), ALU.subtract)
                    dve.tensor_tensor(ms[:, 3, d, :], ms[:, 1, d, :], ms[:, 0, d, :], ALU.subtract).then_inc(s.cs, 1)
                dve.wait_ge(s.ex, i + 1)
                dve.tensor_tensor(ms[:, 4, 0, 0:3], ms[:, 3, 0, 0:3], ms[:, 2, 0, 1:4], ALU.mult)
                dve.tensor_tensor(ms[:, 4, 1, 1:4], ms[:, 3, 1, 1:4], ms[:, 2, 1, 0:3], ALU.mult)
                dve.wait_ge(s.rn, i + 1)
                dve.wait_ge(s.kkp, i + 1)
                c.link(dve.tensor_tensor(kk, kkp[:], rn[:], ALU.mult))
                for d in range(2):
                    a = af[:, d, ds(i, 1), :]
                    dve.tensor_tensor(ft[:, d, B_, :].unsqueeze(1), kk.unsqueeze(1), a, ALU.mult)
                    c.link(dve.tensor_scalar(ar[:, d, :].unsqueeze(1), a, parh[:, 1:2], parh[:, 5:6], ALU.mult, ALU.add))
                    c.link(dve.tensor_tensor(kd[:, d, :], k, ar[:, d, :], ALU.mult))
                    dve.tensor_tensor(ft[:, d, A_, :], kk, flat(Eex[:, d]), ALU.mult)
                    dve.tensor_tensor(ft[:, d, R_, :], r, flat(Ein[:, d]), ALU.mult)
                    dve.tensor_tensor(ft[:, d, B_, :], ft[:, d, B_, :], flat(Einv[:, d]), ALU.mult)
                    dve.tensor_tensor(ft[:, d, K_, :], kd[:, d, :], flat(Einv[:, d]), ALU.mult).then_inc(s.ft, 1)
                c.link(dve.tensor_tensor(kd[:, 0, :], kd[:, 0, :], kd[:, 1, :], ALU.add))
                dve.scalar_tensor_tensor(ar[:, 0, :], kd[:, 0, :], parh[:, 2:3], r, ALU.mult, ALU.mult).then_inc(s.bon, 1)
                dve.wait_ge(s.bon, i + 1)
                dve.wait_ge(s.ft, i * 2 + 2)
                for m, (ty, e, d) in enumerate(grams):
                    dve.wait_ge(s.nt, i * 16 + (m + 1))
                    mask = strict[d] if ty < 2 else incl[d]
                    dst = NTm[:, e, d] if ty == 0 else GA[:, ty - 1, e, d]
                    dve.tensor_tensor(dst, four(bank[m % 8]), over4(mask), ALU.mult).then_inc(s.gram, 1)
                dve.wait_ge(s.gram, i * 16 + 16)
                for e in range(2):
                    invert_dve(dve, G, s, NTm[:, e], Tm, Wm[:, e], Xs,
                               ((bank[2], bank[3]), (bank[4], bank[5]), (bank[6], bank[7])), i * 28 + e * 14, i * 24 + e * 12)
                for st in range(NT):
                    for d in range(2):
                        dve.wait_ge(s.rhs, i * 8 + (2 * st + d + 1))
                        dve.tensor_copy(R[:, d, st % 2, :], bank[2 + d][:, 0:P]).then_inc(s.rr, 1)
                    if st < NT - 1:
                        for d in range(2):
                            n = chunk(d, st)
                            sc = ms[:, 4, d, n:n + 1]
                            dve.wait_ge(s.su, i * 6 + (2 * st + d + 1))
                            if st:
                                dve.wait_ge(s.st, i * 6 + (2 * (st - 1) + d + 1))
                                c.link(dve.tensor_tensor(St[:, d, :], S[:, d, (st - 1) % 2, :], bank[6 + d][:, 0:P], ALU.add))
                                ins = dve.scalar_tensor_tensor(S[:, d, st % 2, :], St[:, d, :], sc, G.c("blk64"), ALU.mult, ALU.mult)
                            else:
                                ins = dve.scalar_tensor_tensor(S[:, d, 0, :], bank[6 + d][:, 0:P], sc, G.c("blk64"), ALU.mult, ALU.mult)
                            ins.then_inc(s.st, 1)
                dve.wait_ge(s.yc, i + 1)
                dve.tensor_tensor(ysb[:], ysb[:], bank[1][:, :], ALU.add).then_inc(s.ys, 1)
                dve.wait_ge(s.mean, i + 1)
                dve.wait_ge(s.ys, i + 1)
                dve.scalar_tensor_tensor(ysb[:], bank[2][:, :], -1.0 / HR, ysb[:], ALU.mult, ALU.add).then_inc(s.cen, 1)
                dve.wait_ge(s.bo, i + 1)
                dve.tensor_tensor(ar[:, 1, :], bank[4][:, :], v, ALU.mult)
                dve.wait_ge(s.rv, i + 1)
                c.link(dve.tensor_tensor(ysb[:], ysb[:], rn[:], ALU.mult))
                c.link(dve.tensor_scalar(ysb[:], ysb[:], parh[:, 3:4], parh[:, 4:5], ALU.mult, ALU.add))
                c.link(dve.tensor_tensor(ysb[:], ysb[:], ar[:, 1, :], ALU.add))
                dve.tensor_tensor(G.oaT[:, ds(i, 1), :], ysb[:].unsqueeze(1), gg[:, ds(i, 1), :], ALU.mult).then_inc(s.fin, 1)
                c.clear()


OUT_SHAPE = (1, T, D)


def layout(x, give, tiles):
    for n in ("x", "rel_bias", "w_in", "w_branch_a", "w_branch_b", "w_out", "w_ff1", "w_ff2",
              "ln_mix_pre", "ln_mix_post", "ln_mlp_pre", "ln_mlp_post"):
        give(n, x[n])
    const, hot, band = constants()
    give("dt", np.concatenate([x["dt_bias_f"][0], x["dt_bias_b"][0]]))
    give("alog", np.concatenate([x["a_log_f"][0], x["a_log_b"][0]]))
    give("convw", np.asarray(x["conv_w"][0]).reshape(5, 3, GH, P).transpose(3, 2, 1, 0).reshape(P, GH, 15))
    give("norm_a", np.asarray(x["norm_a"][0]).reshape(P, 1))
    give("norm1_g", x["norm1_g_2"])
    for n in ("w_in", "w_up_f", "w_up_b", "a_up_f", "a_up_b", "g_up", "rpb", "w_o_rwkv", "w_o_na", "w_out",
              "w_gate_e", "w_up_e", "w_down_e", "w0_f", "w0_b", "norm2_g"):
        give(n + "_2" if n in ("w_in", "w_out") else n, x[n + "_2"])
    give("gains", np.stack([np.tile(x["q_gain_2"][0], 2), np.tile(x["k_gain_2"][0], 2)], 1))
    give("gate_bias", np.asarray(x["b_gate_2"][0]).reshape(2, KT, P).transpose(2, 1, 0))
    give("a0", np.stack([tiles(x["a0_f_2"][0], 4), tiles(x["a0_b_2"][0], 4)], 1))
    mp, mn = np.asarray(x["mu_prev_2"][0]), np.asarray(x["mu_next_2"][0])
    mu = np.stack([mp, np.zeros_like(mp), mn], 1)
    give("mu_rkv", mu[:R_LORA].reshape(3, 4, P, 3).transpose(2, 1, 0, 3).reshape(P, 4, 9))
    lora = np.zeros((P, 5, 3), mu.dtype)
    lora[:64, 0:4] = mu[R_LORA:R_LORA + 256].reshape(4, 64, 3).transpose(1, 0, 2)
    lora[:, 4] = mu[R_LORA + 256:]
    give("mu_lora", lora)
    room = np.zeros_like(x["k_k_2"][0])
    give("rw_par", np.stack([tiles(a, 4) for a in (x["k_k_2"][0], x["k_a_2"][0], np.asarray(x["r_k_2"][0]).reshape(-1),
                                                    x["lnx_g_2"][0], x["lnx_b_2"][0], room)], 2))
    give("w_router", np.concatenate([x["w_router_group_2"][0], x["w_router_expert_2"][0]], 1))
    give("b_router", np.concatenate([x["b_router_group_2"][0], x["b_router_expert_2"][0]]))
    give("const", const)
    give("hot", hot)
    give("band", band)


def build(nc, A, out):
    lines_dram = nc.dram_tensor("bias_lines", (4, LINES * (LINE + 1)), F32, kind="Internal").ap()
    pad_dram = nc.dram_tensor("rpb_padded", (120, 127), F32, kind="Internal").ap()
    rows_dram = nc.dram_tensor("token_rows", (T, D), F32, kind="Internal").ap()
    y_dram = nc.dram_tensor("expert_rows", (SLOTS * P, D), F32, kind="Internal").ap()
    with ExitStack() as ctx:
        G = Shared()
        G.const = ctx.enter_context(nc.sbuf_tensor("const", [P, NCONST], F32))
        G.X = ctx.enter_context(nc.sbuf_tensor("X", [P, NT, D], F32))
        G.hT = ctx.enter_context(nc.sbuf_tensor("hT", [P, KT, T], F32))
        G.oaT = ctx.enter_context(nc.sbuf_tensor("oaT", [P, KT, T], F32))
        G.obT = ctx.enter_context(nc.sbuf_tensor("obT", [P, NT, T], F32))
        G.c = lambda n, a=0, b=None: G.const[:, CC[n][0] + a:CC[n][0] + (CC[n][1] if b is None else b)]
        G.eps = ctx.enter_context(nc.sbuf_tensor("eps", [P, 4], F32))
        G.Y = ctx.enter_context(nc.sbuf_tensor("Y", [P, NT, D], F32))
        G.mT = G.Y[:].rearrange("p t (a c) -> p (t a) c", a=2)
        norm_phase(nc, G, "n1", A.ln_mix_pre, (A.x, A.const))
        attention_phase(nc, G, A.w_in[0], A.rel_bias, A.hot, A.band, lines_dram)
        gdn_phase(nc, G, A.w_in[0], A.dt, A.alog, A.convw, A.norm_a)
        merge_phase(nc, G, "m1", A.w_branch_a[0], A.w_branch_b[0], A.w_in[0], (C_GA, C_GB))
        out_phase(nc, G, "o1", A.w_out[0], False)
        norm_phase(nc, G, "n2", A.ln_mlp_pre, None, A.ln_mix_post)
        w1 = A.w_ff1[0].rearrange("(k p) c -> p k c", p=P)
        w2 = A.w_ff2[0].rearrange("(g f p) d -> g p f d", f=2, p=P)
        mlp_phase(nc, G, "ff", DF // DE, lambda g: w1[:, :, ds(g * DE, DE)], None, lambda g: group_of(w2, g))
        norm_phase(nc, G, "n3", A.norm1_g, None, A.ln_mlp_post)
        w_in2 = A.w_in_2[0]
        grid_attention_phase(nc, G, w_in2, A.rpb[0], A.gains, pad_dram)
        with nc.sbuf_tensor("af", [P, 2, 4, T], F32) as af:
            lw = G.Y[:].rearrange("p t d -> p (t d)").rearrange("p (d n c) -> p d n c", d=2, n=NT)
            gg = G.oaT[:, NT:2 * NT]
            rwkv_pre_phase(nc, G, w_in2, A, lw, af, gg)
            rwkv_phase(nc, G, w_in2, A, lw, af, gg)
        merge_phase(nc, G, "m2", A.w_o_rwkv[0], A.w_o_na[0], w_in2, (N_GA, N_GB), A.gate_bias)
        out_phase(nc, G, "o2", A.w_out_2[0], True)
        norm_phase(nc, G, "n4", A.norm2_g, rows_dram=rows_dram)
        rows = ctx.enter_context(nc.sbuf_tensor("rows", [P, SLOTS], U32))
        expert = ctx.enter_context(nc.sbuf_tensor("expert", [P, SLOTS], U32))
        place = ctx.enter_context(nc.sbuf_tensor("place", [P, NT, 2], U32))
        weight = ctx.enter_context(nc.sbuf_tensor("weight", [P, NT, 2], F32))
        router_phase(nc, G, A.w_router, A.b_router, rows, expert, place, weight)
        wge = A.w_gate_e[0].rearrange("e (p k) f -> e p k f", p=P)
        wue = A.w_up_e[0].rearrange("e (p k) f -> e p k f", p=P)
        wde = A.w_down_e[0].rearrange("e (f p) d -> e p f d", p=P)
        moe_phase(nc, G, wge, wue, wde, rows, expert, rows_dram, y_dram)
        final_phase(nc, G, place, weight, y_dram, out)


def group_of(view, g):
    return view[g] if isinstance(g, int) else view[ds(g, 1)].rearrange("a p k c -> p (a k) c")


def kernel(**inputs):
    import concourse.bacc as _bacc
    from concourse import mybir as _mybir
    from concourse.bass_utils import run_bass_kernel_spmd as _run

    nc = _bacc.Bacc("TRN2", target_bir_lowering=False, num_devices=1)
    arrays, args = {}, {}

    def give(name, a):
        a = np.ascontiguousarray(a)
        arrays[f"in_{name}"] = a
        args[name] = nc.dram_tensor(f"in_{name}", a.shape, _mybir.dt.from_np(a.dtype), kind="ExternalInput").ap()

    def tiles(v, n):
        return np.asarray(v).reshape(n, P).T

    layout(inputs, give, tiles)
    out = nc.dram_tensor("out_0", OUT_SHAPE, F32, kind="ExternalOutput").ap()
    build(nc, namedtuple("Inputs", list(args))(*args.values()), out)
    r = _run(nc, [arrays], core_ids=[0])
    return r.results[0]["out_0"]
```

```python
import math
from contextlib import ExitStack, contextmanager
from collections import namedtuple

import numpy as np
import concourse.bass as bass
from concourse import mybir

F32 = mybir.dt.float32
F32R = mybir.dt.float32r
ALU = mybir.AluOpType
ACT = mybir.ActivationFunctionType
AX = mybir.AxisListType.X
U32 = mybir.dt.uint32
ds = bass.ds

P = 128
T = 512
NT = T // P
D = 1024
KT = D // P
EPS = 1e-6
NEG = -1e30
CLIP = 0.0

GH, GD = 8, 128
C_QA, C_KA, C_VA, C_ZA, C_AB = 0, 1024, 2048, 3072, 4096
C_QB = 4128
DG, DHG = 3, 4
DW = DG * DHG * P
C_KB, C_VB = C_QB + DW, C_QB + 2 * DW
C_GA, C_GB = C_QB + 3 * DW, C_QB + 3 * DW + D
SIG = 4
DF = 4 * D
LINES, LINE = 9, 2 * P - 1

RW = 512
R_LORA = 3 * RW
N_Q, N_K, N_V = 1920, 2432, 2944
N_GA, N_GB = 3456, 4480
NAROW, NAR = 64, 8
NEXP, NGRP, DE = 32, 4, 256
GN_EPS = 64e-5
DECAY = math.exp(-0.5)

CC = {}
_at = 0
for _n, _w in (("ident", P), ("ones", P), ("blk64", P), ("le", P), ("ge", P), ("lt", P), ("gt", P),
               ("levf", 7 * P), ("levb", 7 * P), ("colmask", 64), ("idx", 32), ("iota", P), ("tok", 4)):
    CC[_n] = (_at, _w)
    _at += _w
NCONST = _at


def t5_bucket(rel):
    nb = 16
    ret = (rel > 0).astype(np.int32) * nb
    n = np.abs(rel)
    large = 8 + (np.log(np.maximum(n, 1) / 8) / math.log(1024 / 8) * 8).astype(np.int32)
    return ret + np.where(n < 8, n, np.minimum(large, nb - 1)).astype(np.int32)


def constants():
    c = np.zeros((P, NCONST), np.float32)
    r, q = np.arange(P)[:, None], np.arange(P)[None, :]

    def put(name, a):
        c[:, CC[name][0]:CC[name][0] + CC[name][1]] = a

    put("ident", r == q)
    put("ones", 1.0)
    put("blk64", (r // 64) == (q // 64))
    put("le", r <= q)
    put("ge", r >= q)
    put("lt", r < q)
    put("gt", r > q)
    for lev in range(7):
        b = 1 << lev
        m = (r // (2 * b) == q // (2 * b)) & ((r // b) % 2 == 1) & ((q // b) % 2 == 0)
        c[:, CC["levf"][0] + lev * P:CC["levf"][0] + (lev + 1) * P] = m
        c[:, CC["levb"][0] + lev * P:CC["levb"][0] + (lev + 1) * P] = m.T
    qc = 63 - (np.arange(P) % 64)
    st = np.clip(qc - 8, 0, 48)[:, None]
    kc = np.arange(64)[None, :]
    put("colmask", np.where((kc >= st) & (kc < st + 16), 0.0, NEG))
    put("iota", q)
    put("tok", r + P * np.arange(4)[None, :])
    put("idx", 64.0 - np.arange(32)[None, :])
    m = np.arange(LINE) - (P - 1)
    hot = np.zeros((32, LINES, LINE + 1), np.float32)
    band = np.full((LINES, LINE + 1), NEG, np.float32)
    for j in range(LINES):
        if j < 7:
            off = 4 * m + (j - 3)
            rel, ok = off, np.abs(off) <= 64
        elif j == 7:
            rel, ok = m * 4, np.abs(m) <= 64
        else:
            rel, ok = m * 4, m % 4 == 0
        bk = t5_bucket(rel)
        hot[bk, j, np.arange(LINE)] = 1.0
        band[j, :LINE] = np.where(ok, 0.0, NEG)
    return c, hot.reshape(32, -1), np.ascontiguousarray(np.broadcast_to(band.reshape(1, -1), (4, LINES * (LINE + 1))))


def bcast_rows(row, n, width, parts=P):
    return bass.AP(tensor=row.tensor, offset=row.offset, ap=[[0, parts], [1, width]])


class Shared:
    pass


class Chain:

    def __init__(self, eng, sem):
        self.eng, self.sem, self.n = eng, sem, 0

    def link(self, ins):
        self.n += 1
        ins.then_inc(self.sem, 1)
        self.eng.wait_ge(self.sem, self.n)

    def clear(self):
        if self.n:
            self.eng.sem_clear(self.sem)
            self.n = 0


class Phase:

    def __init__(self, nc, name, sems):
        self.nc, self.name, self.names = nc, name, sems

    def __enter__(self):
        self.ctx = ExitStack()
        self.ctx.__enter__()
        self.used = []
        self.s = namedtuple("Semaphores", self.names)(*[self.sem(n) for n in self.names.split()])
        return self

    def sem(self, name):
        self.used.append(self.nc.alloc_semaphore(name=f"{self.name}_{name}"))
        return self.used[-1]

    def sems(self, name, n):
        return [self.sem(f"{name}{i}") for i in range(n)]

    def sb(self, name, shape, dt=F32):
        return self.ctx.enter_context(self.nc.sbuf_tensor(f"{self.name}_{name}", shape, dt))

    def banks(self, n=8):
        return [self.ctx.enter_context(self.nc.psum_tensor(f"{self.name}_bank{i}", [P, 512], F32)) for i in range(n)]

    def block(self):
        return self.ctx.enter_context(self.nc.Block())

    def __exit__(self, *failed):
        if failed[0] is not None:
            return False
        self.ctx.__exit__(None, None, None)
        self.nc.clear_and_free_semaphores(self.used)
        self.nc.all_engine_barrier()
        return False


def norm_phase(nc, G, name, ln_row, first=None, add_row=None, rows_dram=None):
    with Phase(nc, name, "x_in ln_in const_in mean root h_ready turned rows_out chain") as ph:
        s = ph.s
        lnw = ph.sb("lnw", [P, 2, D])
        h = ph.sb("h", [P, NT, D])
        ss = ph.sb("ss", [P, 4 * NT])
        bank = ph.banks()
        block = ph.block()
        rows = [r for r in (add_row, ln_row) if r is not None]

        @block.sync
        def _(sp):
            if first is not None:
                sp.dma_start(G.X[:], first[0][0].rearrange("(t p) d -> p t d", p=P)).then_inc(s.x_in, 16)
                sp.dma_start(G.const[:], first[1]).then_inc(s.const_in, 16)
            for j, row in enumerate(rows):
                sp.dma_start(lnw[:, j], bcast_rows(row, 1, D)).then_inc(s.ln_in, 16)
            if rows_dram is not None:
                for t in range(NT):
                    sp.wait_ge(s.h_ready, t + 1)
                    sp.dma_start(rows_dram[t * P:(t + 1) * P, :], h[:, t, :]).then_inc(s.rows_out, 16)
                sp.wait_ge(s.rows_out, 16 * NT)

        @block.vector
        def _(dve):
            c = Chain(dve, s.chain)
            if first is not None:
                for j, value in enumerate((EPS, GN_EPS, 1e-12, 1.0)):
                    dve.memset(G.eps[:, j:j + 1], value)
                dve.wait_ge(s.x_in, 16)

            def rms(src, turn):
                for t in range(NT):
                    ins = dve.tensor_tensor_reduce(h[:, t, :], src[:, t, :], src[:, t, :], 1.0, 0.0, ALU.mult, ALU.add,
                                                   ss[:, t:t + 1])
                c.link(ins)
                dve.tensor_scalar(ss[:, NT:2 * NT], ss[:, 0:NT], 1.0 / D, EPS, ALU.mult, ALU.add).then_inc(s.mean, 1)
                dve.wait_ge(s.root, turn)
                c.link(dve.reciprocal(ss[:, 3 * NT:4 * NT], ss[:, 2 * NT:3 * NT]))

            if add_row is not None:
                rms(G.Y, 1)
                dve.wait_ge(s.ln_in, 16 * len(rows))
                for t in range(NT):
                    ins = dve.scalar_tensor_tensor(G.Y[:, t, :], G.Y[:, t, :], ss[:, 3 * NT + t:3 * NT + t + 1], lnw[:, 0],
                                                   ALU.mult, ALU.mult)
                c.link(ins)
                for t in range(NT):
                    ins = dve.tensor_tensor(G.X[:, t, :], G.X[:, t, :], G.Y[:, t, :], ALU.add)
                c.link(ins)
            rms(G.X, len(rows))
            dve.wait_ge(s.ln_in, 16 * len(rows))
            for t in range(NT):
                dve.scalar_tensor_tensor(h[:, t, :], G.X[:, t, :], ss[:, 3 * NT + t:3 * NT + t + 1], lnw[:, len(rows) - 1],
                                         ALU.mult, ALU.mult).then_inc(s.h_ready, 1)

        @block.scalar
        def _(act):
            for n in range(len(rows)):
                act.wait_ge(s.mean, n + 1)
                act.activation(ss[:, 2 * NT:3 * NT], ss[:, NT:2 * NT], ACT.Sqrt).then_inc(s.root, 1)
            for k in range(KT):
                act.wait_ge(s.turned, k + 1)
                act.activation(G.hT[:, k, :], bank[k][:, :], ACT.Copy)

        @block.tensor
        def _(pe):
            if first is not None:
                pe.wait_ge(s.const_in, 16)
            for k in range(KT):
                for t in range(NT):
                    if k == 0:
                        pe.wait_ge(s.h_ready, t + 1)
                    ins = pe.transpose(bank[k][:, t * P:(t + 1) * P], h[:, t, k * P:(k + 1) * P], G.c("ident"))
                ins.then_inc(s.turned, 1)


def attention_phase(nc, G, w_in, rel_bias, hot, band, lines_dram):
    W9 = 9
    with Phase(nc, "att", "small line_mm lines_ready lines_out toep proj logits logits_taken "
               "negmax expd p_ready turned pt_ready out out_taken copied chain") as ph:
        s = ph.s
        w_ready = ph.sems("w_ready", W9)
        wr = ph.sb("wr", [P, W9, KT, P])
        rb = ph.sb("rb", [32, 12])
        hots = ph.sb("hots", [32, LINES * (LINE + 1)])
        bands = ph.sb("bands", [4, LINES * (LINE + 1)])
        lines = ph.sb("lines", [4, LINES * (LINE + 1)])
        bias = ph.sb("bias", [P, DHG, LINES, P])
        qT = ph.sb("qT", [P, DG, SIG, P])
        kT = ph.sb("kT", [P, DG, SIG, P])
        v = ph.sb("v", [P, SIG, DG, P])
        L = ph.sb("L", [P, SIG, 6 * P])
        PT = ph.sb("PT", [P, 2, 6 * P])
        st = ph.sb("st", [P, SIG, 4])
        bank = ph.banks()
        block = ph.block()
        LW = LINE + 1
        obT = G.obT[:].rearrange("p h (l s) -> p h l s", s=SIG)
        hview = G.hT[:].rearrange("p k (l s) -> p k s l", s=SIG)
        cols = [(C_QB, C_KB, C_VB)[n % 3] + (n // 3) * DHG * P for n in range(W9)]
        wv = w_in.rearrange("(k p) c -> p k c", p=P)

        @block.sync
        def _(sp):
            sp.dma_start(rb[:], rel_bias).then_inc(s.small, 16)
            sp.dma_start(hots[:], hot).then_inc(s.small, 16)
            sp.dma_start(bands[:], band).then_inc(s.small, 16)
            for n in range(W9):
                sp.dma_start(wr[:, n], wv[:, :, cols[n]:cols[n] + P]).then_inc(w_ready[n], 16)
            sp.wait_ge(s.lines_ready, 3)
            sp.dma_start(lines_dram, lines[:]).then_inc(s.lines_out, 16)
            sp.wait_ge(s.lines_out, 16)
            for h in range(DHG):
                src = bass.AP(tensor=lines_dram.tensor, offset=lines_dram.offset + h * LINES * LW,
                              ap=[[1, P], [LW, LINES], [1, P]])
                sp.dma_start(bias[:, h], src).then_inc(s.toep, 16)
            with sp.Fori(1, DHG) as i:
                for n in range(W9):
                    col = sp.snap(i * P + cols[n])
                    used = sp.snap(i * W9 + (n + 1 - W9))
                    sp.wait_ge(s.proj, used)
                    sp.dma_start(wr[:, n], wv[:, :, ds(col, P)]).then_inc(w_ready[n], 16)

        @block.tensor
        def _(pe):
            pe.wait_ge(s.small, 48)
            for b in range(4):
                ins = pe.matmul(bank[b][0:4, 0:2 * LW if b < 3 else LW], rb[:, 0:4],
                                hots[:, b * 2 * LW:min((b * 2 + 2) * LW, 7 * LW)], start=True, stop=True)
            pe.matmul(bank[4][0:4, 0:LW], rb[:, 4:8], hots[:, 7 * LW:8 * LW], start=True, stop=True)
            pe.matmul(bank[5][0:4, 0:LW], rb[:, 8:12], hots[:, 8 * LW:9 * LW], start=True, stop=True).then_inc(s.line_mm, 1)
            pe.wait_ge(s.lines_ready, 3)

            def logits(i, rho):
                pe.wait_ge(s.logits_taken, i * SIG + (rho + 1))
                b0 = 3 - 3 * (rho % 2)
                pe.matmul(bank[b0][:, :], qT[:, 0, rho, :], kT[:, 0, :, :], start=True, stop=True)
                pe.matmul(bank[b0 + 1][:, 0:P], qT[:, 1, rho, :], kT[:, 1, rho, :], start=True, stop=True)
                pe.matmul(bank[b0 + 1][:, P:2 * P], qT[:, 2, rho, :], kT[:, 2, rho, :], start=True, stop=True).then_inc(s.logits, 1)

            def turn(i, rho):
                pe.wait_ge(s.p_ready, i * SIG + (rho + 1))
                pe.wait_ge(s.pt_ready, i * SIG + (rho + 1))
                for j in range(6):
                    ins = pe.transpose(bank[5 + j // 4][:, (j % 4) * P:(j % 4 + 1) * P], L[:, rho, j * P:(j + 1) * P], G.c("ident"))
                ins.then_inc(s.turned, 1)

            def values(i, rho):
                pe.wait_ge(s.pt_ready, i * SIG + (rho + 2))
                pe.wait_ge(s.out_taken, i * SIG + (rho + 1))
                for j in range(6):
                    sig, g = (j, 0) if j < 4 else (rho, j - 3)
                    ins = pe.matmul(bank[7][:, 0:P], v[:, sig, g, :], PT[:, rho % 2, j * P:(j + 1) * P], start=(j == 0), stop=(j == 5))
                ins.then_inc(s.out, 1)

            with pe.Fori(0, DHG) as i:
                for n in range(W9):
                    g, which = n // 3, n % 3
                    pe.wait_ge(w_ready[n], i * 16 + 16)
                    pe.wait_ge(s.copied, i * W9 + (n + 1))
                    if which < 2:
                        for k in range(KT):
                            ins = pe.matmul(bank[which][:, :], wr[:, n, k, :], G.hT[:, k, :], start=(k == 0), stop=(k == KT - 1))
                    else:
                        for sig in range(SIG):
                            for k in range(KT):
                                ins = pe.matmul(bank[2][:, sig * P:(sig + 1) * P], hview[:, k, sig, :], wr[:, n, k, :],
                                                start=(k == 0), stop=(k == KT - 1))
                    ins.then_inc(s.proj, 1)
                pe.wait_ge(s.copied, i * W9 + (W9 + 3))
                logits(i, 0)
                logits(i, 1)
                for rho in range(SIG):
                    turn(i, rho)
                    if rho + 2 < SIG:
                        logits(i, rho + 2)
                    values(i, rho)

        @block.scalar
        def _(act):
            act.sem_inc(s.copied, 3)
            act.sem_inc(s.pt_ready, 1)
            with act.Fori(0, DHG) as i:
                act.wait_ge(s.out_taken, i * SIG + 1)
                for n in range(W9):
                    g, which = n // 3, n % 3
                    act.wait_ge(s.proj, i * W9 + (n + 1))
                    if which < 2:
                        src = bank[which][:, :].rearrange("p (l s) -> p s l", s=SIG)
                        if which == 0:
                            src = src[:, :, ::-1]
                        ins = act.activation((qT, kT)[which][:, g], src, ACT.Copy, scale=P ** -0.5 if which == 0 else 1.0)
                    else:
                        ins = act.activation(v[:, :, g, :], bank[2][:, :].rearrange("p (s c) -> p s c", s=SIG), ACT.Copy)
                    ins.then_inc(s.copied, 1)

                def exps(rho):
                    act.wait_ge(s.negmax, i * SIG + (rho + 1))
                    act.activation(L[:, rho, :], L[:, rho, :], ACT.Exp, bias=st[:, rho, 1:2],
                                   accum_out=st[:, rho, 2:3]).then_inc(s.expd, 1)

                def turn(rho):
                    act.wait_ge(s.turned, i * SIG + (rho + 1))
                    act.activation(PT[:, rho % 2, 0:512], bank[5][:, :], ACT.Copy)
                    act.activation(PT[:, rho % 2, 512:768], bank[6][:, 0:256], ACT.Copy).then_inc(s.pt_ready, 1)

                for rho in range(SIG):
                    exps(rho)
                    if rho:
                        turn(rho - 1)
                turn(SIG - 1)

        @block.vector
        def _(dve):
            c = Chain(dve, s.chain)
            dve.sem_inc(s.logits_taken, 2)
            dve.sem_inc(s.out_taken, 1)
            dve.wait_ge(s.line_mm, 1)
            dve.wait_ge(s.small, 48)
            for b in range(6):
                j0 = b * 2 if b < 4 else b + 3
                n = 2 if b < 3 else 1
                ins = dve.tensor_tensor(lines[:, j0 * LW:(j0 + n) * LW], bank[b][0:4, 0:n * LW], bands[:, j0 * LW:(j0 + n) * LW], ALU.add)
                if b in (1, 3, 5):
                    ins.then_inc(s.lines_ready, 1)
            def take_out(i, rho):
                dve.wait_ge(s.out, i * SIG + (rho + 1))
                src = bank[7][:, P - 1::-1][:, 0:P].rearrange("p (a l) -> p a l", a=1)
                dve.tensor_scalar(obT[:, ds(i, 1), :, rho], src, 1.0, None, ALU.mult).then_inc(s.out_taken, 1)

            dve.wait_ge(s.toep, 16 * DHG)
            with dve.Fori(0, DHG) as i:

                def biased(rho):
                    r, b0 = rho, 3 - 3 * (rho % 2)
                    dve.wait_ge(s.logits, i * SIG + (rho + 1))
                    lo = L[:, r, :].rearrange("p (a j c) -> p a j c", a=1, c=P)
                    dve.tensor_tensor(lo[:, :, 0:4], bank[b0][:, :].rearrange("p (a j c) -> p a j c", a=1, c=P), bias[:, ds(i, 1), 3 - rho:7 - rho, :], ALU.add)
                    dve.tensor_tensor(lo[:, :, 4:6], bank[b0 + 1][:, 0:2 * P].rearrange("p (a j c) -> p a j c", a=1, c=P),
                                      bias[:, ds(i, 1), 7:9, :], ALU.add).then_inc(s.logits_taken, 1)
                    dve.wait_ge(s.logits_taken, i * SIG + (rho + 3))
                    c.link(dve.tensor_reduce(st[:, r, 0:1], L[:, r, :], AX, ALU.max))
                    dve.tensor_scalar(st[:, r, 1:2], st[:, r, 0:1], -1.0, None, ALU.mult).then_inc(s.negmax, 1)

                biased(0)
                for rho in range(SIG):
                    r = rho
                    if rho + 1 < SIG:
                        biased(rho + 1)
                    dve.wait_ge(s.expd, i * SIG + (rho + 1))
                    c.link(dve.reciprocal(st[:, r, 3:4], st[:, r, 2:3]))
                    dve.tensor_scalar(L[:, r, :], L[:, r, :], st[:, r, 3:4], None, ALU.mult).then_inc(s.p_ready, 1)
                    if rho:
                        take_out(i, rho - 1)
                take_out(i, SIG - 1)
                c.clear()


LEV = 7
InvertSems = namedtuple("InvertSems", "tw xs x yz nt")


def over4(a):
    return a.unsqueeze(1).to_broadcast([P, 4, P])


def each4(col):
    return col.unsqueeze(2).to_broadcast([P, 4, P])


def four(bank):
    return bank[:, :].rearrange("p (n c) -> p n c", n=4)


def invert_pe(pe, G, s, NTm, Tm, Wm, Xs, banks, i2, i14, meanwhile=None):
    bX, bY, bZ = banks
    for lev in range(LEV):
        for d in range(2):
            if lev:
                pe.wait_ge(s.tw, i14 + (2 * (lev - 1) + d + 1))
            else:
                pe.wait_ge(s.nt, i2 + (d + 1))
            for n in range(4):
                rhs = Tm[:, d, n, :] if lev else G.c("ident")
                ins = pe.matmul(bX[d][:, n * P:(n + 1) * P], NTm[:, d, n, :], rhs, start=True, stop=True)
            ins.then_inc(s.x, 1)
        if lev == 0:
            if meanwhile:
                meanwhile(0)
            continue
        for d in range(2):
            pe.wait_ge(s.xs, i14 + (2 * lev + d + 1))
            for n in range(4):
                if lev < LEV - 1:
                    pe.matmul(bY[d][:, n * P:(n + 1) * P], Wm[:, d, n, :], Xs[:, d, n, :], start=True, stop=True)
            for n in range(4):
                ins = pe.matmul(bZ[d][:, n * P:(n + 1) * P], Xs[:, d, n, :], Wm[:, d, n, :], start=True, stop=True)
            ins.then_inc(s.yz, 1)
        if meanwhile:
            meanwhile(lev)


def invert_dve(dve, G, s, NTm, Tm, Wm, Xs, banks, i14, i12):
    bX, bY, bZ = banks
    for lev in range(LEV):
        for d in range(2):
            mask = G.c("levb" if d else "levf", lev * P, (lev + 1) * P)
            maskT = G.c("levf" if d else "levb", lev * P, (lev + 1) * P)
            dve.wait_ge(s.x, i14 + (2 * lev + d + 1))
            if lev:
                dve.tensor_tensor(Xs[:, d], four(bX[d]), over4(mask), ALU.mult).then_inc(s.xs, 1)
            else:
                dve.tensor_tensor(Xs[:, d], four(bX[d]), over4(mask), ALU.mult)
                dve.tensor_tensor(Wm[:, d], NTm[:, d], over4(maskT), ALU.mult).then_inc(s.xs, 1)
                dve.wait_ge(s.xs, i14 + (d + 1))
                dve.tensor_tensor(Tm[:, d], over4(G.c("ident")), Xs[:, d], ALU.subtract)
                dve.tensor_tensor(Wm[:, d], over4(G.c("ident")), Wm[:, d], ALU.subtract).then_inc(s.tw, 1)
        if lev == 0:
            continue
        for d in range(2):
            dve.wait_ge(s.yz, i12 + (2 * (lev - 1) + d + 1))
            if lev < LEV - 1:
                dve.tensor_tensor(Tm[:, d], Tm[:, d], four(bY[d]), ALU.subtract)
            dve.tensor_tensor(Wm[:, d], Wm[:, d], four(bZ[d]), ALU.subtract).then_inc(s.tw, 1)


K_G, K_GC, K_B, K_NEG, K_EGL, K_ESUM = range(6)
NK = 6


def gdn_phase(nc, G, w_in, dt_row, alog_row, convw, norm_col):
    with Phase(nc, "gdn", "small ab abs_ sc1 sc2 sc3 gd cum cums sm_ready proj cb conv silu sq ssq rn qk kvt tok "
               "coef zs vsilu smh gB rb kk egB dmin dexp bst qe kdec nt x xs yz tw ks r u vn o su st oc osum osq oss orn fin "
               "chain achain pchain") as ph:
        s = ph.s
        w_ready = ph.sems("w_ready", 4)
        wr = ph.sb("wr", [P, 4, KT, P])
        wab = ph.sb("wab", [P, KT, 32])
        dtb = ph.sb("dtb", [P, 16])
        alog = ph.sb("alog", [P, 16])
        cw = ph.sb("cw", [P, GH, 15])
        cwh = ph.sb("cwh", [P, 15])
        na = ph.sb("na", [P, 1])
        ab = ph.sb("ab", [P, NT, 32])
        tmp = ph.sb("tmp", [P, 6, NT, 16])
        gd = ph.sb("gd", [P, 16, NT])
        sm = ph.sb("sm", [P, GH, NK, 2, NT])
        smh = ph.sb("smh", [P, NK, 2, NT])
        smg = ph.sb("smg", [P, 2, 2, NT])
        cb = ph.sb("cb", [P, 3, T + 4])
        cv = ph.sb("cv", [P, 3, T])
        wt = ph.sb("wt", [P, 2, T])
        zs = ph.sb("zs", [P, T])
        zn = ph.sb("zn", [P, T])
        osqb = ph.sb("osqb", [P, T])
        ornb = ph.sb("ornb", [P, T])
        sq = ph.sb("sq", [P, 2, T])
        rn = ph.sb("rn", [P, 2, T])
        qT = ph.sb("qT", [P, T])
        kT = ph.sb("kT", [P, T])
        ktok = ph.sb("ktok", [P, NT, P])
        vtok = ph.sb("vtok", [P, NT, P])
        kdec = ph.sb("kdec", [P, 2, NT, P])
        gB = ph.sb("gB", [P, 2, NT, P])
        egB = ph.sb("egB", [P, 2, T])
        qe = ph.sb("qe", [P, 2, T])
        Dx = ph.sb("Dx", [P, 2, NT, P])
        bst = ph.sb("bst", [P, 2, NT, P])
        AqT = ph.sb("AqT", [P, 2, NT, P])
        NTm = ph.sb("NTm", [P, 2, NT, P])
        Tm = ph.sb("Tm", [P, 2, NT, P])
        Wm = ph.sb("Wm", [P, 2, NT, P])
        Xs = ph.sb("Xs", [P, 2, NT, P])
        S = ph.sb("S", [P, 2, 2, P])
        R = ph.sb("R", [P, 2, 2, P])
        vn = ph.sb("vn", [P, 2, 2, P])
        osb = ph.sb("osb", [P, T])
        bank = ph.banks()
        block = ph.block()
        inv = (NTm, Tm, Wm, Xs, ((bank[2], bank[3]), (bank[4], bank[5]), (bank[6], bank[7])))
        cols = (C_QA, C_KA, C_VA, C_ZA)
        wv = w_in.rearrange("(k p) c -> p k c", p=P)
        incl, strict = (G.c("le"), G.c("ge")), (G.c("lt"), G.c("gt"))

        def chunk(d, st):
            return st if d == 0 else NT - 1 - st

        @block.sync
        def _(sp):
            sp.dma_start(wab[:], wv[:, :, C_AB:C_AB + 32]).then_inc(s.small, 16)
            sp.dma_start(dtb[:], bcast_rows(dt_row, 1, 16)).then_inc(s.small, 16)
            sp.dma_start(alog[:], bcast_rows(alog_row, 1, 16)).then_inc(s.small, 16)
            sp.dma_start(cw[:], convw).then_inc(s.small, 16)
            sp.dma_start(na[:], norm_col).then_inc(s.small, 16)
            for n in range(4):
                sp.dma_start(wr[:, n], wv[:, :, cols[n]:cols[n] + P]).then_inc(w_ready[n], 16)
            with sp.Fori(1, GH) as i:
                for n in range(4):
                    col = sp.snap(i * P + cols[n])
                    used = sp.snap(i * 4 + (n + 1 - 4))
                    sp.wait_ge(s.proj, used)
                    sp.dma_start(wr[:, n], wv[:, :, ds(col, P)]).then_inc(w_ready[n], 16)

        @block.gpsimd
        def _(pool):
            c = Chain(pool, s.pchain)
            pool.wait_ge(s.small, 80)

            def front(i):
                pool.wait_ge(s.coef, i + 1)
                for d in range(2):
                    pool.tensor_tensor(gB[:, d], over4(G.c("ones")), each4(smg[:, K_G, d, :]), ALU.mult).then_inc(s.gB, 1)
                for j in range(3):
                    pool.wait_ge(s.cb, i * 4 + (j + 3))
                    def weighed(dst, tap):
                        return pool.tensor_tensor(dst, cb[:, j, tap:tap + T], cwh[:, 5 * j + tap:5 * j + tap + 1].to_broadcast([P, T]), ALU.mult)

                    weighed(cv[:, j, :], 0)
                    for tap in range(1, 5):
                        c.link(weighed(wt[:, tap % 2, :], tap))
                        ins = pool.tensor_tensor(cv[:, j, :], cv[:, j, :], wt[:, tap % 2, :], ALU.add)
                        if tap < 4:
                            c.link(ins)
                    ins.then_inc(s.conv, 1)
                c.clear()

            def head(i, more):
                pool.wait_ge(s.smh, i + 1)
                for d in range(2):
                    pool.tensor_tensor(bst[:, d], over4(strict[d]), each4(smh[:, K_B, d, :]), ALU.mult).then_inc(s.bst, 1)
                pool.wait_ge(s.tok, i * 2 + 1)
                for d in range(2):
                    pool.tensor_tensor(kdec[:, d], ktok[:], each4(smh[:, K_EGL, d, :]), ALU.mult).then_inc(s.kdec, 1)
                for d in range(2):
                    pool.wait_ge(s.egB, i * 2 + (d + 1))
                    pool.tensor_tensor(qe[:, d], qT[:], egB[:, d], ALU.mult).then_inc(s.qe, 1)
                if more:
                    pool.wait_ge(s.tok, i * 2 + 2)
                    front(i + 1)

            front(0)
            with pool.Fori(0, GH - 1) as i:
                head(i, True)
            head(GH - 1, False)

        @block.tensor
        def _(pe):
            pe.wait_ge(s.small, 80)
            for t in range(NT):
                for k in range(KT):
                    ins = pe.matmul(bank[0][:, t * 32:(t + 1) * 32], G.hT[:, k, t * P:(t + 1) * P], wab[:, k, :],
                                    start=(k == 0), stop=(k == KT - 1))
            ins.then_inc(s.ab, 1)
            pe.wait_ge(s.gd, 1)
            pe.matmul(bank[1][:, 0:32], incl[0], gd[:, 0:8, :], start=True, stop=True)
            pe.matmul(bank[1][:, 32:64], incl[1], gd[:, 8:16, :], start=True, stop=True)
            pe.matmul(bank[1][:, 64:128], G.c("ones"), gd[:, :, :], start=True, stop=True).then_inc(s.cum, 1)
            pe.wait_ge(s.sm_ready, 1)

            def project(i, n, k0=0, k1=KT):
                if k0 == 0:
                    pe.wait_ge(w_ready[n], i * 16 + 16)
                    pe.wait_ge(s.cb, i * 4 + (n + 1))
                for k in range(k0, k1):
                    ins = pe.matmul(bank[n % 2][:, :], wr[:, n, k, :], G.hT[:, k, :], start=(k == 0), stop=(k == KT - 1))
                if k1 == KT:
                    ins.then_inc(s.proj, 1)

            def squares(i):
                pe.wait_ge(s.cb, i * 4 + 6)
                for j in range(2):
                    pe.wait_ge(s.sq, i * 2 + (j + 1))
                    pe.matmul(bank[j][:, :], G.c("ones"), sq[:, j, :], start=True, stop=True).then_inc(s.ssq, 1)

            def ahead(i, lev):
                if lev < 4:
                    project(i, 1 + lev // 2, 4 * (lev % 2), 4 * (lev % 2) + 4)
                elif lev == 4:
                    project(i, 3)
                elif lev == 5:
                    squares(i)

            def front(i):
                for d in range(2):
                    pe.wait_ge(s.gB, i * 2 + (d + 1))
                    for n in range(4):
                        ins = pe.matmul(bank[4 + d][:, n * P:(n + 1) * P], gB[:, d, n, :], incl[d], start=True, stop=True)
                    ins.then_inc(s.rb, 1)

            def norm(i):
                pe.wait_ge(s.osq, i + 1)
                pe.matmul(bank[1][:, :], G.c("ones"), osqb[:, :], start=True, stop=True).then_inc(s.oss, 1)

            def head(i, more, first=False):
                front(i)
                pe.wait_ge(s.qk, i * 2 + 2)
                for n in range(4):
                    ins = pe.transpose(bank[2][:, n * P:(n + 1) * P], kT[:, n * P:(n + 1) * P], G.c("ident"))
                ins.then_inc(s.kvt, 1)
                pe.wait_ge(s.vsilu, i + 1)
                for n in range(4):
                    ins = pe.transpose(bank[3][:, n * P:(n + 1) * P], cv[:, 2, n * P:(n + 1) * P], G.c("ident"))
                ins.then_inc(s.kvt, 1)
                for n in range(4):
                    c0 = slice(n * P, (n + 1) * P)
                    pe.matmul(bank[6][:, c0], kT[:, c0], kT[:, c0], start=True, stop=True)
                for n in range(4):
                    c0 = slice(n * P, (n + 1) * P)
                    ins = pe.matmul(bank[7][:, c0], kT[:, c0], qT[:, c0], start=True, stop=True)
                ins.then_inc(s.kk, 1)
                if not first:
                    norm(i - 1)
                if more:
                    pe.wait_ge(s.osum, i + 1)
                    project(i + 1, 0)
                    pe.wait_ge(s.orn, i + 1)
                pe.wait_ge(s.tok, i * 2 + 2)
                pe.wait_ge(s.egB, i * 2 + 2)
                invert_pe(pe, G, s, *inv, i * 2, i * 14, lambda lev: ahead(i + 1, lev) if more else None)
                for st in range(NT):
                    for d in range(2):
                        n = chunk(d, st)
                        if st:
                            pe.wait_ge(s.st, i * 6 + (2 * (st - 1) + d + 1))
                            pe.matmul(bank[2 + d][:, 0:P], kT[:, n * P:(n + 1) * P], S[:, d, (st - 1) % 2, :],
                                      start=True, stop=True).then_inc(s.ks, 1)
                    for d in range(2):
                        n = chunk(d, st)
                        if st:
                            pe.wait_ge(s.r, i * 6 + (2 * (st - 1) + d + 1))
                        else:
                            pe.wait_ge(s.tw, i * 14 + (12 + d + 1))
                        pe.matmul(bank[4 + d][:, 0:P], Wm[:, d, n, :], R[:, d, st % 2, :] if st else vtok[:, n, :],
                                  start=True, stop=True).then_inc(s.u, 1)
                    if st == 0 and more:
                        pe.wait_ge(s.rn, i * 2 + 4)
                    elif st == 0:
                        pe.wait_ge(s.orn, i + 1)
                    for d in range(2):
                        n = chunk(d, st)
                        pe.wait_ge(s.vn, i * 8 + (2 * st + d + 1))
                        pe.wait_ge(s.kdec, i * 2 + (d + 1))
                        if st < NT - 1:
                            pe.matmul(bank[6 + d][:, 0:P], kdec[:, d, n, :], vn[:, d, st % 2, :], start=True, stop=True).then_inc(s.su, 1)
                        pe.wait_ge(s.qe, i * 2 + (d + 1))
                        if st:
                            pe.matmul(bank[d][:, n * P:(n + 1) * P], S[:, d, (st - 1) % 2, :], qe[:, d, n * P:(n + 1) * P],
                                      start=True, stop=False)
                        pe.matmul(bank[d][:, n * P:(n + 1) * P], vn[:, d, st % 2, :], AqT[:, d, n, :],
                                  start=(st == 0), stop=True).then_inc(s.o, 1)

            for n in range(4):
                project(0, n)
            squares(0)
            pe.wait_ge(s.rn, 2)
            head(0, True, True)
            with pe.Fori(1, GH - 1) as i:
                head(i, True)
            head(GH - 1, False)
            norm(GH - 1)

        @block.scalar
        def _(act):
            c = Chain(act, s.achain)
            act.sem_inc(s.cb, 2)
            act.wait_ge(s.abs_, 1)
            act.activation(tmp[:, 3], tmp[:, 2], ACT.Exp).then_inc(s.sc1, 1)
            c.link(act.activation(tmp[:, 5], ab[:, :, 16:32], ACT.Exp, scale=-1.0))
            act.activation(alog[:], alog[:], ACT.Exp).then_inc(s.sc2, 1)
            act.activation(tmp[:, 4], tmp[:, 3], ACT.Ln, bias=G.eps[:, 3:4]).then_inc(s.sc3, 1)
            act.wait_ge(s.cums, 2)
            smv = [sm[:, :, k, :, :].rearrange("p h d n -> p d h n") for k in range(NK)]
            gcv = smv[K_GC]
            act.activation(smv[K_NEG], gcv, ACT.Exp)
            act.activation(smv[K_EGL], smv[K_EGL], ACT.Exp)
            act.activation(smv[K_ESUM], smv[K_ESUM], ACT.Exp).then_inc(s.sc3, 1)
            c.clear()
            act.sem_inc(s.orn, 1)

            def front(i):
                for n in range(3):
                    act.wait_ge(s.proj, i * 4 + (n + 1))
                    act.activation(cb[:, n, 2:T + 2], bank[n % 2][:, :], ACT.Copy).then_inc(s.cb, 1)
                for j in range(2):
                    act.wait_ge(s.conv, i * 3 + (j + 1))
                    c.link(act.activation(cv[:, j, :], cv[:, j, :], ACT.Silu))
                for j in range(2):
                    act.activation(sq[:, j, :], cv[:, j, :], ACT.Square).then_inc(s.sq, 1)
                act.wait_ge(s.proj, i * 4 + 4)
                act.activation(zn[:], bank[1][:, :], ACT.Silu).then_inc(s.cb, 1)
                act.wait_ge(s.conv, i * 3 + 3)
                act.activation(cv[:, 2, :], cv[:, 2, :], ACT.Silu).then_inc(s.vsilu, 1)
                for j in range(2):
                    act.wait_ge(s.ssq, i * 2 + (j + 1))
                    ins = act.activation(rn[:, j, :], bank[j][:, :], ACT.Ln, bias=G.eps[:, 0:1])
                c.link(ins)
                for j in range(2):
                    act.activation(rn[:, j, :], rn[:, j, :], ACT.Exp, scale=-0.5).then_inc(s.rn, 1)

            def norm(i):
                act.wait_ge(s.oss, i + 1)
                c.link(act.activation(ornb[:], bank[1][:, :], ACT.Ln, bias=G.eps[:, 0:1], scale=1.0 / P))
                act.activation(ornb[:], ornb[:], ACT.Exp, scale=-0.5).then_inc(s.orn, 1)

            def head(i, more, first=False):
                for d in range(2):
                    act.wait_ge(s.dmin, i * 2 + (d + 1))
                    act.activation(Dx[:, d], Dx[:, d], ACT.Exp).then_inc(s.dexp, 1)
                    act.activation(egB[:, d], bank[4 + d][:, :], ACT.Exp).then_inc(s.egB, 1)
                act.wait_ge(s.kvt, i * 2 + 1)
                act.activation(ktok[:], four(bank[2]), ACT.Copy).then_inc(s.tok, 1)
                act.wait_ge(s.kvt, i * 2 + 2)
                act.activation(vtok[:], four(bank[3]), ACT.Copy).then_inc(s.tok, 1)
                if not first:
                    norm(i - 1)
                act.wait_ge(s.fin, i + 1)
                act.activation(zs[:], zn[:], ACT.Copy).then_inc(s.zs, 1)
                if more:
                    act.wait_ge(s.zs, i + 1)
                    front(i + 1)
                for st in range(NT):
                    for d in range(2):
                        n = chunk(d, st)
                        act.wait_ge(s.u, i * 8 + (2 * st + d + 1))
                        act.activation(vn[:, d, st % 2, :], bank[4 + d][:, 0:P], ACT.Copy,
                                       scale=smh[:, K_B, d, n:n + 1]).then_inc(s.vn, 1)
                act.wait_ge(s.o, i * 8 + 8)
                act.activation(osb[:], bank[0][:, :], ACT.Copy).then_inc(s.oc, 1)
                act.wait_ge(s.osum, i + 2)
                act.activation(osqb[:], osb[:], ACT.Square).then_inc(s.osq, 1)
                c.clear()

            front(0)
            c.clear()
            head(0, True, True)
            with act.Fori(1, GH - 1) as i:
                head(i, True)
            head(GH - 1, False)
            norm(GH - 1)

        @block.vector
        def _(dve):
            c = Chain(dve, s.chain)
            dve.sem_inc(s.osum, 1)
            dve.sem_inc(s.fin, 1)
            c.link(dve.memset(cb[:], 0.0))
            dve.wait_ge(s.ab, 1)
            dve.wait_ge(s.small, 80)
            c.link(dve.tensor_copy(ab[:], bank[0][:, 0:NT * 32].rearrange("p (t c) -> p t c", c=32)))
            c.link(dve.tensor_tensor(tmp[:, 0], ab[:, :, 0:16], dtb[:].unsqueeze(1).to_broadcast([P, NT, 16]), ALU.add))
            dve.tensor_scalar(tmp[:, 1], tmp[:, 0], 0.0, None, ALU.max)
            c.link(dve.tensor_scalar(tmp[:, 2], tmp[:, 0], -1.0, None, ALU.mult))
            dve.tensor_tensor(tmp[:, 2], tmp[:, 0], tmp[:, 2], ALU.min).then_inc(s.abs_, 1)
            dve.wait_ge(s.sc2, 1)
            c.link(dve.tensor_scalar(alog[:], alog[:], -1.0, None, ALU.mult))
            c.link(dve.tensor_scalar(tmp[:, 5], tmp[:, 5], 1.0, None, ALU.add))
            c.link(dve.reciprocal(tmp[:, 5], tmp[:, 5]))
            dve.wait_ge(s.sc3, 1)
            c.link(dve.tensor_tensor(tmp[:, 4], tmp[:, 4], tmp[:, 1], ALU.add))
            dve.tensor_tensor(gd[:].rearrange("p m n -> p n m"), tmp[:, 4], alog[:].unsqueeze(1).to_broadcast([P, NT, 16]),
                              ALU.mult).then_inc(s.gd, 1)
            dve.wait_ge(s.gd, 1)
            smv = [sm[:, :, k, :, :].rearrange("p h d n -> p d h n") for k in range(NK)]
            dve.tensor_copy(smv[K_G], gd[:].rearrange("p (d h) n -> p d h n", d=2))
            for d in range(2):
                dve.tensor_copy(sm[:, :, K_B, d, :], tmp[:, 5, :, d * 8:(d + 1) * 8].rearrange("p n h -> p h n"))
            dve.wait_ge(s.cum, 1)
            cum = bank[1][:, 0:64].rearrange("p (d h n) -> p d h n", d=2, h=8)
            tot = bank[1][:, 64:128].rearrange("p (d h n) -> p d h n", d=2, h=8)
            c.link(dve.tensor_copy(smv[K_GC], cum))
            dve.tensor_copy(smv[K_ESUM], tot).then_inc(s.cums, 1)
            dve.tensor_tensor(smv[K_EGL], tot, smv[K_GC], ALU.subtract).then_inc(s.cums, 1)
            dve.wait_ge(s.sc3, 2)
            dve.tensor_scalar(smv[K_NEG], smv[K_NEG], -1.0, None, ALU.mult).then_inc(s.sm_ready, 1)
            dve.wait_ge(s.sm_ready, 1)
            c.clear()

            def coefficients(i):
                cws, sms = cw[:, ds(i, 1), :] if not isinstance(i, int) else cw[:, i:i + 1, :], sm[:].rearrange("p h k d n -> p h (k d n)")
                c.link(dve.tensor_scalar(cwh[:].unsqueeze(1), cws, 1.0, None, ALU.mult))
                sms = sms[:, ds(i, 1), 0:4 * NT] if not isinstance(i, int) else sms[:, i:i + 1, 0:4 * NT]
                dve.tensor_scalar(smg[:].rearrange("p m d n -> p (m d n)").unsqueeze(1), sms, 1.0, None, ALU.mult).then_inc(s.coef, 1)

            def front_qk(i):
                dve.wait_ge(s.rn, i * 2 + 1)
                dve.scalar_tensor_tensor(qT[:], cv[:, 0, :], P ** -0.5, rn[:, 0, :], ALU.mult, ALU.mult).then_inc(s.qk, 1)
                dve.wait_ge(s.rn, i * 2 + 2)
                dve.tensor_tensor(kT[:], cv[:, 1, :], rn[:, 1, :], ALU.mult).then_inc(s.qk, 1)

            def front(i):
                smf, smhf = sm[:].rearrange("p h k d n -> p h (k d n)"), smh[:].rearrange("p k d n -> p (k d n)")
                smf = smf[:, ds(i, 1), :] if not isinstance(i, int) else smf[:, i:i + 1, :]
                dve.tensor_scalar(smhf.unsqueeze(1), smf, 1.0, None, ALU.mult).then_inc(s.smh, 1)
                for d in range(2):
                    dve.wait_ge(s.rb, i * 2 + (d + 1))
                    c.link(dve.tensor_tensor(Dx[:, d], four(bank[4 + d]), each4(smg[:, K_GC, d, :]), ALU.subtract))
                    dve.tensor_scalar(Dx[:, d], Dx[:, d], 0.0, None, ALU.min).then_inc(s.dmin, 1)

            def finish(i):
                dve.wait_ge(s.orn, i + 2)
                c.link(dve.scalar_tensor_tensor(osb[:], osb[:], na[:, 0:1], ornb[:], ALU.mult, ALU.mult))
                dve.wait_ge(s.zs, i + 1)
                dst = G.oaT[:, ds(i, 1), :] if not isinstance(i, int) else G.oaT[:, i:i + 1, :]
                dve.tensor_tensor(dst, osb[:].unsqueeze(1), zs[:].unsqueeze(1), ALU.mult).then_inc(s.fin, 1)

            def head(i, more, first=False):
                for d in range(2):
                    dve.wait_ge(s.dexp, i * 2 + (d + 1))
                    c.link(dve.tensor_tensor(Dx[:, d], Dx[:, d], over4(incl[d]), ALU.mult))
                    dve.wait_ge(s.bst, i * 2 + (d + 1))
                    c.link(dve.tensor_tensor(bst[:, d], bst[:, d], Dx[:, d], ALU.mult))
                    dve.wait_ge(s.kk, i + 1)
                    dve.tensor_tensor(AqT[:, d], Dx[:, d], four(bank[7]), ALU.mult)
                    dve.tensor_tensor(NTm[:, d], bst[:, d], four(bank[6]), ALU.mult).then_inc(s.nt, 1)
                dve.wait_ge(s.nt, i * 2 + 2)
                if not first:
                    finish(i - 1)
                if more:
                    coefficients(i + 1)
                invert_dve(dve, G, s, *inv, i * 14, i * 12)
                for st in range(NT):
                    if st:
                        for d in range(2):
                            n = chunk(d, st)
                            dve.wait_ge(s.ks, i * 6 + (2 * (st - 1) + d + 1))
                            dve.scalar_tensor_tensor(R[:, d, st % 2, :], bank[2 + d][:, 0:P], smh[:, K_NEG, d, n:n + 1],
                                                     vtok[:, n, :], ALU.mult, ALU.add).then_inc(s.r, 1)
                    if st < NT - 1:
                        for d in range(2):
                            n = chunk(d, st)
                            dve.wait_ge(s.su, i * 6 + (2 * st + d + 1))
                            if st:
                                dve.wait_ge(s.st, i * 6 + (2 * (st - 1) + d + 1))
                                ins = dve.scalar_tensor_tensor(S[:, d, st % 2, :], S[:, d, (st - 1) % 2, :], smh[:, K_ESUM, d, n:n + 1],
                                                               bank[6 + d][:, 0:P], ALU.mult, ALU.add)
                            else:
                                ins = dve.tensor_copy(S[:, d, 0, :], bank[6 + d][:, 0:P])
                            ins.then_inc(s.st, 1)
                if more:
                    front_qk(i + 1)
                dve.wait_ge(s.oc, i + 1)
                dve.tensor_tensor(osb[:], osb[:], bank[1][:, :], ALU.add).then_inc(s.osum, 1)
                if more:
                    front(i + 1)
                c.clear()

            coefficients(0)
            front_qk(0)
            front(0)
            c.clear()
            head(0, True, True)
            with dve.Fori(1, GH - 1) as i:
                head(i, True)
            head(GH - 1, False)
            dve.wait_ge(s.osum, GH + 1)
            finish(GH - 1)


def products(pe, bank, left, right, pairs, start=True, stop=True):
    for n, (l, r) in enumerate(pairs):
        pe.matmul(bank, left(0, l), right(0, r), start=(start and n == 0), stop=False)
        pe.matmul(bank, left(0, l), right(1, r), start=False, stop=False)
        ins = pe.matmul(bank, left(1, l), right(0, r), start=False, stop=(stop and n == len(pairs) - 1))
    return ins


def merge_phase(nc, G, name, w_a, w_b, wg_dram, cols, gate_bias=None):
    ka, kb = w_a.shape[0] // P, w_b.shape[0] // P
    with Phase(nc, name, "h_h h_l high low mm sig part mixed bias_in bias_h") as ph:
        s = ph.s
        a_ready, b_ready, g_ready = (ph.sems(n, 2) for n in ("a_ready", "b_ready", "g_ready"))
        wa = ph.sb("wa", [P, 2, ka, P])
        wb = ph.sb("wb", [P, 2, kb, P])
        wg = ph.sb("wg", [P, 2, KT, P])
        wgs = ph.sb("wgs", [P, 2, 2, 2, KT, P], F32R)
        hh = ph.sb("hh", [P, KT, T], F32R)
        hl = ph.sb("hl", [P, KT, T], F32R)
        sg = ph.sb("sg", [P, 2, 2, T])
        gb = ph.sb("gb", [P, KT, 2])
        gbh = ph.sb("gbh", [P, 2, 2])
        bank = ph.banks()
        block = ph.block()
        va, vb, vg = (w.rearrange("(k p) c -> p k c", p=P) for w in (w_a, w_b, wg_dram))

        @block.sync
        def _(sp):
            for q in range(2):
                sp.dma_start(wa[:, q], va[:, :, q * P:(q + 1) * P]).then_inc(a_ready[q], 16)
                sp.dma_start(wb[:, q], vb[:, :, q * P:(q + 1) * P]).then_inc(b_ready[q], 16)
                for n in range(2):
                    if q:
                        sp.wait_ge(s.low, n + 1)
                    sp.dma_start(wg[:, n], vg[:, :, cols[n] + q * P:cols[n] + (q + 1) * P]).then_inc(g_ready[n], 16)
                if q == 0 and gate_bias is not None:
                    sp.dma_start(gb[:], gate_bias).then_inc(s.bias_in, 16)
            with sp.Fori(1, KT // 2) as i:
                for j in range(2):
                    col = sp.snap(i * 2 * P + j * P)
                    sp.wait_ge(s.mm, sp.snap(i * 8 + (4 * j - 7)))
                    sp.dma_start(wa[:, j], va[:, :, ds(col, P)]).then_inc(a_ready[j], 16)
                    sp.wait_ge(s.mm, sp.snap(i * 8 + (4 * j - 6)))
                    sp.dma_start(wb[:, j], vb[:, :, ds(col, P)]).then_inc(b_ready[j], 16)
                    for n in range(2):
                        gcol = sp.snap(i * 2 * P + (j * P + cols[n]))
                        sp.wait_ge(s.low, sp.snap(i * 4 + (2 * j + n - 1)))
                        sp.dma_start(wg[:, n], vg[:, :, ds(gcol, P)]).then_inc(g_ready[n], 16)

        @block.gpsimd
        def _(pool):
            with pool.Fori(0, KT // 2) as i:
                for j in range(2):
                    for n in range(2):
                        pool.wait_ge(s.high, i * 4 + (2 * j + n + 1))
                        pool.tensor_tensor(wgs[:, j, n, 1], wg[:, n], wgs[:, j, n, 0], ALU.subtract).then_inc(s.low, 1)

        @block.tensor
        def _(pe):
            def step(i, j):
                pe.wait_ge(s.mixed, i * 2 + (j + 1))
                pe.wait_ge(a_ready[j], i * 16 + 16)
                for k in range(ka):
                    ins = pe.matmul(bank[4 * j][:, :], wa[:, j, k, :], G.oaT[:, k, :], start=(k == 0), stop=(k == ka - 1))
                ins.then_inc(s.mm, 1)
                pe.wait_ge(b_ready[j], i * 16 + 16)
                for k in range(kb):
                    ins = pe.matmul(bank[4 * j + 1][:, :], wb[:, j, k, :], G.obT[:, k, :], start=(k == 0), stop=(k == kb - 1))
                ins.then_inc(s.mm, 1)
                if isinstance(i, int) and j == 0:
                    pe.wait_ge(s.h_l, KT)
                for n in range(2):
                    pe.wait_ge(s.low, i * 4 + (2 * j + n + 1))
                    products(pe, bank[4 * j + 2 + n][:, :], lambda part, k: wgs[:, j, n, part, k, :],
                             lambda part, k: (hh, hl)[part][:, k, :], [(k, k) for k in range(KT)]).then_inc(s.mm, 1)

            step(0, 0)
            step(0, 1)
            with pe.Fori(1, KT // 2) as i:
                step(i, 0)
                step(i, 1)

        @block.scalar
        def _(act):
            def high(i, j):
                for n in range(2):
                    act.wait_ge(g_ready[n], i * 32 + (16 * j + 16))
                    if not (isinstance(i, int) and i == 0):
                        act.wait_ge(s.mm, i * 8 + (4 * j + n - 5))
                        act.wait_ge(s.low, i * 4 + (2 * j + n - 3))
                    act.activation(wgs[:, j, n, 0], wg[:, n], ACT.Copy).then_inc(s.high, 1)

            def gates(i, j):
                act.wait_ge(s.mixed, i * 2 + (j + 1))
                if gate_bias is not None:
                    act.wait_ge(s.bias_h, i * 2 + (j + 1))
                for n in range(2):
                    act.wait_ge(s.mm, i * 8 + (j * 4 + n + 3))
                    act.activation(sg[:, j, n, :], bank[j * 4 + 2 + n][:, :], ACT.Sigmoid,
                                   bias=gbh[:, j, n:n + 1] if gate_bias is not None else 0.0).then_inc(s.sig, 1)

            for k in range(KT):
                act.activation(hh[:, k, :], G.hT[:, k, :], ACT.Copy).then_inc(s.h_h, 1)
            high(0, 0)
            high(0, 1)
            gates(0, 0)
            high(1, 0)
            gates(0, 1)
            with act.Fori(1, KT // 2 - 1) as i:
                high(i, 1)
                gates(i, 0)
                high(i + 1, 0)
                gates(i, 1)
            high(KT // 2 - 1, 1)
            gates(KT // 2 - 1, 0)
            gates(KT // 2 - 1, 1)

        @block.vector
        def _(dve):
            dve.sem_inc(s.mixed, 2)
            for k in range(KT):
                dve.wait_ge(s.h_h, k + 1)
                dve.tensor_tensor(hl[:, k, :], G.hT[:, k, :], hh[:, k, :], ALU.subtract).then_inc(s.h_l, 1)
            if gate_bias is not None:
                dve.wait_ge(s.bias_in, 16)
            with dve.Fori(0, KT // 2) as i:
                for j in range(2):
                    if gate_bias is not None:
                        dve.wait_ge(s.mixed, i * 2 + (j + 1))
                        dve.tensor_scalar(gbh[:, j:j + 1, :], gb[:, ds(i * 2 + j, 1), :], 1.0, None, ALU.mult).then_inc(s.bias_h, 1)
                for j in range(2):
                    for n in range(2):
                        dve.wait_ge(s.sig, i * 4 + (j * 2 + n + 1))
                        dve.tensor_tensor(sg[:, j, n, :], sg[:, j, n, :], bank[j * 4 + n][:, :], ALU.mult).then_inc(s.part, 1)
                    dve.wait_ge(s.part, i * 4 + (j * 2 + 2))
                    dve.tensor_tensor(G.mT[:, ds(i * 2 + j, 1), :], sg[:, j, 0:1, :], sg[:, j, 1:2, :], ALU.add).then_inc(s.mixed, 1)


def out_phase(nc, G, name, w_out, residual):
    with Phase(nc, name, "w_h w_l m_h m_l done") as ph:
        s = ph.s
        w_ready = ph.sems("w_ready", KT)
        wr = ph.sb("wr", [P, KT, D])
        ws = ph.sb("ws", [P, KT, 2, D], F32R)
        ms = ph.sb("ms", [P, KT, 2, T], F32R)
        bank = ph.banks()
        block = ph.block()

        @block.sync
        def _(sp):
            for k in range(KT):
                sp.dma_start(wr[:, k, :], w_out[k * P:(k + 1) * P, :]).then_inc(w_ready[k], 16)

        @block.tensor
        def _(pe):
            for k in range(KT):
                pe.wait_ge(s.m_l, k + 1)
                pe.wait_ge(s.w_l, k + 1)
                for t in range(NT):
                    for half in range(2):
                        ins = products(pe, bank[2 * t + half][:, :], lambda part, k: ms[:, k, part, t * P:(t + 1) * P],
                                       lambda part, k: ws[:, k, part, half * 512:(half + 1) * 512], [(k, k)],
                                       start=(k == 0), stop=(k == KT - 1))
                        if k == KT - 1:
                            ins.then_inc(s.done, 1)

        @block.scalar
        def _(act):
            for k in range(KT):
                act.activation(ms[:, k, 0], G.mT[:, k, :], ACT.Copy).then_inc(s.m_h, 1)
                act.wait_ge(w_ready[k], 16)
                act.activation(ws[:, k, 0], wr[:, k, :], ACT.Copy).then_inc(s.w_h, 1)

        @block.gpsimd
        def _(pool):
            for k in range(KT):
                pool.wait_ge(s.w_h, k + 1)
                pool.tensor_tensor(ws[:, k, 1], wr[:, k, :], ws[:, k, 0], ALU.subtract).then_inc(s.w_l, 1)

        @block.vector
        def _(dve):
            for k in range(KT):
                dve.wait_ge(s.m_h, k + 1)
                dve.tensor_tensor(ms[:, k, 1], G.mT[:, k, :], ms[:, k, 0], ALU.subtract).then_inc(s.m_l, 1)
            for b in range(8):
                dve.wait_ge(s.done, b + 1)
                t, c0 = b // 2, slice((b % 2) * 512, (b % 2 + 1) * 512)
                if residual:
                    dve.tensor_tensor(G.X[:, t, c0], G.X[:, t, c0], bank[b][:, :], ALU.add)
                else:
                    dve.tensor_copy(G.Y[:, t, c0], bank[b][:, :])


def ffn_phase(nc, G, groups, view_up, view_down):
    with Phase(nc, "ff", "up_in down_in up_h up_l down_h down_l h_h h_l up relu square he_h he_l down added zero") as ph:
        s = ph.s
        wu = ph.sb("wu", [P, KT, DE])
        wd = ph.sb("wd", [P, 2, D])
        wus = ph.sb("wus", [P, 2, 2, KT, DE], F32R)
        wds = ph.sb("wds", [P, 2, 2, 2, D], F32R)
        he = ph.sb("he", [P, 2, T])
        hes = ph.sb("hes", [P, 2, 2, 2, T], F32R)
        rl = ph.sb("rl", [P, 2, T])
        hh = ph.sb("hh", [P, KT, T], F32R)
        hl = ph.sb("hl", [P, KT, T], F32R)
        bank = ph.banks()
        block = ph.block()
        last = groups // 2 - 1

        @block.sync
        def _(sp):
            def load_up(g):
                sp.dma_start(wu[:], view_up(g)).then_inc(s.up_in, 16)

            def load_down(g):
                sp.dma_start(wd[:], view_down(g)).then_inc(s.down_in, 16)

            load_up(0)
            load_down(0)
            sp.wait_ge(s.up_l, 1)
            load_up(1)
            with sp.Fori(0, last) as i:
                for j in range(2):
                    g1, g2 = sp.snap(i * 2 + (j + 1)), sp.snap(i * 2 + (j + 2))
                    sp.wait_ge(s.up_l, g2)
                    load_up(g2)
                    sp.wait_ge(s.down_l, g1)
                    load_down(g1)
            sp.wait_ge(s.down_l, groups - 1)
            load_down(groups - 1)

        @block.gpsimd
        def _(pool):
            def low_up(i, j):
                pool.wait_ge(s.up_h, i * 2 + (j + 1))
                pool.tensor_tensor(wus[:, j, 1], wu[:], wus[:, j, 0], ALU.subtract).then_inc(s.up_l, 1)

            def low_down(i, j):
                pool.wait_ge(s.down_h, i * 2 + (j + 1))
                pool.tensor_tensor(wds[:, j, 1], wd[:], wds[:, j, 0], ALU.subtract).then_inc(s.down_l, 1)

            low_up(0, 0)
            low_up(0, 1)
            low_down(0, 0)
            with pool.Fori(0, last) as i:
                low_up(i + 1, 0)
                low_down(i, 1)
                low_up(i + 1, 1)
                low_down(i + 1, 0)
            low_down(last, 1)

        @block.tensor
        def _(pe):
            def up(i, j):
                pe.wait_ge(s.up_l, i * 2 + (j + 1))
                for f in range(2):
                    pe.wait_ge(s.relu, (i * 2 + j) * 2 + (f + 1))
                    if isinstance(i, int) and i == 0 and j == 0:
                        pe.wait_ge(s.h_l, KT)
                    ins = products(pe, bank[2 * j + f][:, :], lambda part, k: wus[:, j, part, k, f * P:(f + 1) * P],
                                   lambda part, k: (hh, hl)[part][:, k, :], [(k, k) for k in range(KT)])
                    ins.then_inc(s.up, 1)

            def down(i, j):
                pe.wait_ge(s.down_l, i * 2 + (j + 1))
                pe.wait_ge(s.he_l, i * 2 + (j + 1))
                for o in range(8):
                    t, half = o // 2, o % 2
                    pe.wait_ge(s.added, (i * 2 + j) * 8 + (o + 1))
                    ins = products(pe, bank[4 + o % 4][:, :], lambda part, f: hes[:, j, part, f, t * P:(t + 1) * P],
                                   lambda part, f: wds[:, j, part, f, half * 512:(half + 1) * 512], [(0, 0), (1, 1)])
                    ins.then_inc(s.down, 1)

            up(0, 0)
            with pe.Fori(0, last) as i:
                up(i, 1)
                down(i, 0)
                up(i + 1, 0)
                down(i, 1)
            up(last, 1)
            down(last, 0)
            down(last, 1)

        @block.scalar
        def _(act):
            act.sem_inc(s.relu, 4)

            def high_up(i, j):
                act.wait_ge(s.up_in, i * 32 + (j * 16 + 16))
                if not (isinstance(i, int) and i == 0):
                    act.wait_ge(s.up, i * 4 + 2 * (j - 1))
                    act.wait_ge(s.up_l, i * 2 + (j - 1))
                act.activation(wus[:, j, 0], wu[:], ACT.Copy).then_inc(s.up_h, 1)

            def high_down(i, j):
                act.wait_ge(s.down_in, i * 32 + (j * 16 + 16))
                if not (isinstance(i, int) and i == 0):
                    act.wait_ge(s.down, i * 16 + 8 * (j - 1))
                act.activation(wds[:, j, 0], wd[:], ACT.Copy).then_inc(s.down_h, 1)

            def units(i, j):
                for f in range(2):
                    act.wait_ge(s.up, (i * 2 + j) * 2 + (f + 1))
                    if not (isinstance(i, int) and i == 0 and j == 0):
                        act.wait_ge(s.square, (i * 2 + j) * 2 + (f - 1))
                    act.activation(rl[:, f, :], bank[2 * j + f][:, :], ACT.Relu).then_inc(s.relu, 1)
                act.wait_ge(s.square, (i * 2 + j) * 2 + 2)
                if not (isinstance(i, int) and i == 0):
                    act.wait_ge(s.down, i * 16 + 8 * (j - 1))
                act.activation(hes[:, j, 0], he[:], ACT.Copy).then_inc(s.he_h, 1)

            for k in range(KT):
                act.activation(hh[:, k, :], G.hT[:, k, :], ACT.Copy).then_inc(s.h_h, 1)
            high_up(0, 0)
            high_down(0, 0)
            high_up(0, 1)
            units(0, 0)
            high_up(1, 0)
            high_down(0, 1)
            units(0, 1)
            high_up(1, 1)
            high_down(1, 0)
            with act.Fori(1, last) as i:
                units(i, 0)
                high_up(i + 1, 0)
                high_down(i, 1)
                units(i, 1)
                high_up(i + 1, 1)
                high_down(i + 1, 0)
            units(last, 0)
            high_down(last, 1)
            units(last, 1)

        @block.vector
        def _(dve):
            dve.sem_inc(s.added, 4)
            for k in range(KT):
                dve.wait_ge(s.h_h, k + 1)
                dve.tensor_tensor(hl[:, k, :], G.hT[:, k, :], hh[:, k, :], ALU.subtract).then_inc(s.h_l, 1)
            dve.memset(G.Y[:], 0.0).then_inc(s.zero, 1)
            dve.wait_ge(s.zero, 1)

            def hidden(i, j):
                for f in range(2):
                    dve.wait_ge(s.relu, (i * 2 + j) * 2 + (f + 1 + 4))
                    if f == 0 and not (isinstance(i, int) and i == 0 and j == 0):
                        dve.wait_ge(s.he_l, i * 2 + j)
                    dve.tensor_tensor(he[:, f, :], rl[:, f, :], rl[:, f, :], ALU.mult).then_inc(s.square, 1)
                dve.wait_ge(s.he_h, i * 2 + (j + 1))
                dve.tensor_tensor(hes[:, j, 1], he[:], hes[:, j, 0], ALU.subtract).then_inc(s.he_l, 1)

            def add(i, j):
                for o in range(8):
                    y = G.Y[:, o // 2, (o % 2) * 512:(o % 2 + 1) * 512]
                    dve.wait_ge(s.down, (i * 2 + j) * 8 + (o + 1))
                    if o == 0:
                        dve.wait_ge(s.added, (i * 2 + j) * 8 + 4)
                    dve.tensor_tensor(y, y, bank[4 + o % 4][:, :], ALU.add).then_inc(s.added, 1)

            hidden(0, 0)
            hidden(0, 1)
            add(0, 0)
            hidden(1, 0)
            add(0, 1)
            with dve.Fori(1, last) as i:
                hidden(i, 1)
                add(i, 0)
                hidden(i + 1, 0)
                add(i, 1)
            hidden(last, 1)
            add(last, 0)
            add(last, 1)


SLOTS = 40


def router_phase(nc, G, w_router, b_router, rows, expert, place, weight):
    NR = NGRP + NEXP
    with Phase(nc, "rt", "ins mm dif e1 e2 picked counted sel listed chain") as ph:
        s = ph.s
        wr = ph.sb("wr", [P, KT, NR])
        br = ph.sb("br", [P, NR])
        lg = ph.sb("lg", [P, NT, NR])
        w4 = ph.sb("w4", [P, 4, NT, NGRP])
        w32 = ph.sb("w32", [P, 5, NT, NEXP])
        c1 = ph.sb("c1", [P, 10, NT])
        both = ph.sb("both", [P, NT, NEXP])
        cnt = ph.sb("cnt", [P, NT, NEXP])
        ne = ph.sb("ne", [P, 6, NEXP])
        pos = ph.sb("pos", [P, 6, 2, NT])
        R1 = ph.sb("R1", [P, 2, NT, P])
        S1 = ph.sb("S1", [P, 2, NT, SLOTS])
        past = ph.sb("past", [P, SLOTS, NEXP])
        es = ph.sb("es", [P, SLOTS])
        bank = ph.banks(3)
        block = ph.block()

        @block.sync
        def _(sp):
            sp.dma_start(wr[:], w_router.rearrange("(k p) c -> p k c", p=P)).then_inc(s.ins, 16)
            sp.dma_start(br[:], bcast_rows(b_router, 1, NR)).then_inc(s.ins, 16)

        @block.tensor
        def _(pe):
            pe.wait_ge(s.ins, 32)
            for t in range(NT):
                for k in range(KT):
                    ins = pe.matmul(bank[0][:, t * NR:(t + 1) * NR], G.hT[:, k, t * P:(t + 1) * P], wr[:, k, :],
                                    start=(k == 0), stop=(k == KT - 1))
            ins.then_inc(s.mm, 1)
            pe.wait_ge(s.picked, 1)
            for t in range(NT):
                for u in range(t + 1):
                    pe.matmul(bank[1][:, t * NEXP:(t + 1) * NEXP], G.c("lt" if u == t else "ones"), both[:, u, :],
                              start=(u == 0), stop=(u == t))
            for u in range(NT):
                ins = pe.matmul(bank[1][:, NT * NEXP:(NT + 1) * NEXP], G.c("ones"), both[:, u, :], start=(u == 0), stop=(u == NT - 1))
            ins.then_inc(s.counted, 1)
            pe.wait_ge(s.sel, 1)
            for m in range(2 * NT):
                ins = pe.matmul(bank[2][:, 0:SLOTS], R1[:, m // NT, m % NT, :], S1[:, m // NT, m % NT, :],
                                start=(m == 0), stop=(m == 2 * NT - 1))
            ins.then_inc(s.listed, 1)

        @block.scalar
        def _(act):
            act.wait_ge(s.dif, 1)
            act.activation(w4[:, 1], w4[:, 1], ACT.Exp).then_inc(s.e1, 1)
            act.wait_ge(s.dif, 2)
            act.activation(c1[:, 6], c1[:, 6], ACT.Exp).then_inc(s.e2, 1)

        @block.vector
        def _(dve):
            c = Chain(dve, s.chain)

            def wide(col, n):
                return col.unsqueeze(2).to_broadcast([P, NT, n])

            def first_max(x, n, value, mask, work):
                index = G.c("idx", 0, n).unsqueeze(1).to_broadcast([P, NT, n])
                c.link(dve.tensor_reduce(value, x, AX, ALU.max))
                c.link(dve.tensor_tensor(work, x, wide(value, n), ALU.is_equal))
                c.link(dve.tensor_tensor(work, work, index, ALU.mult))
                c.link(dve.tensor_reduce(c1[:, 9], work, AX, ALU.max))
                c.link(dve.tensor_tensor(mask, work, wide(c1[:, 9], n), ALU.is_equal))

            dve.wait_ge(s.mm, 1)
            c.link(dve.tensor_tensor(lg[:], bank[0][:, 0:NT * NR].rearrange("p (t c) -> p t c", t=NT),
                                     br[:].unsqueeze(1).to_broadcast([P, NT, NR]), ALU.add))
            g, e = lg[:, :, 0:NGRP], lg[:, :, NGRP:NR]
            first_max(g, NGRP, c1[:, 0], w4[:, 0], w4[:, 2])
            dve.tensor_tensor(w4[:, 1], g, wide(c1[:, 0], NGRP), ALU.subtract).then_inc(s.dif, 1)
            dve.wait_ge(s.e1, 1)
            c.link(dve.tensor_reduce(c1[:, 1], w4[:, 1], AX, ALU.add))
            c.link(dve.reciprocal(c1[:, 2], c1[:, 1]))
            em, el = w32[:, 0], w32[:, 1]
            for q in range(NGRP):
                ins = dve.tensor_scalar(em[:, :, 8 * q:8 * q + 8], w4[:, 0, :, q:q + 1].to_broadcast([P, NT, 8]), 1.0, None, ALU.mult)
            c.link(ins)
            c.link(dve.tensor_tensor(el, e, em, ALU.mult))
            c.link(dve.tensor_scalar(em, em, -NEG, NEG, ALU.mult, ALU.add))
            c.link(dve.tensor_tensor(el, el, em, ALU.add))
            first_max(el, NEXP, c1[:, 3], w32[:, 2], w32[:, 4])
            c.link(dve.tensor_scalar(em, w32[:, 2], NEG, None, ALU.mult))
            c.link(dve.tensor_tensor(el, el, em, ALU.add))
            first_max(el, NEXP, c1[:, 4], w32[:, 3], w32[:, 4])
            dve.tensor_tensor(c1[:, 6], c1[:, 4], c1[:, 3], ALU.subtract).then_inc(s.dif, 1)
            dve.wait_ge(s.e2, 1)
            c.link(dve.tensor_scalar(c1[:, 7], c1[:, 6], 1.0, None, ALU.add))
            c.link(dve.reciprocal(c1[:, 7], c1[:, 7]))
            c.link(dve.tensor_tensor(weight[:, :, 0], c1[:, 7], c1[:, 2], ALU.mult))
            dve.tensor_tensor(weight[:, :, 1], weight[:, :, 0], c1[:, 6], ALU.mult)
            mk = (w32[:, 2], w32[:, 3])
            dve.tensor_tensor(both[:], mk[0], mk[1], ALU.add).then_inc(s.picked, 1)
            dve.wait_ge(s.counted, 1)
            c.link(dve.tensor_copy(cnt[:], bank[1][:, 0:NT * NEXP].rearrange("p (t e) -> p t e", t=NT)))
            c.link(dve.tensor_copy(ne[:, 0], bank[1][:, NT * NEXP:(NT + 1) * NEXP]))

            def steps(out, x, first, n, spare):
                c.link(dve.tensor_scalar(out, x, float(first), None, ALU.is_ge))
                for m in range(1, n):
                    c.link(dve.tensor_scalar(spare, x, float(first + P * m), None, ALU.is_ge))
                    c.link(dve.tensor_tensor(out, out, spare, ALU.add))

            steps(ne[:, 1], ne[:, 0], 1, NT, ne[:, 2])
            c.link(dve.tensor_copy(ne[:, 3], ne[:, 1]))
            src, dst = 3, 4
            for m in range(5):
                sh = 1 << m
                c.link(dve.tensor_copy(ne[:, dst, 0:sh], ne[:, src, 0:sh]))
                c.link(dve.tensor_tensor(ne[:, dst, sh:NEXP], ne[:, src, sh:NEXP], ne[:, src, 0:NEXP - sh], ALU.add))
                src, dst = dst, src
            last = ne[:, src]
            c.link(dve.tensor_tensor(ne[:, 5], last, ne[:, 1], ALU.subtract))
            for q in range(2):
                for what, table in ((0, cnt[:]), (1, ne[:, 5].unsqueeze(1).to_broadcast([P, NT, NEXP]))):
                    c.link(dve.tensor_tensor(w32[:, 4], mk[q], table, ALU.mult))
                    c.link(dve.tensor_reduce(pos[:, what, q, :], w32[:, 4], AX, ALU.add))
            steps(pos[:, 2], pos[:, 0], P, NT - 1, pos[:, 5])
            c.link(dve.tensor_tensor(pos[:, 3], pos[:, 1], pos[:, 2], ALU.add))
            c.link(dve.scalar_tensor_tensor(pos[:, 4], pos[:, 2], -float(P), pos[:, 0], ALU.mult, ALU.add))
            c.link(dve.scalar_tensor_tensor(pos[:, 5], pos[:, 3], float(P), pos[:, 4], ALU.mult, ALU.add))
            dve.tensor_copy(place[:].rearrange("p t q -> p q t"), pos[:, 5])
            for q in range(2):
                for t in range(NT):
                    dve.tensor_scalar(R1[:, q, t, :], G.c("iota"), pos[:, 4, q, t:t + 1], G.c("tok", t, t + 1), ALU.is_equal, ALU.mult)
                    ins = dve.tensor_scalar(S1[:, q, t, :], G.c("iota", 0, SLOTS), pos[:, 3, q, t:t + 1], None, ALU.is_equal)
            ins.then_inc(s.sel, 1)
            c.link(dve.tensor_tensor(past[:], last.unsqueeze(1).to_broadcast([P, SLOTS, NEXP]),
                                     G.c("iota", 0, SLOTS).unsqueeze(2).to_broadcast([P, SLOTS, NEXP]), ALU.is_le))
            c.link(dve.tensor_reduce(es[:], past[:], AX, ALU.add))
            c.link(dve.tensor_scalar(expert[:], es[:], float(NEXP - 1), None, ALU.min))
            dve.wait_ge(s.listed, 1)
            dve.tensor_copy(rows[:], bank[2][:, 0:SLOTS])


def moe_phase(nc, G, w_gate, w_up, w_down, rows, expert, rows_dram, y_dram):
    with Phase(nc, "moe", "turned hg_in act_s hid turned2 heT gu down stored y0 y1") as ph:
        s = ph.s
        gu_ready, dn_ready, h_in, y_out = (ph.sems(n, 2) for n in ("gu_ready", "dn_ready", "h_in", "y_out"))
        wgu = ph.sb("wgu", [P, 2, KT, 2 * DE])
        wd = ph.sb("wd", [P, 2, 2, D])
        hg = ph.sb("hg", [P, 2, D])
        hgT = ph.sb("hgT", [P, 2, KT, P])
        sl = ph.sb("sl", [P, 2, DE])
        he = ph.sb("he", [P, 2, DE])
        heT = ph.sb("heT", [P, 2, 2, P])
        yo = ph.sb("yo", [P, 2, D])
        bank = ph.banks()
        block = ph.block()
        HALF = SLOTS // 2

        @block.sync
        def _(sp):
            def load(slot, j, gu_used, dn_used):
                e = sp.value_load(expert[0:1, ds(slot, 1)] if not isinstance(slot, int) else expert[0:1, slot:slot + 1],
                                  min_val=0, max_val=NEXP - 1)
                if gu_used is not None:
                    sp.wait_ge(s.gu, gu_used)
                sp.dma_start(wgu[:, j, :, 0:DE], one_of(w_gate, e)).then_inc(gu_ready[j], 16)
                sp.dma_start(wgu[:, j, :, DE:2 * DE], one_of(w_up, e)).then_inc(gu_ready[j], 16)
                if dn_used is not None:
                    sp.wait_ge(s.down, dn_used)
                sp.dma_start(wd[:, j], one_of(w_down, e)).then_inc(dn_ready[j], 16)

            load(0, 0, None, None)
            load(1, 1, None, None)
            with sp.Fori(1, HALF) as i:
                for j in range(2):
                    load(sp.snap(i * 2 + j), j, sp.snap(i * 2 + (j - 1)), sp.snap(i * 4 + 2 * (j - 1)))

        @block.gpsimd
        def _(pool):
            for slot in range(SLOTS):
                j = slot % 2
                if slot >= 2:
                    pool.wait_ge(s.turned, 2 * (slot - 1))
                pool.indirect_dma_start(hg[:, j, :], None, rows_dram, bass.IndirectOffsetOnAxis(rows[:, slot:slot + 1], 0)
                                        ).then_inc(h_in[j], 16)

        @block.tensor
        def _(pe):
            def turn(i, j):
                pe.wait_ge(h_in[j], i * 16 + 16)
                for half in range(2):
                    pe.wait_ge(s.act_s, (i * 2 + j) * 2 + half + 1)
                    for k in range(4):
                        kk = 4 * half + k
                        ins = pe.transpose(bank[half][:, k * P:(k + 1) * P], hg[:, j].rearrange("p (c k) -> p k c", k=KT)[:, kk], G.c("ident"))
                    ins.then_inc(s.turned, 1)

            def gate_up(i, j):
                pe.wait_ge(gu_ready[j], i * 32 + 32)
                pe.wait_ge(s.act_s, (i * 2 + j) * 2 + 4)
                pe.wait_ge(s.hid, i * 2 + (j + 1))
                for k in range(KT):
                    ins = pe.matmul(bank[2 + j][:, :], hgT[:, j, k, :], wgu[:, j, k, :], start=(k == 0), stop=(k == KT - 1))
                ins.then_inc(s.gu, 1)

            def turn_hidden(i, j):
                pe.wait_ge(s.hid, i * 2 + (j + 3))
                pe.wait_ge(s.heT, i * 2 + (j + 1))
                for f in range(2):
                    ins = pe.transpose(bank[4][:, f * P:(f + 1) * P], he[:, j, f * P:(f + 1) * P], G.c("ident"))
                ins.then_inc(s.turned2, 1)

            def down(i, j):
                pe.wait_ge(dn_ready[j], i * 16 + 16)
                pe.wait_ge(s.heT, i * 2 + (j + 2))
                for half in range(2):
                    pe.wait_ge(s.y0 if half == 0 else s.y1, i * 2 + (j + 1))
                    for f in range(2):
                        ins = pe.matmul(bank[5 + half][:, :], heT[:, j, f, :], wd[:, j, f, half * 512:(half + 1) * 512],
                                        start=(f == 0), stop=(f == 1))
                    ins.then_inc(s.down, 1)

            def body(i, more):
                gate_up(i, 1)
                turn_hidden(i, 0)
                if more:
                    turn(i + 1, 0)
                down(i, 0)
                if more:
                    gate_up(i + 1, 0)
                turn_hidden(i, 1)
                if more:
                    turn(i + 1, 1)
                down(i, 1)

            turn(0, 0)
            gate_up(0, 0)
            turn(0, 1)
            with pe.Fori(0, HALF - 1) as i:
                body(i, True)
            body(HALF - 1, False)

        @block.scalar
        def _(act):
            act.sem_inc(s.act_s, 2)
            act.sem_inc(s.y0, 1)

            def rows_in(i, j):
                for half in range(2):
                    act.wait_ge(s.turned, (i * 2 + j) * 2 + (half + 1))
                    if half == 0:
                        act.wait_ge(s.gu, i * 2 + (j - 1)) if not (isinstance(i, int) and i == 0) else None
                    act.activation(hgT[:, j, 4 * half:4 * half + 4, :], four(bank[half]), ACT.Copy).then_inc(s.act_s, 1)

            def silu(i, j):
                act.wait_ge(s.gu, i * 2 + (j + 1))
                act.activation(sl[:, j, :], bank[2 + j][:, 0:DE], ACT.Silu).then_inc(s.hg_in, 1)

            def take(i, j):
                act.wait_ge(s.down, (i * 2 + j) * 2 + 1)
                act.wait_ge(y_out[j], i * 16) if not (isinstance(i, int) and i == 0) else None
                act.activation(yo[:, j, 0:512], bank[5][:, :], ACT.Copy).then_inc(s.y0, 1)
                act.wait_ge(s.y0, i * 2 + (j + 2))
                act.wait_ge(s.y1, i * 2 + (j + 2))
                if isinstance(i, int):
                    act.dma_start(y_dram[(2 * i + j) * P:(2 * i + j + 1) * P, :], yo[:, j, :]).then_inc(y_out[j], 16)
                else:
                    act.dma_start(y_dram[ds(act.snap(i * (2 * P) + j * P), P), :], yo[:, j, :]).then_inc(y_out[j], 16)

            def body(i, more, first=False):
                silu(i, 1)
                if more:
                    rows_in(i + 1, 0)
                take(i, 0)
                if more:
                    silu(i + 1, 0)
                    rows_in(i + 1, 1)
                take(i, 1)

            rows_in(0, 0)
            silu(0, 0)
            rows_in(0, 1)
            body(0, True)
            with act.Fori(1, HALF - 1) as i:
                body(i, True)
            body(HALF - 1, False)
            for j in range(2):
                act.wait_ge(y_out[j], 16 * HALF)

        @block.vector
        def _(dve):
            dve.sem_inc(s.hid, 2)
            dve.sem_inc(s.heT, 1)
            dve.sem_inc(s.y1, 1)

            def hidden(i, j):
                dve.wait_ge(s.hg_in, i * 2 + (j + 1))
                if not (isinstance(i, int) and i == 0):
                    dve.wait_ge(s.turned2, i * 2 + (j - 1))
                dve.tensor_tensor(he[:, j, :], sl[:, j, :], bank[2 + j][:, DE:2 * DE], ALU.mult).then_inc(s.hid, 1)

            def take_hidden(i, j):
                dve.wait_ge(s.turned2, i * 2 + (j + 1))
                dve.tensor_copy(heT[:, j].rearrange("p f c -> p (f c)"), bank[4][:, 0:2 * P]).then_inc(s.heT, 1)

            def take(i, j):
                dve.wait_ge(s.down, (i * 2 + j) * 2 + 2)
                if not (isinstance(i, int) and i == 0):
                    dve.wait_ge(y_out[j], i * 16)
                dve.tensor_copy(yo[:, j, 512:D], bank[6][:, :]).then_inc(s.y1, 1)

            def body(i, more):
                hidden(i, 1)
                take_hidden(i, 0)
                take(i, 0)
                if more:
                    hidden(i + 1, 0)
                take_hidden(i, 1)
                take(i, 1)

            hidden(0, 0)
            body(0, True)
            with dve.Fori(1, HALF - 1) as i:
                body(i, True)
            body(HALF - 1, False)


def one_of(view, e):
    return view[ds(e, 1)].rearrange("a p k c -> p (a k) c")


def final_phase(nc, G, place, weight, y_dram, out):
    with Phase(nc, "fin", "sum out chain") as ph:
        s = ph.s
        got = ph.sems("got", 2 * NT)
        yg = ph.sb("yg", [P, 2 * NT, D])
        block = ph.block()

        @block.gpsimd
        def _(pool):
            for m in range(2 * NT):
                pool.indirect_dma_start(yg[:, m, :], None, y_dram, bass.IndirectOffsetOnAxis(place[:, m // 2, m % 2:m % 2 + 1], 0)
                                        ).then_inc(got[m], 16)

        @block.vector
        def _(dve):
            c = Chain(dve, s.chain)
            for m in range(2 * NT):
                t, q = m // 2, m % 2
                dve.wait_ge(got[m], 16)
                ins = dve.scalar_tensor_tensor(G.X[:, t], yg[:, m, :], weight[:, t, q:q + 1], G.X[:, t], ALU.mult, ALU.add)
                if q == 0:
                    c.link(ins)
                else:
                    ins.then_inc(s.sum, 1)

        @block.sync
        def _(sp):
            for t in range(NT):
                sp.wait_ge(s.sum, t + 1)
                sp.dma_start(out[0, t * P:(t + 1) * P, :], G.X[:, t, :]).then_inc(s.out, 16)
            sp.wait_ge(s.out, 16 * NT)


def grid_attention_phase(nc, G, w_in, rpb, gains, pad_dram):
    with Phase(nc, "na", "rpb_in zeroed padded pad_out toep small proj copied sqd ssq rn qk pn logits taken negmax expd "
               "p_ready turned pt out out_taken bias_ready chain achain") as ph:
        s = ph.s
        w_ready = ph.sems("w_ready", 3)
        wr = ph.sb("wr", [P, 3, KT, P])
        pad = ph.sb("pad", [120, 127])
        bias = ph.sb("bias", [P, 8, 14, 64])
        gn = ph.sb("gn", [P, 2])
        raw = ph.sb("raw", [P, 2, T])
        sq = ph.sb("sq", [P, 2, T])
        rn = ph.sb("rn", [P, 2, T])
        qT = ph.sb("qT", [P, T])
        kT = ph.sb("kT", [P, T])
        v = ph.sb("v", [P, NT, P])
        L = ph.sb("L", [P, 4, T])
        PT = ph.sb("PT", [P, 2, T])
        st = ph.sb("st", [P, 4, 4])
        bank = ph.banks()
        block = ph.block()
        cols = (N_Q, N_K, N_V)
        wv = w_in.rearrange("(k p) c -> p k c", p=P)

        @block.sync
        def _(sp):
            for n in range(3):
                sp.dma_start(wr[:, n], wv[:, :, cols[n]:cols[n] + P]).then_inc(w_ready[n], 16)
            sp.dma_start(gn[:], gains).then_inc(s.small, 16)
            sp.wait_ge(s.zeroed, 1)
            sp.dma_start(pad[:, 48:79], rpb.rearrange("h r c -> (h r) c")).then_inc(s.rpb_in, 16)
            sp.wait_ge(s.rpb_in, 16)
            sp.dma_start(pad_dram, pad[:]).then_inc(s.pad_out, 16)
            sp.wait_ge(s.pad_out, 16)
            for h in range(8):
                for half in range(2):
                    src = bass.AP(tensor=pad_dram.tensor, offset=pad_dram.offset + (h * 15 + 1 - half) * 127,
                                  ap=[[1, 64], [127, 14], [1, 64]])
                    sp.dma_start(bias[64 * half:64 * half + 64, h], src).then_inc(s.toep, 16)
            with sp.Fori(1, 4) as i:
                for n in range(3):
                    col = sp.snap(i * P + cols[n])
                    used = sp.snap(i * 3 + (n + 1 - 3))
                    sp.wait_ge(s.proj, used)
                    sp.dma_start(wr[:, n], wv[:, :, ds(col, P)]).then_inc(w_ready[n], 16)

        @block.tensor
        def _(pe):
            with pe.Fori(0, 4) as i:
                for n in range(3):
                    pe.wait_ge(w_ready[n], i * 16 + 16)
                    pe.wait_ge(s.copied, i * 3 + (n + 1))
                    if n < 2:
                        for k in range(KT):
                            ins = pe.matmul(bank[n][:, :], wr[:, n, k, :], G.hT[:, k, :], start=(k == 0), stop=(k == KT - 1))
                    else:
                        for t in range(NT):
                            for k in range(KT):
                                ins = pe.matmul(bank[2][:, t * P:(t + 1) * P], G.hT[:, k, t * P:(t + 1) * P], wr[:, n, k, :],
                                                start=(k == 0), stop=(k == KT - 1))
                    ins.then_inc(s.proj, 1)
                for n in range(2):
                    pe.wait_ge(s.sqd, i * 2 + (n + 1))
                    pe.matmul(bank[3 + n][:, :], G.c("blk64"), sq[:, n, :], start=True, stop=True).then_inc(s.ssq, 1)
                pe.wait_ge(s.qk, i * 2 + 2)
                pe.wait_ge(s.copied, i * 3 + 6)

                def logits(m):
                    e, t = m // 4, m % 4
                    pe.wait_ge(s.taken, i * 8 + (m + 1))
                    pe.matmul(bank[(3, 4, 0, 1)[m % 4]][:, :], qT[64 * e:64 * e + 64, t * P:(t + 1) * P], kT[64 * e:64 * e + 64, :],
                              start=True, stop=True).then_inc(s.logits, 1)

                def turn(m):
                    pe.wait_ge(s.p_ready, i * 8 + (m + 1))
                    pe.wait_ge(s.pt, i * 8 + (m + 1))
                    for n in range(NT):
                        ins = pe.transpose(bank[5 + 2 * (m % 2)][:, n * P:(n + 1) * P], L[:, m % 4, n * P:(n + 1) * P], G.c("ident"))
                    ins.then_inc(s.turned, 1)

                def values(m):
                    e, t = m // 4, m % 4
                    pe.wait_ge(s.pt, i * 8 + (m + 3))
                    if m == 0:
                        pe.wait_ge(s.out_taken, i + 1)
                    for n in range(NT):
                        ins = pe.matmul(bank[6][64 * e:64 * e + 64, t * P:(t + 1) * P], v[:, n, 64 * e:64 * e + 64],
                                        PT[:, m % 2, n * P:(n + 1) * P], start=(n == 0), stop=(n == NT - 1))
                    ins.then_inc(s.out, 1)

                logits(0)
                logits(1)
                logits(2)
                turn(0)
                for m in range(8):
                    if m + 3 < 8:
                        logits(m + 3)
                    if m + 1 < 8:
                        turn(m + 1)
                    values(m)

        @block.scalar
        def _(act):
            c = Chain(act, s.achain)
            act.sem_inc(s.copied, 3)
            act.sem_inc(s.pt, 2)
            with act.Fori(0, 4) as i:
                act.wait_ge(s.out_taken, i + 1)
                for n in range(3):
                    act.wait_ge(s.proj, i * 3 + (n + 1))
                    if n < 2:
                        act.activation(raw[:, n, :], bank[n][:, :], ACT.Copy).then_inc(s.copied, 1)
                        act.wait_ge(s.copied, i * 3 + (n + 4))
                        act.activation(sq[:, n, :], raw[:, n, :], ACT.Square).then_inc(s.sqd, 1)
                    else:
                        act.activation(v[:], four(bank[2]), ACT.Copy).then_inc(s.copied, 1)
                for n in range(2):
                    act.wait_ge(s.ssq, i * 2 + (n + 1))
                    c.link(act.activation(rn[:, n, :], bank[3 + n][:, :], ACT.Ln, bias=G.eps[:, 0:1], scale=1.0 / 64))
                    act.activation(rn[:, n, :], rn[:, n, :], ACT.Exp, scale=-0.5).then_inc(s.rn, 1)

                def exps(m):
                    act.wait_ge(s.negmax, i * 8 + (m + 1))
                    act.activation(L[:, m % 4, :], L[:, m % 4, :], ACT.Exp, bias=st[:, m % 4, 1:2],
                                   accum_out=st[:, m % 4, 2:3]).then_inc(s.expd, 1)

                def turn(m):
                    act.wait_ge(s.turned, i * 8 + (m + 1))
                    act.activation(PT[:, m % 2, :], bank[5 + 2 * (m % 2)][:, :], ACT.Copy).then_inc(s.pt, 1)

                for m in range(8):
                    exps(m)
                    if m:
                        turn(m - 1)
                turn(7)
                c.clear()

        @block.vector
        def _(dve):
            c = Chain(dve, s.chain)
            dve.sem_inc(s.taken, 4)
            dve.sem_inc(s.out_taken, 1)
            dve.memset(pad[:], 0.0).then_inc(s.zeroed, 1)
            dve.wait_ge(s.small, 16)
            c.link(dve.tensor_scalar(gn[:, 0:1], gn[:, 0:1], 64 ** -0.5, None, ALU.mult))
            dve.wait_ge(s.toep, 16 * 16)
            bf = bias[:].rearrange("p h x c -> p (h x) c")
            c.link(dve.tensor_tensor(bf, bf, G.c("colmask").unsqueeze(1).to_broadcast([P, 8 * 14, 64]), ALU.add))
            c.clear()
            with dve.Fori(0, 4) as i:
                for n in range(2):
                    dve.wait_ge(s.rn, i * 2 + (n + 1))
                    c.link(dve.tensor_tensor(raw[:, n, :], raw[:, n, :], rn[:, n, :], ALU.mult))
                    if n == 0:
                        src = raw[:, 0, :].rearrange("p (r c) -> p r c", c=NAROW)[:, :, ::-1]
                        dve.tensor_scalar(qT[:].rearrange("p (r c) -> p r c", c=NAROW), src, gn[:, 0:1], None, ALU.mult).then_inc(s.qk, 1)
                    else:
                        dve.tensor_scalar(kT[:], raw[:, 1, :], gn[:, 1:2], None, ALU.mult).then_inc(s.qk, 1)

                def masked(m):
                    e, t, r = m // 4, m % 4, m % 4
                    if m >= 4:
                        dve.wait_ge(s.turned, i * 8 + (m - 3))
                    dve.wait_ge(s.logits, i * 8 + (m + 1))
                    b = bias[:, ds(i * 2 + e, 1), 6 - 2 * t:14 - 2 * t, :]
                    dve.tensor_tensor(L[:, r, :].rearrange("p (a x c) -> p a x c", a=1, c=64),
                                      bank[(3, 4, 0, 1)[r]][:, :].rearrange("p (a x c) -> p a x c", a=1, c=64), b, ALU.add).then_inc(s.taken, 1)
                    dve.wait_ge(s.taken, i * 8 + (m + 5))
                    c.link(dve.tensor_reduce(st[:, r, 0:1], L[:, r, :], AX, ALU.max))
                    dve.tensor_scalar(st[:, r, 1:2], st[:, r, 0:1], -1.0, None, ALU.mult).then_inc(s.negmax, 1)

                def divide(m):
                    r = m % 4
                    dve.wait_ge(s.expd, i * 8 + (m + 1))
                    c.link(dve.reciprocal(st[:, r, 3:4], st[:, r, 2:3]))
                    dve.tensor_scalar(L[:, r, :], L[:, r, :], st[:, r, 3:4], None, ALU.mult).then_inc(s.p_ready, 1)

                masked(0)
                for m in range(8):
                    if m + 1 < 8:
                        masked(m + 1)
                    divide(m)
                dve.wait_ge(s.out, i * 8 + 8)
                src = bank[6][:, :].rearrange("p (r c) -> p r c", c=NAROW)[:, :, ::-1]
                dst = G.obT[:, ds(i, 1), :].rearrange("p a (r c) -> p (a r) c", c=NAROW)
                dve.tensor_scalar(dst, src, 1.0, None, ALU.mult).then_inc(s.out_taken, 1)
                c.clear()


def rwkv_pre_phase(nc, G, w_in, A, lw, af, gg):
    HR = 64
    with Phase(nc, "rp", "proj cb shifted act_done up lw_added out_done ins chain") as ph:
        s = ph.s
        w_ready = ph.sems("w_ready", 3)
        wr = ph.sb("wr", [P, 3, KT, P])
        mul = ph.sb("mul", [P, 5, 3])
        cb = ph.sb("cb", [P, 5, T + 2])
        lo = ph.sb("lo", [P, 5, T])
        wup = ph.sb("wup", [HR, 2, RW])
        aup = ph.sb("aup", [HR, 2, RW])
        gup = ph.sb("gup", [P, RW])
        w0 = ph.sb("w0", [P, 2, RW])
        a0 = ph.sb("a0", [P, 2, 4])
        bank = ph.banks()
        block = ph.block()
        wv = w_in.rearrange("(k p) c -> p k c", p=P)

        @block.sync
        def _(sp):
            for n in range(3):
                c0 = R_LORA + n * P
                sp.dma_start(wr[:, n], wv[:, :, c0:c0 + P]).then_inc(w_ready[n], 16)
            for dst, src in ((mul[:], A.mu_lora), (wup[:, 0], A.w_up_f[0]), (wup[:, 1], A.w_up_b[0]), (aup[:, 0], A.a_up_f[0]),
                             (aup[:, 1], A.a_up_b[0]), (gup[:], A.g_up[0]), (w0[:, 0], bcast_rows(A.w0_f, 1, RW)),
                             (w0[:, 1], bcast_rows(A.w0_b, 1, RW)), (a0[:], A.a0)):
                sp.dma_start(dst, src).then_inc(s.ins, 16)

        parts = ((0, 0, HR), (0, HR, HR), (1, 0, HR), (1, HR, HR), (2, 0, P))

        @block.tensor
        def _(pe):
            for j, (n, c0, m) in enumerate(parts):
                pe.wait_ge(w_ready[n], 16)
                for k in range(KT):
                    ins = pe.matmul(bank[j][0:m, :], wr[:, n, k, c0:c0 + m], G.hT[:, k, :], start=(k == 0), stop=(k == KT - 1))
                ins.then_inc(s.proj, 1)
            pe.wait_ge(s.ins, 16 * 9)
            pe.wait_ge(s.cb, 5)
            pe.wait_ge(s.act_done, 3)
            for o in range(20):
                if o < 8:
                    d, n = o // 4, o % 4
                    ins = pe.matmul(bank[o][:, :], lo[0:HR, d, n * P:(n + 1) * P], wup[:, d, :], start=True, stop=True)
                elif o < 16:
                    d, n = (o - 8) // 4, o % 4
                    pe.wait_ge(s.lw_added, o - 7)
                    ins = pe.matmul(bank[o - 8][:, :], aup[:, d, n * P:(n + 1) * P], lo[0:HR, 2 + d, :], start=True, stop=True)
                else:
                    n = o - 16
                    pe.wait_ge(s.out_done, n + 1)
                    ins = pe.matmul(bank[n][:, :], gup[:, n * P:(n + 1) * P], lo[:, 4, :], start=True, stop=True)
                ins.then_inc(s.up, 1)

        @block.scalar
        def _(act):
            act.wait_ge(s.shifted, 1)
            for j, (n, c0, m) in enumerate(parts):
                act.wait_ge(s.proj, j + 1)
                act.activation(cb[0:m, j, 1:T + 1], bank[j][0:m, :], ACT.Copy).then_inc(s.cb, 1)
            act.wait_ge(s.shifted, 6)
            for j, func in ((0, ACT.Tanh), (1, ACT.Tanh), (4, ACT.Sigmoid)):
                m = parts[j][2]
                act.activation(lo[0:m, j, :], lo[0:m, j, :], func).then_inc(s.act_done, 1)
            for o in range(8, 20):
                n = o % 4
                act.wait_ge(s.up, o + 1)
                if o < 16:
                    d = (o - 8) // 4
                    act.activation(af[:, d, n, :], bank[o - 8][:, :], ACT.Sigmoid, bias=a0[:, d, n:n + 1]).then_inc(s.out_done, 1)
                else:
                    act.activation(gg[:, n, :], bank[n][:, :], ACT.Copy).then_inc(s.out_done, 1)
            act.wait_ge(s.lw_added, 8)
            for d in range(2):
                act.activation(lw[:, d], lw[:, d], ACT.Sigmoid)

        @block.vector
        def _(dve):
            c = Chain(dve, s.chain)
            dve.memset(cb[:], 0.0).then_inc(s.shifted, 1)
            dve.wait_ge(s.ins, 16 * 9)
            c.link(dve.tensor_tensor(mul[:, :, 1:2], mul[:, :, 0:1], mul[:, :, 2:3], ALU.add))
            c.link(dve.tensor_scalar(mul[:, :, 1:2], mul[:, :, 1:2], -1.0, 1.0, ALU.mult, ALU.add))
            for j, (n, c0, m) in enumerate(parts):
                dve.wait_ge(s.cb, j + 1)
                c.link(dve.tensor_scalar(lo[0:m, j, :], cb[0:m, j, 0:T], mul[0:m, j, 0:1], None, ALU.mult))
                c.link(dve.scalar_tensor_tensor(lo[0:m, j, :], cb[0:m, j, 1:T + 1], mul[0:m, j, 1:2], lo[0:m, j, :], ALU.mult, ALU.add))
                dve.scalar_tensor_tensor(lo[0:m, j, :], cb[0:m, j, 2:T + 2], mul[0:m, j, 2:3], lo[0:m, j, :], ALU.mult, ALU.add).then_inc(s.shifted, 1)
            for o in range(8):
                dve.wait_ge(s.up, o + 1)
                dve.tensor_tensor(lw[:, o // 4, o % 4, :], bank[o][:, :], w0[:, o // 4, :], ALU.add).then_inc(s.lw_added, 1)


def rwkv_phase(nc, G, w_in, A, lw, af, gg):
    HR = 64
    with Phase(nc, "rw", "small proj cb shifted lwp cum cs ex sc kkp sq ssq rn feat ft tok gram nt x xs yz tw "
               "rhs rr uu un su st yy yc ys mean cen sq2 var rv bon bo fin chain achain pads dropped") as ph:
        s = ph.s
        w_ready = ph.sems("w_ready", 3)
        wr = ph.sb("wr", [P, 3, KT, P])
        mu = ph.sb("mu", [P, 4, 9])
        muh = ph.sb("muh", [P, 3, 3])
        par = ph.sb("par", [P, 4, 6])
        parh = ph.sb("parh", [P, 6])
        rkv = ph.sb("rkv", [P, 3, T])
        ar = ph.sb("ar", [P, 2, T])
        kkp = ph.sb("kkp", [P, T])
        sq = ph.sb("sq", [P, T])
        rn = ph.sb("rn", [P, T])
        ft = ph.sb("ft", [P, 2, 4, T])
        tk = ph.sb("tk", [P, 2, 2, NT, P])
        vtok = ph.sb("vtok", [P, NT, P])
        NTm = ph.sb("NTm", [P, 2, 2, NT, P])
        GA = ph.sb("GA", [P, 3, 2, 2, NT, P])
        Tm = ph.sb("Tm", [P, 2, NT, P])
        Xs = ph.sb("Xs", [P, 2, NT, P])
        Wm = ph.sb("Wm", [P, 2, 2, NT, P])
        ms = ph.sb("ms", [P, 6, 2, NT])
        S = ph.sb("S", [P, 2, 2, P])
        St = ph.sb("St", [P, 2, P])
        R = ph.sb("R", [P, 2, 2, P])
        bank = ph.banks()
        block = ph.block()
        wv = w_in.rearrange("(k p) c -> p k c", p=P)
        cb = NTm[:].rearrange("p a b c d -> p (a b c d)")[:, 0:3 * (T + 2)].rearrange("p (j c) -> p j c", j=3)
        lwp = Wm[:, 0]
        Ein, Eex = Tm, Xs
        Einv = GA[:, 2, 0]
        ysb = kkp
        un = ar[:, 1, :].rearrange("p (d a c) -> p d a c", d=2, a=2)
        kd = GA[:, 0, 0].rearrange("p d n c -> p d (n c)")
        kk = GA[:, 1, 0, 0].rearrange("p n c -> p (n c)")
        incl, strict = (G.c("le"), G.c("ge")), (G.c("lt"), G.c("gt"))
        A_, B_, K_, R_ = range(4)
        flat = lambda a: a.rearrange("p n c -> p (n c)")

        def chunk(d, st):
            return st if d == 0 else NT - 1 - st

        @block.sync
        def _(sp):
            for n in range(3):
                sp.dma_start(wr[:, n], wv[:, :, n * RW:n * RW + P]).then_inc(w_ready[n], 16)
            sp.dma_start(mu[:], A.mu_rkv).then_inc(s.small, 16)
            sp.dma_start(par[:], A.rw_par).then_inc(s.small, 16)
            with sp.Fori(1, 4) as i:
                for n in range(3):
                    col = sp.snap(i * P + n * RW)
                    used = sp.snap(i * 3 + (n + 1 - 3))
                    sp.wait_ge(s.proj, used)
                    sp.dma_start(wr[:, n], wv[:, :, ds(col, P)]).then_inc(w_ready[n], 16)

        grams = [(ty, e, d) for e in range(2) for d in range(2) for ty in range(4)]
        gram_ops = ((B_, A_), (K_, A_), (B_, R_), (K_, R_))

        @block.tensor
        def _(pe):
            with pe.Fori(0, 4) as i:
                pe.wait_ge(s.fin, i + 1)
                for n in range(3):
                    pe.wait_ge(w_ready[n], i * 16 + 16)
                    for k in range(KT):
                        ins = pe.matmul(bank[n][:, :], wr[:, n, k, :], G.hT[:, k, :], start=(k == 0), stop=(k == KT - 1))
                    ins.then_inc(s.proj, 1)
                for d in range(2):
                    pe.wait_ge(s.lwp, i * 2 + (d + 1))
                    for m, (b, mask) in enumerate(((3, incl[d]), (5, strict[d]))):
                        for n in range(NT):
                            ins = pe.matmul(bank[b + d][:, n * P:(n + 1) * P], lwp[:, d, n, :], mask, start=True, stop=True)
                    ins.then_inc(s.cum, 1)
                pe.wait_ge(s.sq, i + 1)
                pe.matmul(bank[7][:, :], G.c("blk64"), sq[:, :], start=True, stop=True).then_inc(s.ssq, 1)
                pe.wait_ge(s.rn, i + 1)
                pe.wait_ge(s.ex, i + 1)
                for d in range(2):
                    pe.wait_ge(s.ft, i * 2 + (d + 1))
                    for m, kind in enumerate((B_, K_)):
                        for n in range(NT):
                            ins = pe.transpose(bank[3 + 2 * d + m][:, n * P:(n + 1) * P], ft[:, d, kind, n * P:(n + 1) * P], G.c("ident"))
                        ins.then_inc(s.feat, 1)
                for n in range(NT):
                    ins = pe.transpose(bank[7][:, n * P:(n + 1) * P], rkv[:, 2, n * P:(n + 1) * P], G.c("ident"))
                ins.then_inc(s.feat, 1)
                pe.wait_ge(s.cb, i * 3 + 3)
                for m, (ty, e, d) in enumerate(grams):
                    if m < 8 and m >= 3:
                        pe.wait_ge(s.tok, i * 5 + (m - 2))
                    if m >= 8:
                        pe.wait_ge(s.gram, i * 16 + (m - 7))
                    l, r = gram_ops[ty]
                    for n in range(NT):
                        c0 = slice(n * P, (n + 1) * P)
                        ins = pe.matmul(bank[m % 8][:, c0], ft[64 * e:64 * e + 64, d, l, c0], ft[64 * e:64 * e + 64, d, r, c0],
                                        start=True, stop=True)
                    ins.then_inc(s.nt, 1)
                pe.wait_ge(s.gram, i * 16 + 16)
                for e in range(2):
                    invert_pe(pe, G, InvertSems(s.tw, s.xs, s.x, s.yz, s.gram), NTm[:, e], Tm, Wm[:, e], Xs,
                              ((bank[2], bank[3]), (bank[4], bank[5]), (bank[6], bank[7])), i * 16, i * 28 + e * 14)
                for st in range(NT):
                    for d in range(2):
                        n = chunk(d, st)
                        c0 = slice(n * P, (n + 1) * P)
                        if st:
                            pe.wait_ge(s.st, i * 6 + (2 * (st - 1) + d + 1))
                        else:
                            pe.wait_ge(s.tw, i * 28 + 28)
                        if st:
                            pe.matmul(bank[2 + d][:, 0:P], ft[:, d, A_, c0], S[:, d, (st - 1) % 2, :], start=True, stop=False)
                        for e in range(2):
                            h0 = slice(64 * e, 64 * e + 64)
                            ins = pe.matmul(bank[2 + d][:, h0], GA[:, 0, e, d, n, :], vtok[:, n, h0], start=(st == 0), stop=(st == 0 or e == 1))
                        ins.then_inc(s.rhs, 1)
                    for d in range(2):
                        n = chunk(d, st)
                        pe.wait_ge(s.rr, i * 8 + (2 * st + d + 1))
                        for e in range(2):
                            h0 = slice(64 * e, 64 * e + 64)
                            ins = pe.matmul(bank[4 + d][:, h0], Wm[:, e, d, n, :], R[:, d, st % 2, h0], start=True, stop=True)
                        ins.then_inc(s.uu, 1)
                    for d in range(2):
                        n = chunk(d, st)
                        c0 = slice(n * P, (n + 1) * P)
                        pe.wait_ge(s.un, i * 8 + (2 * st + d + 1))
                        if st < NT - 1:
                            pe.matmul(bank[6 + d][:, 0:P], tk[:, d, 0, n, :], un[:, d, st % 2, :], start=True, stop=False)
                            pe.matmul(bank[6 + d][:, 0:P], tk[:, d, 1, n, :], vtok[:, n, :], start=False, stop=True).then_inc(s.su, 1)
                        if st:
                            pe.matmul(bank[d][:, c0], S[:, d, (st - 1) % 2, :], ft[:, d, R_, c0], start=True, stop=False)
                        for e in range(2):
                            h0 = slice(64 * e, 64 * e + 64)
                            pe.matmul(bank[d][h0, c0], un[:, d, st % 2, h0], GA[:, 1, e, d, n, :], start=(st == 0), stop=False)
                            ins = pe.matmul(bank[d][h0, c0], vtok[:, n, h0], GA[:, 2, e, d, n, :], start=False, stop=True)
                        ins.then_inc(s.yy, 1)
                pe.wait_ge(s.bon, i + 1)
                pe.matmul(bank[4][:, :], G.c("blk64"), ar[:, 0, :], start=True, stop=True).then_inc(s.bo, 1)
                pe.wait_ge(s.ys, i + 1)
                pe.matmul(bank[2][:, :], G.c("blk64"), ysb[:, :], start=True, stop=True).then_inc(s.mean, 1)
                pe.wait_ge(s.sq2, i + 1)
                pe.matmul(bank[3][:, :], G.c("blk64"), sq[:, :], start=True, stop=True).then_inc(s.var, 1)

        @block.scalar
        def _(act):
            c = Chain(act, s.achain)
            with act.Fori(0, 4) as i:
                act.wait_ge(s.pads, i + 1)
                for n in range(3):
                    act.wait_ge(s.proj, i * 3 + (n + 1))
                    act.activation(cb[:, n, 1:T + 1], bank[n][:, :], ACT.Copy).then_inc(s.cb, 1)
                act.wait_ge(s.kkp, i + 1)
                act.activation(sq[:], kkp[:], ACT.Square).then_inc(s.sq, 1)
                act.wait_ge(s.cs, i * 2 + 2)
                for d in range(2):
                    act.activation(Einv[:, d], Ein[:, d], ACT.Exp, scale=-1.0)
                    c.link(act.activation(Eex[:, d], Eex[:, d], ACT.Exp))
                    act.activation(Ein[:, d], Ein[:, d], ACT.Exp)
                act.activation(ms[:, 2:4], ms[:, 2:4], ACT.Exp).then_inc(s.ex, 1)
                act.wait_ge(s.ssq, i + 1)
                c.link(act.activation(rn[:], bank[7][:, :], ACT.Ln, bias=G.eps[:, 2:3]))
                act.activation(rn[:], rn[:], ACT.Exp, scale=-0.5).then_inc(s.rn, 1)
                for m in range(5):
                    act.wait_ge(s.feat, i * 5 + (m + 1))
                    dst = tk[:, m // 2, m % 2] if m < 4 else vtok[:]
                    act.activation(dst, four(bank[3 + m]), ACT.Copy).then_inc(s.tok, 1)
                for st in range(NT):
                    for d in range(2):
                        act.wait_ge(s.uu, i * 8 + (2 * st + d + 1))
                        act.activation(un[:, d, st % 2, :], bank[4 + d][:, 0:P], ACT.Copy, scale=-1.0).then_inc(s.un, 1)
                act.wait_ge(s.yy, i * 8 + 8)
                act.activation(ysb[:], bank[0][:, :], ACT.Copy).then_inc(s.yc, 1)
                act.wait_ge(s.cen, i + 1)
                act.activation(sq[:], ysb[:], ACT.Square).then_inc(s.sq2, 1)
                act.wait_ge(s.var, i + 1)
                c.link(act.activation(rn[:], bank[3][:, :], ACT.Ln, bias=G.eps[:, 1:2], scale=1.0 / HR))
                act.activation(rn[:], rn[:], ACT.Exp, scale=-0.5).then_inc(s.rv, 1)
                c.clear()

        @block.vector
        def _(dve):
            c = Chain(dve, s.chain)
            dve.sem_inc(s.fin, 1)
            dve.wait_ge(s.small, 32)
            mv = mu[:].rearrange("p t (j c) -> p (t j) c", c=3)
            c.link(dve.tensor_tensor(mv[:, :, 1:2], mv[:, :, 0:1], mv[:, :, 2:3], ALU.add))
            c.link(dve.tensor_scalar(mv[:, :, 1:2], mv[:, :, 1:2], -1.0, 1.0, ALU.mult, ALU.add))
            c.link(dve.tensor_scalar(par[:, :, 5:6], par[:, :, 1:2], -1.0, 1.0, ALU.mult, ALU.add))
            c.clear()
            with dve.Fori(0, 4) as i:
                dve.wait_ge(s.fin, i + 1)
                dve.tensor_scalar(muh[:].rearrange("p a b -> p (a b)").unsqueeze(1), mu[:, ds(i, 1), :], 1.0, None, ALU.mult)
                c.link(dve.tensor_scalar(parh[:].unsqueeze(1), par[:, ds(i, 1), :], 1.0, None, ALU.mult))
                dve.memset(cb[:, :, 0:1], 0.0)
                dve.memset(cb[:, :, T + 1:T + 2], 0.0).then_inc(s.pads, 1)
                for d in range(2):
                    dve.tensor_scalar(lwp[:, d], lw[:, d, :, ds(i * P, P)], -DECAY, None, ALU.mult).then_inc(s.lwp, 1)
                dve.wait_ge(s.pads, i + 1)
                for j in range(3):
                    dve.wait_ge(s.cb, i * 3 + (j + 1))
                    c.link(dve.tensor_scalar(rkv[:, j, :], cb[:, j, 0:T], muh[:, j, 0:1], None, ALU.mult))
                    for tap in (1, 2):
                        c.link(dve.scalar_tensor_tensor(rkv[:, j, :], cb[:, j, tap:tap + T], muh[:, j, tap:tap + 1], rkv[:, j, :],
                                                        ALU.mult, ALU.add))
                r, k, v = rkv[:, 0, :], rkv[:, 1, :], rkv[:, 2, :]
                dve.tensor_scalar(kkp[:], k, parh[:, 0:1], None, ALU.mult).then_inc(s.kkp, 1)
                for d in range(2):
                    dve.wait_ge(s.cum, i * 2 + (d + 1))
                    mid, end = (63, 127) if d == 0 else (64, 0)
                    cin = four(bank[3 + d])
                    dve.tensor_copy(ms[:, 0, d, :].unsqueeze(2), cin[:, :, mid:mid + 1])
                    dve.tensor_copy(ms[:, 2, d, :].unsqueeze(2), cin[:, :, mid:mid + 1])
                    c.link(dve.tensor_copy(ms[:, 1, d, :].unsqueeze(2), cin[:, :, end:end + 1]))
                    dve.tensor_tensor(Ein[:, d], cin, each4(ms[:, 0, d, :]), ALU.subtract)
                    dve.tensor_tensor(Eex[:, d], four(bank[5 + d]), each4(ms[:, 0, d, :]), ALU.subtract)
                    dve.tensor_tensor(ms[:, 3, d, :], ms[:, 1, d, :], ms[:, 0, d, :], ALU.subtract).then_inc(s.cs, 1)
                dve.wait_ge(s.ex, i + 1)
                dve.tensor_tensor(ms[:, 4, 0, 0:3], ms[:, 3, 0, 0:3], ms[:, 2, 0, 1:4], ALU.mult)
                dve.tensor_tensor(ms[:, 4, 1, 1:4], ms[:, 3, 1, 1:4], ms[:, 2, 1, 0:3], ALU.mult)
                dve.wait_ge(s.rn, i + 1)
                dve.wait_ge(s.kkp, i + 1)
                c.link(dve.tensor_tensor(kk, kkp[:], rn[:], ALU.mult))
                for d in range(2):
                    a = af[:, d, ds(i, 1), :]
                    dve.tensor_tensor(ft[:, d, B_, :].unsqueeze(1), kk.unsqueeze(1), a, ALU.mult)
                    c.link(dve.tensor_scalar(ar[:, d, :].unsqueeze(1), a, parh[:, 1:2], parh[:, 5:6], ALU.mult, ALU.add))
                    c.link(dve.tensor_tensor(kd[:, d, :], k, ar[:, d, :], ALU.mult))
                    dve.tensor_tensor(ft[:, d, A_, :], kk, flat(Eex[:, d]), ALU.mult)
                    dve.tensor_tensor(ft[:, d, R_, :], r, flat(Ein[:, d]), ALU.mult)
                    dve.tensor_tensor(ft[:, d, B_, :], ft[:, d, B_, :], flat(Einv[:, d]), ALU.mult)
                    dve.tensor_tensor(ft[:, d, K_, :], kd[:, d, :], flat(Einv[:, d]), ALU.mult).then_inc(s.ft, 1)
                c.link(dve.tensor_tensor(kd[:, 0, :], kd[:, 0, :], kd[:, 1, :], ALU.add))
                dve.scalar_tensor_tensor(ar[:, 0, :], kd[:, 0, :], parh[:, 2:3], r, ALU.mult, ALU.mult).then_inc(s.bon, 1)
                dve.wait_ge(s.bon, i + 1)
                dve.wait_ge(s.ft, i * 2 + 2)
                for m, (ty, e, d) in enumerate(grams):
                    dve.wait_ge(s.nt, i * 16 + (m + 1))
                    mask = strict[d] if ty < 2 else incl[d]
                    dst = NTm[:, e, d] if ty == 0 else GA[:, ty - 1, e, d]
                    dve.tensor_tensor(dst, four(bank[m % 8]), over4(mask), ALU.mult).then_inc(s.gram, 1)
                dve.wait_ge(s.gram, i * 16 + 16)
                for e in range(2):
                    invert_dve(dve, G, s, NTm[:, e], Tm, Wm[:, e], Xs,
                               ((bank[2], bank[3]), (bank[4], bank[5]), (bank[6], bank[7])), i * 28 + e * 14, i * 24 + e * 12)
                for st in range(NT):
                    for d in range(2):
                        dve.wait_ge(s.rhs, i * 8 + (2 * st + d + 1))
                        dve.tensor_copy(R[:, d, st % 2, :], bank[2 + d][:, 0:P]).then_inc(s.rr, 1)
                    if st < NT - 1:
                        for d in range(2):
                            n = chunk(d, st)
                            sc = ms[:, 4, d, n:n + 1]
                            dve.wait_ge(s.su, i * 6 + (2 * st + d + 1))
                            if st:
                                dve.wait_ge(s.st, i * 6 + (2 * (st - 1) + d + 1))
                                c.link(dve.tensor_tensor(St[:, d, :], S[:, d, (st - 1) % 2, :], bank[6 + d][:, 0:P], ALU.add))
                                ins = dve.scalar_tensor_tensor(S[:, d, st % 2, :], St[:, d, :], sc, G.c("blk64"), ALU.mult, ALU.mult)
                            else:
                                ins = dve.scalar_tensor_tensor(S[:, d, 0, :], bank[6 + d][:, 0:P], sc, G.c("blk64"), ALU.mult, ALU.mult)
                            ins.then_inc(s.st, 1)
                dve.wait_ge(s.yc, i + 1)
                dve.tensor_tensor(ysb[:], ysb[:], bank[1][:, :], ALU.add).then_inc(s.ys, 1)
                dve.wait_ge(s.mean, i + 1)
                dve.wait_ge(s.ys, i + 1)
                dve.scalar_tensor_tensor(ysb[:], bank[2][:, :], -1.0 / HR, ysb[:], ALU.mult, ALU.add).then_inc(s.cen, 1)
                dve.wait_ge(s.bo, i + 1)
                dve.tensor_tensor(ar[:, 1, :], bank[4][:, :], v, ALU.mult)
                dve.wait_ge(s.rv, i + 1)
                c.link(dve.tensor_tensor(ysb[:], ysb[:], rn[:], ALU.mult))
                c.link(dve.tensor_scalar(ysb[:], ysb[:], parh[:, 3:4], parh[:, 4:5], ALU.mult, ALU.add))
                c.link(dve.tensor_tensor(ysb[:], ysb[:], ar[:, 1, :], ALU.add))
                dve.tensor_tensor(G.oaT[:, ds(i, 1), :], ysb[:].unsqueeze(1), gg[:, ds(i, 1), :], ALU.mult).then_inc(s.fin, 1)
                c.clear()


OUT_SHAPE = (1, T, D)


def layout(x, give, tiles):
    for n in ("x", "rel_bias", "w_in", "w_branch_a", "w_branch_b", "w_out", "w_ff1", "w_ff2",
              "ln_mix_pre", "ln_mix_post", "ln_mlp_pre", "ln_mlp_post"):
        give(n, x[n])
    const, hot, band = constants()
    give("dt", np.concatenate([x["dt_bias_f"][0], x["dt_bias_b"][0]]))
    give("alog", np.concatenate([x["a_log_f"][0], x["a_log_b"][0]]))
    give("convw", np.asarray(x["conv_w"][0]).reshape(5, 3, GH, P).transpose(3, 2, 1, 0).reshape(P, GH, 15))
    give("norm_a", np.asarray(x["norm_a"][0]).reshape(P, 1))
    give("norm1_g", x["norm1_g_2"])
    for n in ("w_in", "w_up_f", "w_up_b", "a_up_f", "a_up_b", "g_up", "rpb", "w_o_rwkv", "w_o_na", "w_out",
              "w_gate_e", "w_up_e", "w_down_e", "w0_f", "w0_b", "norm2_g"):
        give(n + "_2" if n in ("w_in", "w_out") else n, x[n + "_2"])
    give("gains", np.stack([np.tile(x["q_gain_2"][0], 2), np.tile(x["k_gain_2"][0], 2)], 1))
    give("gate_bias", np.asarray(x["b_gate_2"][0]).reshape(2, KT, P).transpose(2, 1, 0))
    give("a0", np.stack([tiles(x["a0_f_2"][0], 4), tiles(x["a0_b_2"][0], 4)], 1))
    mp, mn = np.asarray(x["mu_prev_2"][0]), np.asarray(x["mu_next_2"][0])
    mu = np.stack([mp, np.zeros_like(mp), mn], 1)
    give("mu_rkv", mu[:R_LORA].reshape(3, 4, P, 3).transpose(2, 1, 0, 3).reshape(P, 4, 9))
    lora = np.zeros((P, 5, 3), mu.dtype)
    lora[:64, 0:4] = mu[R_LORA:R_LORA + 256].reshape(4, 64, 3).transpose(1, 0, 2)
    lora[:, 4] = mu[R_LORA + 256:]
    give("mu_lora", lora)
    room = np.zeros_like(x["k_k_2"][0])
    give("rw_par", np.stack([tiles(a, 4) for a in (x["k_k_2"][0], x["k_a_2"][0], np.asarray(x["r_k_2"][0]).reshape(-1),
                                                    x["lnx_g_2"][0], x["lnx_b_2"][0], room)], 2))
    give("w_router", np.concatenate([x["w_router_group_2"][0], x["w_router_expert_2"][0]], 1))
    give("b_router", np.concatenate([x["b_router_group_2"][0], x["b_router_expert_2"][0]]))
    give("const", const)
    give("hot", hot)
    give("band", band)


@contextmanager
def branches(nc, G, n):
    with nc.sbuf_tensor(f"oaT{n}", [P, KT, T], F32) as G.oaT, nc.sbuf_tensor(f"obT{n}", [P, NT, T], F32) as G.obT:
        yield


def build(nc, A, out):
    lines_dram = nc.dram_tensor("bias_lines", (4, LINES * (LINE + 1)), F32, kind="Internal").ap()
    pad_dram = nc.dram_tensor("rpb_padded", (120, 127), F32, kind="Internal").ap()
    rows_dram = nc.dram_tensor("token_rows", (T, D), F32, kind="Internal").ap()
    y_dram = nc.dram_tensor("expert_rows", (SLOTS * P, D), F32, kind="Internal").ap()
    with ExitStack() as ctx:
        G = Shared()
        G.const = ctx.enter_context(nc.sbuf_tensor("const", [P, NCONST], F32))
        G.X = ctx.enter_context(nc.sbuf_tensor("X", [P, NT, D], F32))
        G.hT = ctx.enter_context(nc.sbuf_tensor("hT", [P, KT, T], F32))
        G.c = lambda n, a=0, b=None: G.const[:, CC[n][0] + a:CC[n][0] + (CC[n][1] if b is None else b)]
        G.eps = ctx.enter_context(nc.sbuf_tensor("eps", [P, 4], F32))
        G.Y = ctx.enter_context(nc.sbuf_tensor("Y", [P, NT, D], F32))
        G.mT = G.Y[:].rearrange("p t (a c) -> p (t a) c", a=2)
        norm_phase(nc, G, "n1", A.ln_mix_pre, (A.x, A.const))
        with branches(nc, G, 1):
            attention_phase(nc, G, A.w_in[0], A.rel_bias, A.hot, A.band, lines_dram)
            gdn_phase(nc, G, A.w_in[0], A.dt, A.alog, A.convw, A.norm_a)
            merge_phase(nc, G, "m1", A.w_branch_a[0], A.w_branch_b[0], A.w_in[0], (C_GA, C_GB))
        out_phase(nc, G, "o1", A.w_out[0], False)
        norm_phase(nc, G, "n2", A.ln_mlp_pre, None, A.ln_mix_post)
        w1 = A.w_ff1[0].rearrange("(k p) c -> p k c", p=P)
        w2 = A.w_ff2[0].rearrange("(g f p) d -> g p f d", f=2, p=P)
        ffn_phase(nc, G, DF // DE, lambda g: w1[:, :, ds(g * DE, DE)], lambda g: group_of(w2, g))
        norm_phase(nc, G, "n3", A.norm1_g, None, A.ln_mlp_post)
        w_in2 = A.w_in_2[0]
        with branches(nc, G, 2):
            grid_attention_phase(nc, G, w_in2, A.rpb[0], A.gains, pad_dram)
            with nc.sbuf_tensor("af", [P, 2, 4, T], F32) as af:
                lw = G.Y[:].rearrange("p t d -> p (t d)").rearrange("p (d n c) -> p d n c", d=2, n=NT)
                gg = G.oaT[:, NT:2 * NT]
                rwkv_pre_phase(nc, G, w_in2, A, lw, af, gg)
                rwkv_phase(nc, G, w_in2, A, lw, af, gg)
            merge_phase(nc, G, "m2", A.w_o_rwkv[0], A.w_o_na[0], w_in2, (N_GA, N_GB), A.gate_bias)
        out_phase(nc, G, "o2", A.w_out_2[0], True)
        norm_phase(nc, G, "n4", A.norm2_g, rows_dram=rows_dram)
        rows = ctx.enter_context(nc.sbuf_tensor("rows", [P, SLOTS], U32))
        expert = ctx.enter_context(nc.sbuf_tensor("expert", [P, SLOTS], U32))
        place = ctx.enter_context(nc.sbuf_tensor("place", [P, NT, 2], U32))
        weight = ctx.enter_context(nc.sbuf_tensor("weight", [P, NT, 2], F32))
        router_phase(nc, G, A.w_router, A.b_router, rows, expert, place, weight)
        wge = A.w_gate_e[0].rearrange("e (p k) f -> e p k f", p=P)
        wue = A.w_up_e[0].rearrange("e (p k) f -> e p k f", p=P)
        wde = A.w_down_e[0].rearrange("e (f p) d -> e p f d", p=P)
        moe_phase(nc, G, wge, wue, wde, rows, expert, rows_dram, y_dram)
        final_phase(nc, G, place, weight, y_dram, out)


def group_of(view, g):
    return view[g] if isinstance(g, int) else view[ds(g, 1)].rearrange("a p k c -> p (a k) c")




def kernel(**inputs):
    import concourse.bacc as _bacc
    from concourse import mybir as _mybir
    from concourse.bass_utils import run_bass_kernel_spmd as _run

    nc = _bacc.Bacc("TRN2", target_bir_lowering=False, num_devices=1)
    arrays, args = {}, {}

    def give(name, a):
        a = np.ascontiguousarray(a)
        arrays[f"in_{name}"] = a
        args[name] = nc.dram_tensor(f"in_{name}", a.shape, _mybir.dt.from_np(a.dtype), kind="ExternalInput").ap()

    def tiles(v, n):
        return np.asarray(v).reshape(n, P).T

    layout(inputs, give, tiles)
    out = nc.dram_tensor("out_0", OUT_SHAPE, F32, kind="ExternalOutput").ap()
    build(nc, namedtuple("Inputs", list(args))(*args.values()), out)
    r = _run(nc, [arrays], core_ids=[0])
    return r.results[0]["out_0"]
```
